# Optimizing a Trainium2 kernel written in Bass

```python
import math
import jax
import jax.numpy as jnp
from jax import lax
import numpy as np

D_MODEL = 2048
BATCH = 1
SEQ = 256
DEPTH = 1

GRID_W = 64
CTX_LEN = 256
N_MOD = 6
NORM_EPS = 1e-6
RW_HEAD = 64
RW_WIDTH = D_MODEL
RW_HEADS = RW_WIDTH // RW_HEAD
LORA_W = 96
LORA_A = 96
LORA_G = 256
LN_X_EPS = 64e-5
SSM_WIDTH = D_MODEL
SSM_HEADDIM = 64
SSM_HEADS = SSM_WIDTH // SSM_HEADDIM
SSM_GROUPS = 8
SSM_HPG = SSM_HEADS // SSM_GROUPS
SSM_STATE = 128
SSM_CONV = 5
SSM_CHUNK = 128
PEER_HEADS = 8
PEER_KEYS = 128
PEER_EXPERTS = PEER_KEYS * PEER_KEYS
PEER_TOPK = 16
PEER_QDIM = 256
PEER_HALF = PEER_QDIM // 2
PEER_BLOCK = 128
RW_COLS = 3 * RW_WIDTH + 2 * LORA_W + 2 * LORA_A + LORA_G
XBC_COLS = SSM_WIDTH + 2 * SSM_GROUPS * SSM_STATE
IN_COLS = RW_COLS + SSM_WIDTH + XBC_COLS + 2 * SSM_HEADS + 2 * D_MODEL
IN_SPLITS = (RW_COLS, RW_COLS + SSM_WIDTH, RW_COLS + SSM_WIDTH + XBC_COLS, RW_COLS + SSM_WIDTH + XBC_COLS + 2 * SSM_HEADS)
RW_SPLITS = (RW_WIDTH, 2 * RW_WIDTH, 3 * RW_WIDTH, 3 * RW_WIDTH + LORA_W, 3 * RW_WIDTH + 2 * LORA_W, 3 * RW_WIDTH + 2 * LORA_W + LORA_A, 3 * RW_WIDTH + 2 * LORA_W + 2 * LORA_A)

kernel_name = 'hybrid_rwkv7_ssd_peer_dit_block'

def rms_norm(u, gain):
    uf = u.astype(jnp.float32)
    uf = uf * lax.rsqrt(jnp.mean(uf * uf, axis=-1, keepdims=True) + NORM_EPS)
    return (uf * gain.astype(jnp.float32)).astype(u.dtype)

def centred_token_shift(p, mu):
    pad = jnp.pad(p, ((0, 0), (1, 1), (0, 0)))
    return p + mu * (0.5 * (pad[:, :-2] + pad[:, 2:]) - p)

def raster_to_column(u, rows):
    b, s, ch = u.shape
    return u.reshape(b, rows, GRID_W, ch).transpose(0, 2, 1, 3).reshape(b, s, ch)

def column_to_raster(u, rows):
    b, s, ch = u.shape
    return u.reshape(b, GRID_W, rows, ch).transpose(0, 2, 1, 3).reshape(b, s, ch)

def wkv7_scan(s0, r, decay, k, v, kk, kka, reverse):
    def step(state, inp):
        r_t, w_t, k_t, v_t, kk_t, kka_t = inp
        sa = jnp.einsum('bhvk,bhk->bhv', state, kk_t)
        state = state * w_t[:, :, None, :] - sa[..., None] * kka_t[:, :, None, :] + v_t[..., None] * k_t[:, :, None, :]
        return state, jnp.einsum('bhvk,bhk->bhv', state, r_t)
    seq_major = tuple(jnp.moveaxis(u, 1, 0) for u in (r, decay, k, v, kk, kka))
    s_last, y = lax.scan(step, s0, seq_major, reverse=reverse)
    return jnp.moveaxis(y, 0, 1), s_last

def rwkv7_branch(slab, s0_fwd, s0_bwd, w0, w2, a0, a2, g2, k_k, k_a, r_k, ln_w, ln_b):
    bsz, t, _ = slab.shape
    f32 = jnp.float32
    r, k, v, wd_f, wd_b, ad_f, ad_b, gd = jnp.split(slab.astype(f32), RW_SPLITS, axis=-1)
    heads = lambda u: u.reshape(bsz, t, RW_HEADS, RW_HEAD)
    kk = heads(k * k_k.astype(f32))
    kk = kk / jnp.maximum(jnp.sqrt(jnp.sum(kk * kk, axis=-1, keepdims=True)), 1e-12)

    def direction_inputs(wd, ad, d):
        w_log = -jax.nn.softplus(-(w0[d].astype(f32) + jnp.tanh(wd) @ w2[d].astype(f32))) - 0.5
        a = jax.nn.sigmoid(a0[d].astype(f32) + ad @ a2[d].astype(f32))
        k_dir = k * (1.0 + (a - 1.0) * k_a.astype(f32))
        return heads(jnp.exp(-jnp.exp(w_log))), heads(a), heads(k_dir)

    rh, vh = heads(r), heads(v)
    dec_f, a_f, k_f = direction_inputs(wd_f, ad_f, 0)
    dec_b, a_b, k_b = direction_inputs(wd_b, ad_b, 1)
    y_f, s_fwd = wkv7_scan(s0_fwd, rh, dec_f, k_f, vh, kk, kk * a_f, reverse=False)
    y_b, s_bwd = wkv7_scan(s0_bwd, rh, dec_b, k_b, vh, kk, kk * a_b, reverse=True)
    y = y_f + y_b
    mean = jnp.mean(y, axis=-1, keepdims=True)
    var = jnp.mean(jnp.square(y - mean), axis=-1, keepdims=True)
    y = ((y - mean) * lax.rsqrt(var + LN_X_EPS)).reshape(bsz, t, RW_WIDTH) * ln_w.astype(f32) + ln_b.astype(f32)
    bonus = jnp.sum(rh * (k_f + k_b) * r_k.astype(f32), axis=-1, keepdims=True) * vh
    gate = jax.nn.sigmoid(gd) @ g2.astype(f32)
    out = (y + bonus.reshape(bsz, t, RW_WIDTH)) * gate
    return out, s_fwd, s_bwd

def centred_depthwise_conv(u, w):
    ch = u.shape[-1]
    return lax.conv_general_dilated(u, w.astype(jnp.float32)[:, None, :], window_strides=(1,), padding=[(SSM_CONV // 2, SSM_CONV // 2)], dimension_numbers=('NWC', 'WIO', 'NWC'), feature_group_count=ch)

def ssd_chunked(xdt, log_a, bm, cm, h0):
    bsz, t = xdt.shape[:2]
    nc = t // SSM_CHUNK
    xdt = xdt.reshape(bsz, nc, SSM_CHUNK, SSM_GROUPS, SSM_HPG, SSM_HEADDIM)
    log_a = log_a.reshape(bsz, nc, SSM_CHUNK, SSM_GROUPS, SSM_HPG)
    bm = bm.reshape(bsz, nc, SSM_CHUNK, SSM_GROUPS, SSM_STATE)
    cm = cm.reshape(bsz, nc, SSM_CHUNK, SSM_GROUPS, SSM_STATE)
    cs = jnp.cumsum(log_a, axis=2)
    cs_t = jnp.moveaxis(cs, 2, -1)
    lower = jnp.tril(jnp.ones((SSM_CHUNK, SSM_CHUNK), dtype=bool))
    seg = jnp.exp(jnp.where(lower, cs_t[..., :, None] - cs_t[..., None, :], -jnp.inf))
    cb = jnp.einsum('bclgn,bcsgn->bcgls', cm, bm)
    y_diag = jnp.einsum('bcgels,bcsgep->bclgep', cb[:, :, :, None] * seg, xdt)
    to_end = jnp.exp(cs[:, :, -1:] - cs)
    states = jnp.einsum('bclgn,bclgep->bcgepn', bm, xdt * to_end[..., None])
    chunk_decay = jnp.exp(cs[:, :, -1])

    def carry_step(h, inp):
        st, dec = inp
        return h * dec[..., None, None] + st, h
    h_last, h_in = lax.scan(carry_step, h0, (jnp.moveaxis(states, 1, 0), jnp.moveaxis(chunk_decay, 1, 0)))
    h_in = jnp.moveaxis(h_in, 0, 1)
    y_off = jnp.einsum('bclgn,bcgepn->bclgep', cm, h_in) * jnp.exp(cs)[..., None]
    return (y_diag + y_off).reshape(bsz, t, SSM_GROUPS, SSM_HPG, SSM_HEADDIM), h_last

def mamba2_branch(xbc, dt_raw, h0_fwd, h0_bwd, conv_w, conv_b, dt_bias, a_log, d_skip):
    bsz, t, _ = xbc.shape
    f32 = jnp.float32
    xbc = jax.nn.silu(centred_depthwise_conv(xbc.astype(f32), conv_w) + conv_b.astype(f32))
    xs, bm, cm = jnp.split(xbc, (SSM_WIDTH, SSM_WIDTH + SSM_GROUPS * SSM_STATE), axis=-1)
    xs = xs.reshape(bsz, t, SSM_GROUPS, SSM_HPG, SSM_HEADDIM)
    bm = bm.reshape(bsz, t, SSM_GROUPS, SSM_STATE)
    cm = cm.reshape(bsz, t, SSM_GROUPS, SSM_STATE)
    dt = jax.nn.softplus(dt_raw.astype(f32).reshape(bsz, t, 2, SSM_HEADS) + dt_bias.astype(f32))
    dt = dt.reshape(bsz, t, 2, SSM_GROUPS, SSM_HPG)
    log_a = -jnp.exp(a_log.astype(f32)).reshape(2, SSM_GROUPS, SSM_HPG) * dt
    y_f, h_f = ssd_chunked(xs * dt[:, :, 0, ..., None], log_a[:, :, 0], bm, cm, h0_fwd)
    flip = lambda u: jnp.flip(u, axis=1)
    y_b, h_b = ssd_chunked(flip(xs * dt[:, :, 1, ..., None]), flip(log_a[:, :, 1]), flip(bm), flip(cm), h0_bwd)
    y = y_f + flip(y_b) + d_skip.astype(f32).reshape(SSM_GROUPS, SSM_HPG)[..., None] * xs
    return y.reshape(bsz, t, SSM_WIDTH), h_f, h_b

def gated_group_rmsnorm(y, z, gain):
    bsz, t, _ = y.shape
    u = (y * jax.nn.silu(z.astype(jnp.float32))).reshape(bsz, t, SSM_GROUPS, SSM_WIDTH // SSM_GROUPS)
    u = u * lax.rsqrt(jnp.mean(u * u, axis=-1, keepdims=True) + NORM_EPS)
    return u.reshape(bsz, t, SSM_WIDTH) * gain.astype(jnp.float32)

def merge_branches(y_a, y_b, gates, w_a, w_b, w_o):
    g_a, g_b = jnp.split(gates, 2, axis=-1)
    m = jax.nn.sigmoid(g_a) * (y_a @ w_a) + jax.nn.sigmoid(g_b) * (y_b @ w_b)
    return m @ w_o

def peer_ffn(h, wq, subkeys, u_tab, v_tab):
    bsz, t, d = h.shape
    n = bsz * t
    tok = h.reshape(n, d)
    q = (tok @ wq).astype(jnp.float32).reshape(n, PEER_HEADS, 2, PEER_HALF)
    s = jnp.einsum('nhsd,hskd->nhsk', q, subkeys.astype(jnp.float32))
    top_s, top_i = lax.top_k(s, PEER_TOPK)
    cand = (top_s[:, :, 0, :, None] + top_s[:, :, 1, None, :]).reshape(n, PEER_HEADS, PEER_TOPK * PEER_TOPK)
    best_s, best_j = lax.top_k(cand, PEER_TOPK)
    i1 = jnp.take_along_axis(top_i[:, :, 0], best_j // PEER_TOPK, axis=-1)
    i2 = jnp.take_along_axis(top_i[:, :, 1], best_j % PEER_TOPK, axis=-1)
    expert = i1 * PEER_KEYS + i2
    gate = jax.nn.softmax(best_s, axis=-1)

    def block(args):
        xb, eb, gb = args
        act = jax.nn.gelu(jnp.einsum('nd,nhkd->nhk', xb, jnp.take(u_tab, eb, axis=0)), approximate=False)
        return jnp.einsum('nhk,nhkd->nd', (gb * act).astype(v_tab.dtype), jnp.take(v_tab, eb, axis=0))
    nb = n // PEER_BLOCK
    out = lax.map(block, (tok.reshape(nb, PEER_BLOCK, d), expert.reshape(nb, PEER_BLOCK, PEER_HEADS, PEER_TOPK), gate.reshape(nb, PEER_BLOCK, PEER_HEADS, PEER_TOPK)))
    return out.reshape(bsz, t, d).astype(h.dtype)

def setup_inputs(seed: int = 0) -> dict:
    key = jax.random.key(seed)
    ks = iter(jax.random.split(key, 48))
    L, D = DEPTH, D_MODEL
    nrm = lambda shape, scale: scale * jax.random.normal(next(ks), shape, jnp.float32)
    uni = lambda shape, lo, hi: jax.random.uniform(next(ks), shape, jnp.float32, minval=lo, maxval=hi)
    dt_init = jnp.exp(uni((L, 2, SSM_HEADS), math.log(1e-3), math.log(1e-1)))
    return {
        'x': nrm((BATCH, SEQ, D), 1.0),
        'c': nrm((BATCH, D), 1.0),
        'ctx': nrm((BATCH, CTX_LEN, D), 1.0),
        'c_ctx': nrm((D,), 1.0),
        'w_mod': nrm((L, D, N_MOD * D), 0.5 * D ** -0.5),
        'b_mod': nrm((L, N_MOD * D), 0.02),
        'norm_pre1': 1.0 + nrm((L, D), 0.1),
        'norm_post1': 1.0 + nrm((L, D), 0.1),
        'norm_pre2': 1.0 + nrm((L, D), 0.1),
        'norm_post2': 1.0 + nrm((L, D), 0.1),
        'w_in': nrm((L, D, IN_COLS), D ** -0.5),
        'rw_mu': uni((L, RW_COLS), 0.0, 1.0),
        'rw_w0': uni((L, 2, RW_WIDTH), -5.0, -1.0),
        'rw_w2': nrm((L, 2, LORA_W, RW_WIDTH), 0.1 * LORA_W ** -0.5),
        'rw_a0': nrm((L, 2, RW_WIDTH), 0.5),
        'rw_a2': nrm((L, 2, LORA_A, RW_WIDTH), 0.1 * LORA_A ** -0.5),
        'rw_g2': nrm((L, LORA_G, RW_WIDTH), LORA_G ** -0.5),
        'rw_k_k': 0.85 + nrm((L, RW_WIDTH), 0.05),
        'rw_k_a': 1.0 + nrm((L, RW_WIDTH), 0.05),
        'rw_r_k': nrm((L, RW_HEADS, RW_HEAD), 0.1),
        'rw_ln_w': 1.0 + nrm((L, RW_WIDTH), 0.1),
        'rw_ln_b': nrm((L, RW_WIDTH), 0.02),
        'ssm_conv_w': nrm((L, SSM_CONV, XBC_COLS), SSM_CONV ** -0.5),
        'ssm_conv_b': nrm((L, XBC_COLS), 0.02),
        'ssm_dt_bias': dt_init + jnp.log(-jnp.expm1(-dt_init)),
        'ssm_a_log': jnp.log(uni((L, 2, SSM_HEADS), 1.0, 16.0)),
        'ssm_d': 1.0 + nrm((L, SSM_HEADS), 0.1),
        'ssm_norm_w': 1.0 + nrm((L, SSM_WIDTH), 0.1),
        'w_branch_a': nrm((L, RW_WIDTH, D), RW_WIDTH ** -0.5),
        'w_branch_b': nrm((L, SSM_WIDTH, D), SSM_WIDTH ** -0.5),
        'w_out': nrm((L, D, D), D ** -0.5),
        'peer_wq': nrm((L, D, PEER_HEADS * PEER_QDIM), D ** -0.5),
        'peer_subkeys': nrm((L, PEER_HEADS, 2, PEER_KEYS, PEER_HALF), PEER_HALF ** -0.5),
        'peer_u': nrm((L, PEER_EXPERTS, D), D ** -0.5),
        'peer_v': nrm((L, PEER_EXPERTS, D), D ** -0.5),
    }

def reference(x, c, ctx, c_ctx, w_mod, b_mod, norm_pre1, norm_post1, norm_pre2, norm_post2, w_in, rw_mu, rw_w0, rw_w2, rw_a0, rw_a2, rw_g2, rw_k_k, rw_k_a, rw_r_k, rw_ln_w, rw_ln_b, ssm_conv_w, ssm_conv_b, ssm_dt_bias, ssm_a_log, ssm_d, ssm_norm_w, w_branch_a, w_branch_b, w_out, peer_wq, peer_subkeys, peer_u, peer_v):
    act_dtype = x.dtype
    bsz, seq, _ = x.shape
    rows = seq // GRID_W
    rw_zero = jnp.zeros((bsz, RW_HEADS, RW_HEAD, RW_HEAD), jnp.float32)
    ssm_zero = jnp.zeros((bsz, SSM_GROUPS, SSM_HPG, SSM_HEADDIM, SSM_STATE), jnp.float32)
    for l in range(DEPTH):
        mod_x = (jax.nn.silu(c) @ w_mod[l] + b_mod[l])[:, None, :]
        mod_c = (jax.nn.silu(c_ctx) @ w_mod[l] + b_mod[l])[None, None, :]
        sh1x, sc1x, g1x, sh2x, sc2x, g2x = jnp.split(mod_x, N_MOD, axis=-1)
        sh1c, sc1c, g1c, sh2c, sc2c, g2c = jnp.split(mod_c, N_MOD, axis=-1)

        hx = rms_norm(x, norm_pre1[l]) * (1.0 + sc1x) + sh1x
        hc = rms_norm(ctx, norm_pre1[l]) * (1.0 + sc1c) + sh1c
        rw_x, z_x, xbc_x, dt_x, gate_x = jnp.split(hx @ w_in[l], IN_SPLITS, axis=-1)
        rw_c, z_c, xbc_c, dt_c, gate_c = jnp.split(hc @ w_in[l], IN_SPLITS, axis=-1)

        rw_params = (rw_w0[l], rw_w2[l], rw_a0[l], rw_a2[l], rw_g2[l], rw_k_k[l], rw_k_a[l], rw_r_k[l], rw_ln_w[l], rw_ln_b[l])
        ya_c, s_fwd, s_bwd = rwkv7_branch(centred_token_shift(rw_c, rw_mu[l]), rw_zero, rw_zero, *rw_params)
        ya_x, _, _ = rwkv7_branch(centred_token_shift(rw_x, rw_mu[l]), s_fwd, s_bwd, *rw_params)

        ssm_params = (ssm_conv_w[l], ssm_conv_b[l], ssm_dt_bias[l], ssm_a_log[l], ssm_d[l])
        yb_c, h_fwd, h_bwd = mamba2_branch(xbc_c, dt_c, ssm_zero, ssm_zero, *ssm_params)
        yb_x, _, _ = mamba2_branch(raster_to_column(xbc_x, rows), raster_to_column(dt_x, rows), h_fwd, h_bwd, *ssm_params)
        yb_x = column_to_raster(yb_x, rows)

        mix_x = merge_branches(ya_x.astype(act_dtype), gated_group_rmsnorm(yb_x, z_x, ssm_norm_w[l]).astype(act_dtype), gate_x, w_branch_a[l], w_branch_b[l], w_out[l])
        x = x + g1x * rms_norm(mix_x, norm_post1[l])

        h2x = rms_norm(x, norm_pre2[l]) * (1.0 + sc2x) + sh2x
        x = x + g2x * rms_norm(peer_ffn(h2x, peer_wq[l], peer_subkeys[l], peer_u[l], peer_v[l]), norm_post2[l])

        if l + 1 < DEPTH:
            mix_c = merge_branches(ya_c.astype(act_dtype), gated_group_rmsnorm(yb_c, z_c, ssm_norm_w[l]).astype(act_dtype), gate_c, w_branch_a[l], w_branch_b[l], w_out[l])
            ctx = ctx + g1c * rms_norm(mix_c, norm_post1[l])
            h2c = rms_norm(ctx, norm_pre2[l]) * (1.0 + sc2c) + sh2c
            ctx = ctx + g2c * rms_norm(peer_ffn(h2c, peer_wq[l], peer_subkeys[l], peer_u[l], peer_v[l]), norm_post2[l])
    return x


_drawn_inputs = setup_inputs


def setup_inputs(seed=0):
    import zlib

    import numpy as np

    out = dict(_drawn_inputs(seed))
    spreads = {}
    factors = {'rw_w2': 4.268, 'rw_ln_b': 3.322}
    for name, (base, spread) in spreads.items():
        noise = np.random.default_rng([zlib.crc32(name.encode()), seed]).standard_normal(out[name].shape)
        drawn = base * np.exp(spread * noise) if base else spread * noise
        out[name] = jnp.asarray(drawn.astype(out[name].dtype))
    for name, factor in factors.items():
        out[name] = (out[name] * factor).astype(out[name].dtype)
    return out
```

```python
from contextlib import ExitStack

import concourse.bass as bass
from concourse import mybir

F32 = mybir.dt.float32
U32 = mybir.dt.uint32
ALU = mybir.AluOpType
ACT = mybir.ActivationFunctionType
AX = mybir.AxisListType.X
ds = bass.ds

P = 128
D = 2048
KC = D // P
SEQ = 256
TOK = 2 * SEQ
NT = TOK // P
GRID_W = 64
GRID_R = SEQ // GRID_W
EPS = 1e-6
HEAD = 64
PAIRS = D // P
LW, LA, LG = 96, 96, 256
LN_X_EPS = 64e-5
GROUPS = 8
GW = D // GROUPS
STATE = 128
CONV = 5
SH = 32
R0, K0, V0, L0 = 0, D, 2 * D, 3 * D
RW_COLS = 3 * D + 2 * LW + 2 * LA + LG
Z0 = RW_COLS
X0 = Z0 + D
B0 = X0 + D
C0 = B0 + GROUPS * STATE
DT0 = C0 + GROUPS * STATE
GA0 = DT0 + 2 * SH
N_MOD = 6
PH, PK, TOPK = 8, 128, 16
SLOTS = PH * TOPK
DECAY = -0.6065306597126334


class Steps:

    def __init__(self, sem, names, loop=False):
        self.sem, self.names, self.at = sem, names.split(), 0
        assert len(set(self.names)) == len(self.names), [n for n in self.names if self.names.count(n) > 1]
        self.n = len(self.names)
        self.base = self.n if loop else 0

    def open(self, engine):
        engine.sem_inc(self.sem, self.n)

    def did(self, name):
        assert self.at < self.n and self.names[self.at] == name, (name, self.names[self.at:self.at + 2])
        self.at += 1
        return self.sem, 1

    def by(self, name, turn=0):
        return self.sem, turn * self.n + (self.base + self.names.index(name) + 1)

    def before(self, name, turn):
        return self.sem, turn * self.n + (self.names.index(name) + 1)

    def end(self):
        assert self.at == self.n, self.names[self.at:]


def wait_alone(engine, passed, sem, value):
    engine.wait_ge(sem, value)
    engine.sem_inc(passed, 1)


def vector_rows(a):
    rows, at = {}, 0

    def add(name, ap, n, width=P):
        nonlocal at
        rows[name] = (at, ap, n, width)
        at += n

    for name in ("norm_pre1", "norm_post1", "norm_pre2", "norm_post2"):
        add(name, a[name].rearrange("l (j p) -> (l j) p", p=P), KC)
    add("a0", a["rw_a0"].rearrange("l d (j p) -> (l d j) p", p=P), 2 * KC)
    for name in ("rw_k_k", "rw_k_a", "rw_ln_w", "rw_ln_b", "ssm_norm_w"):
        add(name, a[name].rearrange("l (j p) -> (l j) p", p=P), KC)
    add("rw_r_k", a["rw_r_k"].rearrange("l (j e) k -> (l j) (e k)", e=2), KC)
    add("mu", a["rw_mu"][:, 0:L0].rearrange("l (j p) -> (l j) p", p=P), L0 // P)
    add("mu_l", a["rw_mu"][:, L0:L0 + 4 * LW].rearrange("l (j p) -> (l j) p", p=LW), 4, LW)
    add("mu_g", a["rw_mu"][:, L0 + 4 * LW:RW_COLS].rearrange("l (j p) -> (l j) p", p=P), 2)
    add("conv_w", a["ssm_conv_w"].rearrange("l t (j p) -> (l t j) p", p=P), CONV * (D + 2 * GROUPS * STATE) // P)
    add("conv_b", a["ssm_conv_b"].rearrange("l (j p) -> (l j) p", p=P), (D + 2 * GROUPS * STATE) // P)
    add("b_mod", a["b_mod"].rearrange("l (j p) -> (l j) p", p=P), N_MOD * KC)
    add("c", a["c"].rearrange("l (j p) -> (l j) p", p=P), KC)
    add("c_ctx", a["c_ctx"].rearrange("(j p) -> j p", p=P), KC)
    return rows, at


def hybrid_block(nc, a, out):
    rows, n_rows = vector_rows(a)
    tiles = (n_rows + P - 1) // P
    col = {name: r[0] for name, r in rows.items()}

    with ExitStack() as whole:
        whole.enter_context(nc.allow_non_contiguous_dma("weights are read in slices of columns"))
        def sb(name, shape, dt=F32, ctx=whole):
            return ctx.enter_context(nc.sbuf_tensor(name, shape, dt))

        def sem(name):
            return whole.enter_context(nc.semaphore(name))

        ps = whole.enter_context(nc.psum_tensor("ps", [P, 8, 512], F32))
        ident = sb("ident", [P, P])
        ones = sb("ones", [P, P])
        head_ones = sb("head_ones", [P, P])
        head_mean = sb("head_mean", [P, P])
        tri = sb("tri", [P, 2, 2, P])
        below = sb("below", [P, 2, 2, P])
        par = sb("par", [P, (tiles + 1) * P])
        modT = sb("modT", [P, N_MOD * KC, 2])
        hT = sb("hT", [P, KC, TOK])
        yaT = sb("yaT", [P, KC, SEQ])
        minus_half = sb("minus_half", [P, 1])
        pc = lambda name, j=0, n=1: par[:, col[name] + j:col[name] + j + n]
        SKIP_D = tiles * P

        setup(nc, sb, sem, ps, a, rows, tiles, ident, ones, head_ones, head_mean, tri, below, minus_half, par, modT)
        norm_in(nc, sb, sem, ps, a, ident, minus_half, par, col, modT, hT)
        rwkv(nc, sb, sem, ps, a, ident, head_ones, head_mean, tri, below, par, col, hT, yaT)
        ybT = sb("ybT", [P, KC, SEQ])
        ssd(nc, sb, sem, ps, a, ident, ones, below, par, col, SKIP_D, hT, ybT)
        xT = sb("xT", [P, KC, SEQ])
        merge(nc, sb, sem, ps, a, ident, ones, par, col, modT, hT, yaT, ybT, xT)
        peer(nc, sb, sem, ps, a, out, ident, ones, par, col, modT, hT, yaT, ybT, xT)


def setup(nc, sb, sem, ps, a, rows, tiles, ident, ones, head_ones, head_mean, tri, below, minus_half, par, modT):
    with ExitStack() as stage:
        raw = sb("raw", [P, tiles + 1, P], ctx=stage)
        skip = sb("skip", [KC, 2], ctx=stage)
        silu_c = sb("silu_c", [P, KC, 2], ctx=stage)
        sig_c = sb("sig_c", [P, KC, 2], ctx=stage)
        w = sb("w_mod_ring", [P, 2, KC, 512], ctx=stage)
        mod_row = sb("mod_row", [2, 2, 512], ctx=stage)
        consts = sem("consts")
        raw_clear, raw_in = sem("raw_clear"), sem("raw_in")
        w_in = [sem("w_mod_in0"), sem("w_mod_in1")]
        par_tr, par_done, c_sig, c_done = sem("par_tr"), sem("par_done"), sem("c_sig"), sem("c_done")
        skip_done = sem("skip_done")
        row_mm, row_copied, row_tr, mod_done = sem("row_mm"), sem("row_copied"), sem("row_tr"), sem("mod_done")
        w_mod = a["w_mod"].rearrange("l (k p) n -> (l p) k n", p=P)
        BLOCKS = N_MOD * D // 512
        pieces = []
        for name, (at, ap, n, width) in rows.items():
            done = 0
            while done < n:
                tile, row = divmod(at + done, P)
                k = min(n - done, P - row)
                pieces.append((tile, row, k, width, ap[done:done + k, :]))
                done += k

        with nc.Block() as block:

            @block.gpsimd
            def _(pool):
                nc.gpsimd.memset(raw[:, :, :], 0.0).then_inc(raw_clear, 1)
                count = [0]

                def const(ins):
                    count[0] += 1
                    ins.then_inc(consts, 1)
                    pool.wait_ge(consts, count[0])

                def sel(ap, cmp, fill, base, cm, pattern):
                    const(nc.gpsimd.affine_select(out=ap, in_=ap, compare_op=cmp, fill=fill, base=base,
                                                  pattern=pattern, channel_multiplier=cm))

                const(nc.gpsimd.memset(minus_half[:, :], -0.5))
                const(nc.gpsimd.memset(ident[:, :], 0.0))
                sel(ident[:, :], ALU.not_equal, 1.0, 0, 1, [[-1, P]])
                const(nc.gpsimd.memset(ones[:, :], 1.0))
                for t, v in ((head_ones, 1.0), (head_mean, 1.0 / HEAD)):
                    const(nc.gpsimd.memset(t[:, :], 0.0))
                    const(nc.gpsimd.memset(t[0:HEAD, 0:HEAD], v))
                    const(nc.gpsimd.memset(t[HEAD:P, HEAD:P], v))
                const(nc.gpsimd.memset(tri[:, :, :, :], 0.5))
                const(nc.gpsimd.memset(below[:, :, :, :], 1.0))
                for d, sign in ((0, 1), (1, -1)):
                    for e, base in ((0, 0), (1, -1)):
                        sel(tri[:, d, e, :], ALU.is_ge, -0.5, base, -sign, [[sign, P]])
                    for e, base in ((0, -1), (1, 0)):
                        sel(below[:, d, e, :], ALU.is_ge, 0.0, base, -sign, [[sign, P]])
                CONSTS[0] = count[0]

            @block.sync
            def _(sp):
                for n in range(2):
                    sp.dma_start(w[:, n, :, :], w_mod[:, :, n * 512:(n + 1) * 512]).then_inc(w_in[n], 16)
                with sp.Fori(1, BLOCKS // 2) as i:
                    for n in range(2):
                        sp.wait_ge(row_mm, i * 2 + n - 1)
                        sp.dma_start(w[:, n, :, :],
                                     w_mod[:, :, ds(i * 1024 + n * 512, 512)]).then_inc(w_in[n], 16)

            @block.scalar
            def _(act):
                act.dma_start(skip[:, :], a["ssm_d"].rearrange("l (j e) -> (l j) e", e=2)).then_inc(raw_in, 16)
                act.wait_ge(raw_clear, 1)
                for tile, row, k, width, src in pieces:
                    act.dma_start(raw[row:row + k, tile, 0:width], src).then_inc(raw_in, 16)
                act.wait_ge(par_done, 2)
                c0 = rows["c"][0]
                for e in range(2):
                    nc.scalar.activation(sig_c[:, :, e], par[:, c0 + e * KC:c0 + (e + 1) * KC],
                                         ACT.Sigmoid).then_inc(c_sig, 1)
                with act.Fori(0, BLOCKS // 2) as i:
                    for n in range(2):
                        act.wait_ge(row_mm, i * 2 + n + 1)
                        nc.scalar.activation(mod_row[:, n, :], ps[0:2, n, :], ACT.Copy).then_inc(row_copied, 1)

            @block.vector
            def _(dve):
                dve.wait_ge(raw_in, 16 * (len(pieces) + 1))
                for e in range(2):
                    nc.vector.tensor_copy(raw[0:KC, tiles, e * HEAD:(e + 1) * HEAD],
                                          skip[:, e:e + 1].broadcast_to([KC, HEAD])).then_inc(skip_done, 1)
                for half in range(2):
                    lo, hi = half * 4, min(tiles + 1, half * 4 + 4)
                    dve.wait_ge(par_tr, hi)
                    nc.vector.tensor_copy(par[:, lo * P:hi * P], ps[:, 2 + half, 0:(hi - lo) * P]).then_inc(par_done, 1)
                dve.wait_ge(c_sig, 2)
                c0 = rows["c"][0]
                for e in range(2):
                    nc.vector.tensor_tensor(silu_c[:, :, e], sig_c[:, :, e], par[:, c0 + e * KC:c0 + (e + 1) * KC],
                                            ALU.mult).then_inc(c_done, 1)
                b0 = rows["b_mod"][0]
                dve.sem_inc(mod_done, 2)
                with dve.Fori(0, BLOCKS // 2) as i:
                    for n in range(2):
                        dve.wait_ge(row_tr, i * 2 + n + 1)
                        nc.vector.tensor_tensor(
                            modT[:, ds(i * 8 + n * 4, 4), :],
                            ps[:, 4 + n, 0:8].rearrange("p (j e) -> p j e", e=2),
                            par[:, ds(i * 8 + b0 + n * 4, 4)].unsqueeze(2).broadcast_to([P, 4, 2]),
                            ALU.add).then_inc(mod_done, 1)

            @block.tensor
            def _(pe):
                pe.wait_ge(consts, CONSTS[0])
                pe.wait_ge(raw_in, 16 * (len(pieces) + 1))
                pe.wait_ge(skip_done, 2)
                for t in range(tiles + 1):
                    nc.tensor.transpose(ps[:, 2 + t // 4, (t % 4) * P:(t % 4 + 1) * P], raw[:, t, :],
                                        ident[:, :]).then_inc(par_tr, 1)
                pe.wait_ge(c_done, 2)

                def turn_rows(count, n, guard):
                    pe.wait_ge(row_copied, count + 1)
                    pe.wait_ge(mod_done, guard)
                    for j in range(4):
                        last = nc.tensor.matmul(ps[:, 4 + n, 2 * j:2 * j + 2], mod_row[:, n, j * P:(j + 1) * P],
                                                ident[0:2, 0:2], start=True, stop=True)
                    last.then_inc(row_tr, 1)

                with pe.Fori(0, BLOCKS // 2) as i:
                    for n in range(2):
                        pe.wait_ge(w_in[n], i * 16 + 16)
                        for k in range(KC):
                            last = nc.tensor.matmul(ps[0:2, n, :], silu_c[:, k, :], w[:, n, k, :],
                                                    start=(k == 0), stop=(k == KC - 1))
                        last.then_inc(row_mm, 1)
                    for n in range(2):
                        turn_rows(i * 2 + n, n, i * 2 + 2)


CONSTS = [0]


def norm_in(nc, sb, sem, ps, a, ident, minus_half, par, col, modT, hT):
    with ExitStack() as stage:
        rows = sb("in_rows", [P, NT, D], ctx=stage)
        junk = sb("in_sq", [P, D], ctx=stage)
        ssq = sb("in_ssq", [P, NT], ctx=stage)
        rstd = sb("in_rstd", [P, NT], ctx=stage)
        gain = sb("in_gain", [P, KC, 2], ctx=stage)
        rows_in = [sem(f"rows_in{t}") for t in range(NT)]
        sq_done, rstd_done, gain_done, scaled, turned, h_done = (
            sem(x) for x in ("in_sq_done", "in_rstd_done", "in_gain_done", "in_scaled", "in_turned", "h_done"))
        srcs = [a["ctx"], a["ctx"], a["x"], a["x"]]
        with nc.Block() as block:

            @block.sync
            def _(sp):
                for t in range(NT):
                    lo = (t % 2) * P
                    sp.dma_start(rows[:, t, :], srcs[t][0, lo:lo + P, :]).then_inc(rows_in[t], 16)

            @block.scalar
            def _(act):
                for t in range(NT):
                    act.wait_ge(rows_in[t], 16)
                    if t:
                        act.wait_ge(sq_done, t)
                    nc.scalar.activation(junk[:, :], rows[:, t, :], ACT.Square,
                                         accum_out=ssq[:, t:t + 1]).then_inc(sq_done, 1)

            @block.gpsimd
            def _(pool):
                pool.wait_ge(sq_done, NT)
                nc.gpsimd.tensor_scalar(rstd[:, :], ssq[:, :], 1.0 / D, EPS, ALU.mult, ALU.add).then_inc(rstd_done, 1)
                pool.wait_ge(rstd_done, 1)
                nc.gpsimd.tensor_tensor(rstd[:, :], rstd[:, :], minus_half[:, 0:1].broadcast_to([P, NT]),
                                        ALU.pow).then_inc(rstd_done, 1)

            @block.vector
            def _(dve):
                g0 = col["norm_pre1"]
                nc.vector.scalar_tensor_tensor(gain[:, :, :], modT[:, KC:2 * KC, :], 1.0,
                                               par[:, g0:g0 + KC].unsqueeze(2).broadcast_to([P, KC, 2]),
                                               ALU.add, ALU.mult).then_inc(gain_done, 1)
                dve.wait_ge(rstd_done, 2)
                for t in range(NT):
                    nc.vector.tensor_scalar(rows[:, t, :], rows[:, t, :], rstd[:, t:t + 1], None,
                                            ALU.mult).then_inc(scaled, 1)
                dve.wait_ge(gain_done, 1)
                for j in range(KC):
                    dve.wait_ge(turned, j + 1)
                    for s, e in ((0, 1), (1, 0)):
                        nc.vector.tensor_scalar(hT[:, j, s * SEQ:(s + 1) * SEQ], ps[:, j % 4, s * SEQ:(s + 1) * SEQ],
                                                gain[:, j, e:e + 1], modT[:, j, e:e + 1],
                                                ALU.mult, ALU.add).then_inc(h_done, 1)

            @block.tensor
            def _(pe):
                pe.wait_ge(scaled, NT)
                for j in range(KC):
                    if j >= 4:
                        pe.wait_ge(h_done, 2 * (j - 3))
                    for t in range(NT):
                        last = nc.tensor.transpose(ps[:, j % 4, t * P:(t + 1) * P], rows[:, t, j * P:(j + 1) * P],
                                                   ident[:, :])
                    last.then_inc(turned, 1)


PP = ["om_k", "hm_k", "om_v", "hm_v", "om_r", "hm_r", "k_k", "k_a", "om_ka", "a0f", "a0b", "r_k", "ln_w", "ln_b"]


def lora(nc, sb, sem, ps, a, par, col, hT, per_pair, tanh_w, low_a, gate_g):
    with ExitStack() as stage:
        w = sb("w_lora", [P, KC, 4 * LW + LG], ctx=stage)
        om = sb("lora_om", [P, 54], ctx=stage)
        hm = sb("lora_hm", [P, 54], ctx=stage)
        pad = sb("lora_pad", [P, 6, 2, SEQ + 2], ctx=stage)
        kept = sb("lora_kept", [P, 6, TOK], ctx=stage)
        near = sb("lora_near", [P, 6, TOK], ctx=stage)
        w_in, proj, padded, keeps, added, shifted, mus, pads, funcs = (
            sem(x) for x in ("lora_w", "lora_proj", "lora_padded", "lora_keeps", "lora_added", "lora_shifted",
                             "lora_mus", "lora_pads", "lora_funcs"))
        src = a["w_in"].rearrange("l (k p) n -> (l p) k n", p=P)
        m0 = col["mu"]
        parts = [(j * LW, LW, 0) for j in range(4)] + [(4 * LW + j * P, P, SEQ) for j in range(2)]
        with nc.Block() as block:

            @block.sync
            def _(sp):
                sp.dma_start(w[:, :, :], src[:, :, L0:RW_COLS]).then_inc(w_in, 16)

            @block.gpsimd
            def _(pool):
                nc.gpsimd.memset(pad[:, :, :, :], 0.0).then_inc(pads, 1)
                pool.wait_ge(pads, 1)
                nc.gpsimd.memset(tanh_w[LW:LW + 1, :, :], 1.0).then_inc(pads, 1)

            @block.tensor
            def _(pe):
                pe.wait_ge(w_in, 16)
                for n, (c, m, t0) in enumerate(parts):
                    for k in range(KC):
                        last = nc.tensor.matmul(ps[0:m, n, t0:TOK], w[:, k, c:c + m], hT[:, k, t0:TOK],
                                                start=(k == 0), stop=(k == KC - 1))
                    last.then_inc(proj, 1)

            @block.scalar
            def _(act):
                act.wait_ge(pads, 1)
                act.wait_ge(mus, 2)
                for n, (c, m, t0) in enumerate(parts):
                    act.wait_ge(proj, n + 1)
                    s0 = t0 // SEQ
                    nc.scalar.activation(pad[0:m, n, s0:2, 1:SEQ + 1],
                                         ps[0:m, n, t0:TOK].rearrange("p (s t) -> p s t", t=SEQ),
                                         ACT.Copy).then_inc(padded, 1)
                    nc.scalar.activation(kept[0:m, n, t0:TOK], ps[0:m, n, t0:TOK], ACT.Copy,
                                         scale=om[0:m, 48 + n:49 + n]).then_inc(keeps, 1)
                for d in range(2):
                    act.wait_ge(shifted, d + 1)
                    nc.scalar.activation(tanh_w[0:LW, d, :], near[0:LW, d, :], ACT.Tanh).then_inc(funcs, 1)
                for j in range(2):
                    act.wait_ge(shifted, 5 + j)
                    nc.scalar.activation(gate_g[:, j, :], near[:, 4 + j, SEQ:TOK], ACT.Sigmoid).then_inc(funcs, 1)

            @block.vector
            def _(dve):
                nc.vector.tensor_scalar(om[:, :], par[:, m0:m0 + 54], -1.0, 1.0, ALU.mult, ALU.add).then_inc(mus, 1)
                nc.vector.tensor_scalar(hm[:, :], par[:, m0:m0 + 54], 0.5, None, ALU.mult).then_inc(mus, 1)
                dve.wait_ge(mus, 2)
                cols = {"k_k": col["rw_k_k"], "k_a": col["rw_k_a"], "a0f": col["a0"], "a0b": col["a0"] + KC,
                        "r_k": col["rw_r_k"], "ln_w": col["rw_ln_w"], "ln_b": col["rw_ln_b"]}
                for n, name in enumerate(PP):
                    if name in cols:
                        c = cols[name]
                        nc.vector.tensor_copy(per_pair[:, :, n], par[:, c:c + KC])
                    elif name == "om_ka":
                        c = col["rw_k_a"]
                        nc.vector.tensor_scalar(per_pair[:, :, n], par[:, c:c + KC], -1.0, 1.0, ALU.mult, ALU.add)
                    else:
                        t = om if name[0] == "o" else hm
                        c = {"r": 0, "k": KC, "v": 2 * KC}[name[-1]]
                        nc.vector.tensor_copy(per_pair[:, :, n], t[:, c:c + KC])
                for n, (c, m, t0) in enumerate(parts):
                    dve.wait_ge(padded, n + 1)
                    s0 = t0 // SEQ
                    view = near[0:m, n, t0:TOK].rearrange("p (s t) -> p s t", t=SEQ)
                    nc.vector.tensor_tensor(view, pad[0:m, n, s0:2, 0:SEQ], pad[0:m, n, s0:2, 2:SEQ + 2],
                                            ALU.add).then_inc(added, 1)
                    dve.wait_ge(added, n + 1)
                    dve.wait_ge(keeps, n + 1)
                    out = low_a[:, n - 2, :] if n in (2, 3) else near[0:m, n, t0:TOK]
                    nc.vector.scalar_tensor_tensor(out, near[0:m, n, t0:TOK], hm[0:m, 48 + n:49 + n],
                                                   kept[0:m, n, t0:TOK], ALU.mult, ALU.add).then_inc(shifted, 1)


def rwkv(nc, sb, sem, ps, a, ident, head_ones, head_mean, tri, below, par, col, hT, yaT):
    with ExitStack() as stage:
        def t(name, *shape):
            return sb(name, list(shape), ctx=stage)

        per_pair = t("per_pair", P, PAIRS, len(PP))
        tanh_w = t("tanh_w", LW + 1, 2, TOK)
        low_a = t("low_a", LA, 2, TOK)
        gate_g = t("gate_g", P, 2, SEQ)
        lora(nc, sb, sem, ps, a, par, col, hT, per_pair, tanh_w, low_a, gate_g)

        w = t("w_pair", P, 3, KC, P)
        lw2, la2, lg2 = t("lw2", LW + 1, 2, P), t("la2", LA, 2, P), t("lg2", P, 2, P)
        pp = t("pp", P, len(PP))
        blocks = t("blocks", P, 6, P)
        neg2 = t("neg2", P, 2, P)
        ident2 = t("ident2", P, P)
        ln_eps = t("ln_eps", P, 1)
        pad = t("pad", P, 3, 2, SEQ + 2)
        near = t("near", P, 3, TOK)
        kvr = t("kvr", P, 3, TOK)
        k_s, v_s, r_s = kvr[:, 0, :], kvr[:, 1, :], kvr[:, 2, SEQ:TOK]
        X, F = t("X", P, 4, NT, P), t("F", P, 4, NT, P)
        early = X[:, :, :, :].rearrange("p q n t -> p (q n t)")
        rate = early[:, 0:2 * TOK].rearrange("p (d t) -> p d t", d=2)
        rn, kk = early[:, 2 * TOK:3 * TOK], early[:, 3 * TOK:4 * TOK]
        sg, e_ng = F[:, 0:2, :, :], F[:, 2:4, :, :]
        sq, kd = t("sq", P, TOK), t("kd", P, 2, TOK)
        e_in = t("e_in", P, 2, NT, P)
        KR = t("KR", P, 2, NT, 2, P)
        Kh, Ah = t("Kh", P, 2, NT, P), t("Ah", P, 2, NT, P)
        em = t("em", P, 2, 3)
        Vt, Kt, At = t("Vt", P, NT, P), t("Kt", P, 2, NT, P), t("At", P, 2, NT, P)
        Gc, Gx = t("Gc", P, 4, 2, 2, P), t("Gx", P, 4, 2, 4, P)
        XT = t("XT", P, 4, NT, P)
        rhs, nsa, S = t("rhs", P, 4, HEAD), t("nsa", P, 4, HEAD), t("S", P, 2, HEAD)
        gate = t("gate", P, SEQ)
        y, yc, bonus = sq[:, 0:SEQ], sq[:, SEQ:TOK], t("bonus", P, SEQ)
        ysq, rs = rn[:, 0:SEQ], rn[:, SEQ:TOK]
        LEVELS = range(1, 7)
        QS = [(d, h) for d in range(2) for h in range(2)]
        order = [(0, 1, 2, 3), (1, 0, 3, 2)]

        w_sem, lw_sem, m_sem = sem("rw_w_in"), sem("rw_lw_in"), sem("rw_masks")
        PE = Steps(sem("rw_pe"), " ".join(
            ["u0", "u1", "a0", "a1", "gate", "k", "v", "r", "cs0", "cs1", "kss", "vt", "kt0", "at0", "kt1", "at1", "bonus"]
            + [f"g{q}{x}" for q in range(4) for x in "cxz"] + [f"x1_{q}" for q in range(4)]
            + [f"{m}{lev}_{q}" for lev in LEVELS for m in ("E", "X", "T") for q in range(4) if not (m == "X" and lev == 6)]
            + [f"{m}{j}" for j in range(4) for m in ("rhs", "sa", "y", "s") if not (m == "s" and j == 3 or m == "y" and j < 2)]
            + ["mean", "var"]), True)
        AC = Steps(sem("rw_act"), " ".join(
            ["sg0", "sg1", "rate0", "rate1", "gate"] + [f"{x}{n}" for n in range(3) for x in ("pad", "keep")]
            + [f"{x}{d}" for d in range(2) for x in ("exc", "inc", "neg")]
            + ["sq", "norm", "vt", "kt0", "at0", "kt1", "at1"] + [f"x1_{q}" for q in range(4)]
            + [f"xt_{q}" for q in range(4)] + [f"{m}{j}" for j in range(4) for m in ("rhs", "sa")] + ["yf", "ysq", "std"]), True)
        DV = Steps(sem("rw_dve"), " ".join(
            ["pp"] + [f"{x}{n}" for n in range(3) for x in ("near", "shift")]
            + ["nmax", "nrec", "kk"] + [f"{x}{d}" for d in range(2) for x in ("kdf", "kd", "KK", "Kh", "Ah")]
            + ["em0", "em1", "em2", "rk", "bv"] + [f"g{q}{x}" for q in range(4) for x in "cxz"]
            + [f"{m}{lev}_{q}" for lev in LEVELS for m in ("F", "X", "T") for q in range(4) if not (m != "F" and lev == 6)]
            + [f"s{j}_{d}" for j in range(3) for d in range(2)]
            + ["y", "yc", "rec", "yn", "yl", "yb", "out"]), True)
        PO = Steps(sem("rw_pool"), " ".join(
            ["aa0", "rr0", "aa1", "rr1", "kfb", "rkk"]
            + [f"{x}{q}{y}" for q in range(4) for y in "cx" for x in ("m2", "i2", "at")]), True)

        w_in = a["w_in"].rearrange("l (k p) n -> (l p) k n", p=P)
        w2, w0 = a["rw_w2"].rearrange("l d c n -> (l c) d n"), a["rw_w0"]
        a2 = a["rw_a2"].rearrange("l d c n -> (l c) d n")
        g2 = a["rw_g2"].rearrange("l (k p) n -> (l p) k n", p=P)
        head = lambda h: slice(h * HEAD, (h + 1) * HEAD)
        A_T = lambda q, n: Gc[:, q, n, 0, :] if n < 2 else Gx[:, q, n - 2, 0, :]
        B1 = lambda q, n: Gc[:, q, n, 1, :] if n < 2 else Gx[:, q, n - 2, 2, :]

        with nc.Block() as block:

            @block.sync
            def _(sp):
                with sp.Fori(0, PAIRS) as i:
                    sp.wait_ge(*PE.before("r", i))
                    for n, c0 in enumerate((K0, V0, R0)):
                        sp.dma_start(w[:, n, :, :], w_in[:, :, ds(i * P + c0, P)]).then_inc(w_sem, 16)
                    sp.wait_ge(*PE.before("gate", i))
                    sp.dma_start(lw2[0:LW, :, :], w2[:, :, ds(i * P, P)]).then_inc(lw_sem, 16)
                    sp.dma_start(lw2[LW:LW + 1, :, :], w0[:, :, ds(i * P, P)]).then_inc(lw_sem, 16)
                    sp.dma_start(la2[:, :, :], a2[:, :, ds(i * P, P)]).then_inc(lw_sem, 16)
                    sp.dma_start(lg2[:, :, :], g2[:, :, ds(i * P, P)]).then_inc(lw_sem, 16)

            @block.gpsimd
            def _(pool):
                count = [0]

                def const(ins):
                    count[0] += 1
                    ins.then_inc(m_sem, 1)
                    pool.wait_ge(m_sem, count[0])

                PO.open(pool)
                const(nc.gpsimd.memset(blocks[:, :, :], 1.0))
                const(nc.gpsimd.memset(pad[:, :, :, :], 0.0))
                const(nc.gpsimd.memset(ln_eps[:, :], LN_X_EPS))
                for n in range(6):
                    b = 2 << n
                    v = blocks[:, n, :].rearrange("p (j b) -> p j b", b=b)
                    for base, cm, step in ((0, 1, -b), (b - 1, -1, b)):
                        const(nc.gpsimd.affine_select(out=v, in_=v, compare_op=ALU.is_ge, fill=0.0, base=base,
                                                      pattern=[[step, P // b], [0, b]], channel_multiplier=cm))
                for d in range(2):
                    const(nc.gpsimd.tensor_tensor(neg2[:, d, :], blocks[:, 0, :], below[:, d, 0, :], ALU.mult))
                    const(nc.gpsimd.tensor_scalar(neg2[:, d, :], neg2[:, d, :], -1.0, None, ALU.mult))
                const(nc.gpsimd.tensor_scalar(ident2[:, :], ident[:, :], 2.0, None, ALU.mult))
                MASKS[0] = count[0]
                with pool.Fori(0, PAIRS) as i:
                    for d in range(2):
                        pool.wait_ge(*AC.by(f"rate{d}", i))
                        pool.wait_ge(*DV.by("kk", i))
                        pool.wait_ge(*DV.by(f"kdf{d}", i))
                        nc.gpsimd.tensor_tensor(rate[:, d, :], rate[:, d, :], kk, ALU.mult).then_inc(*PO.did(f"aa{d}"))
                        pool.wait_ge(*AC.by(f"inc{d}", i))
                        pool.wait_ge(*DV.by("shift2", i))
                        pool.wait_ge(*PE.before("y3", i))
                        nc.gpsimd.tensor_tensor(KR[:, d, 2:4, 1, :], e_in[:, d, 2:4, :],
                                                r_s.rearrange("p (n t) -> p n t", t=P), ALU.mult).then_inc(*PO.did(f"rr{d}"))
                    pool.wait_ge(*DV.by("kd1", i))
                    pool.wait_ge(*DV.before("yb", i))
                    nc.gpsimd.tensor_tensor(bonus[:, :], kd[:, 0, SEQ:TOK], kd[:, 1, SEQ:TOK], ALU.add).then_inc(*PO.did("kfb"))
                    pool.wait_ge(*PO.by("kfb", i))
                    nc.gpsimd.tensor_tensor(bonus[:, :], bonus[:, :], r_s, ALU.mult).then_inc(*PO.did("rkk"))
                    for q, (d, h) in enumerate(QS):
                        for part, src, lo in (("c", Gc, 0), ("x", Gx, 2)):
                            pool.wait_ge(*DV.by(f"g{q}" + ("c" if part == "c" else "z"), i))
                            pool.wait_ge(*PE.before("sa3", i))
                            u = src[:, q, :, 0, :]
                            v = XT[:, q, lo:lo + 2, :]
                            wide = lambda m: m.unsqueeze(1).broadcast_to([P, 2, P])
                            nc.gpsimd.tensor_tensor(v, u, wide(neg2[:, d, :]), ALU.mult).then_inc(*PO.did(f"m2{q}{part}"))
                            pool.wait_ge(*PO.by(f"m2{q}{part}", i))
                            nc.gpsimd.tensor_tensor(v, v, wide(ident[:, :]), ALU.add).then_inc(*PO.did(f"i2{q}{part}"))
                            nc.gpsimd.tensor_tensor(u, u, wide(ident[:, :]), ALU.add).then_inc(*PO.did(f"at{q}{part}"))
                PO.end()

            @block.scalar
            def _(act):
                AC.open(act)
                act.wait_ge(m_sem, MASKS[0])
                with act.Fori(0, PAIRS) as i:
                    for d in range(2):
                        act.wait_ge(*PE.by(f"u{d}", i))
                        act.wait_ge(*PE.before(f"cs{d}", i))
                        nc.scalar.activation(sg[:, d, :, :], ps[:, d, :].rearrange("p (n c) -> p n c", c=P),
                                             ACT.Sigmoid).then_inc(*AC.did(f"sg{d}"))
                    act.wait_ge(*DV.by("pp", i))
                    for d in range(2):
                        act.wait_ge(*PE.by(f"a{d}", i))
                        act.wait_ge(*DV.before(f"Ah{d}", i))
                        nc.scalar.activation(rate[:, d, :], ps[:, 2 + d, :], ACT.Sigmoid,
                                             bias=pp[:, PP.index("a0f") + d:PP.index("a0f") + d + 1]).then_inc(*AC.did(f"rate{d}"))
                    act.wait_ge(*PE.by("gate", i))
                    act.wait_ge(*DV.before("out", i))
                    nc.scalar.activation(gate[:, :], ps[:, 7, 0:SEQ], ACT.Copy).then_inc(*AC.did("gate"))
                    for n in range(3):
                        s0 = 1 if n == 2 else 0
                        act.wait_ge(*PE.by("kvr"[n], i))
                        nc.scalar.activation(pad[:, n, s0:2, 1:SEQ + 1],
                                             ps[:, 4 + n, s0 * SEQ:TOK].rearrange("p (s t) -> p s t", t=SEQ),
                                             ACT.Copy).then_inc(*AC.did(f"pad{n}"))
                        c = PP.index("om_" + "kvr"[n])
                        nc.scalar.activation(kvr[:, n, s0 * SEQ:TOK], ps[:, 4 + n, s0 * SEQ:TOK], ACT.Copy,
                                             scale=pp[:, c:c + 1]).then_inc(*AC.did(f"keep{n}"))
                    for d in range(2):
                        act.wait_ge(*PE.by(f"cs{d}", i))
                        c = ps[:, 2 * d:2 * d + 2, :].rearrange("p b (n e t) -> p (b n) e t", n=2, e=2)
                        nc.scalar.activation(KR[:, d, :, 0, :], c[:, :, 1, :], ACT.Exp, scale=DECAY).then_inc(*AC.did(f"exc{d}"))
                        nc.scalar.activation(e_in[:, d, :, :], c[:, :, 0, :], ACT.Exp, scale=DECAY).then_inc(*AC.did(f"inc{d}"))
                        nc.scalar.activation(e_ng[:, d, :, :], c[:, :, 0, :], ACT.Exp, scale=-DECAY).then_inc(*AC.did(f"neg{d}"))
                    act.wait_ge(*DV.by("shift0", i))
                    c = PP.index("k_k")
                    nc.scalar.activation(sq[:, :], k_s, ACT.Square, scale=pp[:, c:c + 1]).then_inc(*AC.did("sq"))
                    act.wait_ge(*PE.by("kss", i))
                    nc.scalar.activation(rn, ps[:, 4, :], ACT.Sqrt).then_inc(*AC.did("norm"))
                    for name, bank, dst in (("vt", 5, Vt[:, :, :]), ("kt0", 6, Kt[:, 0, :, :]), ("at0", 7, At[:, 0, :, :]),
                                            ("kt1", 4, Kt[:, 1, :, :]), ("at1", 5, At[:, 1, :, :])):
                        act.wait_ge(*PE.by(name, i))
                        nc.scalar.activation(dst, ps[:, bank, :].rearrange("p (n c) -> p n c", c=P),
                                             ACT.Copy).then_inc(*AC.did(name))
                    for q in range(4):
                        act.wait_ge(*PE.by(f"x1_{q}", i))
                        nc.scalar.activation(X[:, q, :, :], ps[:, 4 + q, :].rearrange("p (n c) -> p n c", c=P),
                                             ACT.Copy).then_inc(*AC.did(f"x1_{q}"))
                    for q in range(4):
                        act.wait_ge(*PE.by(f"T6_{q}", i))
                        nc.scalar.activation(XT[:, q, :, :], ps[:, q, :].rearrange("p (n c) -> p n c", c=P),
                                             ACT.Copy).then_inc(*AC.did(f"xt_{q}"))
                    for j in range(4):
                        act.wait_ge(*PE.by(f"rhs{j}", i))
                        nc.scalar.activation(rhs[:, :, :].rearrange("p (d h) v -> p h d v", h=2),
                                             ps[:, 4:6, 0:2 * HEAD].rearrange("p h (d v) -> p h d v", v=HEAD),
                                             ACT.Copy).then_inc(*AC.did(f"rhs{j}"))
                        act.wait_ge(*PE.by(f"sa{j}", i))
                        nc.scalar.activation(nsa[:, :, :], ps[:, 0, 0:4 * HEAD].rearrange("p (q v) -> p q v", v=HEAD),
                                             ACT.Copy, scale=-1.0).then_inc(*AC.did(f"sa{j}"))
                    act.wait_ge(*PE.by("y3", i))
                    nc.scalar.activation(y, ps[:, 6, 0:SEQ], ACT.Copy).then_inc(*AC.did("yf"))
                    act.wait_ge(*DV.by("yc", i))
                    nc.scalar.activation(ysq, yc, ACT.Square).then_inc(*AC.did("ysq"))
                    act.wait_ge(*PE.by("var", i))
                    nc.scalar.activation(rs, ps[:, 1, 0:SEQ], ACT.Sqrt, bias=ln_eps[:, 0:1]).then_inc(*AC.did("std"))
                AC.end()

            @block.vector
            def _(dve):
                DV.open(dve)
                dve.wait_ge(m_sem, MASKS[0])
                pcol = lambda name: pp[:, PP.index(name):PP.index(name) + 1]
                with dve.Fori(0, PAIRS) as i:
                    dve.wait_ge(*AC.before("std", i))
                    nc.vector.tensor_copy(pp[:, :], per_pair[:, ds(i, 1), :].rearrange("p a n -> p (a n)")).then_inc(*DV.did("pp"))
                    dve.wait_ge(*DV.by("pp", i))
                    for n in range(3):
                        s0 = 1 if n == 2 else 0
                        x = "kvr"[n]
                        dve.wait_ge(*AC.by(f"pad{n}", i))
                        nc.vector.tensor_tensor(near[:, n, s0 * SEQ:TOK].rearrange("p (s t) -> p s t", t=SEQ),
                                                pad[:, n, s0:2, 0:SEQ], pad[:, n, s0:2, 2:SEQ + 2],
                                                ALU.add).then_inc(*DV.did(f"near{n}"))
                        dve.wait_ge(*DV.by(f"near{n}", i))
                        dve.wait_ge(*AC.by(f"keep{n}", i))
                        nc.vector.scalar_tensor_tensor(kvr[:, n, s0 * SEQ:TOK], near[:, n, s0 * SEQ:TOK], pcol("hm_" + x),
                                                       kvr[:, n, s0 * SEQ:TOK], ALU.mult, ALU.add).then_inc(*DV.did(f"shift{n}"))
                    dve.wait_ge(*AC.by("norm", i))
                    nc.vector.tensor_scalar(rn, rn, 1e-12, None, ALU.max).then_inc(*DV.did("nmax"))
                    dve.wait_ge(*DV.by("nmax", i))
                    nc.vector.reciprocal(rn, rn).then_inc(*DV.did("nrec"))
                    dve.wait_ge(*DV.by("nrec", i))
                    nc.vector.scalar_tensor_tensor(kk, k_s, pcol("k_k"), rn, ALU.mult,
                                                   ALU.mult).then_inc(*DV.did("kk"))
                    dve.wait_ge(*DV.by("kk", i))
                    flat = lambda m: m.rearrange("p n t -> p (n t)")
                    for d in range(2):
                        dve.wait_ge(*AC.by(f"rate{d}", i))
                        dve.wait_ge(*PO.before("kfb", i))
                        nc.vector.tensor_scalar(kd[:, d, :], rate[:, d, :], pcol("k_a"), pcol("om_ka"), ALU.mult,
                                                ALU.add).then_inc(*DV.did(f"kdf{d}"))
                        dve.wait_ge(*DV.by(f"kdf{d}", i))
                        nc.vector.tensor_tensor(kd[:, d, :], kd[:, d, :], k_s, ALU.mult).then_inc(*DV.did(f"kd{d}"))
                        dve.wait_ge(*AC.by(f"neg{d}", i))
                        nc.vector.tensor_tensor(KR[:, d, :, 0, :], KR[:, d, :, 0, :],
                                                kk.rearrange("p (n t) -> p n t", t=P), ALU.mult).then_inc(*DV.did(f"KK{d}"))
                        dve.wait_ge(*DV.by(f"kd{d}", i))
                        nc.vector.tensor_tensor(flat(Kh[:, d, :, :]), kd[:, d, :], flat(e_ng[:, d, :, :]),
                                                ALU.mult).then_inc(*DV.did(f"Kh{d}"))
                        dve.wait_ge(*PO.by(f"aa{d}", i))
                        nc.vector.tensor_tensor(flat(Ah[:, d, :, :]), rate[:, d, :], flat(e_ng[:, d, :, :]),
                                                ALU.mult).then_inc(*DV.did(f"Ah{d}"))
                    nc.vector.tensor_tensor(em[:, 0, :], e_in[:, 0, 0:3, P - 1], e_in[:, 0, 1:4, P - 1],
                                            ALU.mult).then_inc(*DV.did("em0"))
                    nc.vector.tensor_tensor(em[:, 1, 0:3:2], e_in[:, 1, 1:4:2, 0], e_in[:, 1, 0:3:2, 0],
                                            ALU.mult).then_inc(*DV.did("em1"))
                    nc.vector.tensor_tensor(em[:, 1, 1:2], e_in[:, 1, 0, 0:1], e_in[:, 1, 3, 0:1],
                                            ALU.mult).then_inc(*DV.did("em2"))
                    dve.wait_ge(*PO.by("rkk", i))
                    nc.vector.tensor_scalar(bonus[:, :], bonus[:, :], pcol("r_k"), None, ALU.mult).then_inc(*DV.did("rk"))
                    dve.wait_ge(*PE.by("bonus", i))
                    nc.vector.tensor_tensor(bonus[:, :], ps[:, 6, SEQ:TOK], v_s[:, SEQ:TOK],
                                            ALU.mult).then_inc(*DV.did("bv"))
                    for q, (d, h) in enumerate(QS):
                        dve.wait_ge(*PE.by(f"g{q}c", i))
                        nc.vector.tensor_tensor(Gc[:, q, :, :, :].rearrange("p n e t -> p (n e) t"),
                                                ps[:, (3 * q) % 4, :].rearrange("p (n t) -> p n t", t=P),
                                                below[:, d, 0:1, :].broadcast_to([P, 4, P]), ALU.mult).then_inc(*DV.did(f"g{q}c"))
                        for n, x in ((0, "x"), (1, "z")):
                            dve.wait_ge(*PE.by(f"g{q}{x}", i))
                            nc.vector.tensor_tensor(Gx[:, q, n, :, :].rearrange("p (k e) t -> p k e t", e=2),
                                                    ps[:, (3 * q + 1 + n) % 4, :].rearrange("p (k e t) -> p k e t", k=2, e=2),
                                                    below[:, d, :, :].unsqueeze(1).broadcast_to([P, 2, 2, P]),
                                                    ALU.mult).then_inc(*DV.did(f"g{q}{x}"))
                    four = lambda m: m.unsqueeze(1).broadcast_to([P, NT, P])
                    for lev in LEVELS:
                        for q in range(4):
                            dve.wait_ge(*PE.by(f"E{lev}_{q}", i))
                            nc.vector.scalar_tensor_tensor(F[:, q, :, :], ps[:, q, :].rearrange("p (n t) -> p n t", t=P), -1.0,
                                                           four(ident2[:, :]), ALU.mult, ALU.add).then_inc(*DV.did(f"F{lev}_{q}"))
                        if lev == 6:
                            break
                        for m, dst, bank in (("X", X, 4), ("T", XT, 0)):
                            for q in range(4):
                                dve.wait_ge(*PE.by(f"{m}{lev}_{q}", i))
                                nc.vector.tensor_tensor(dst[:, q, :, :], ps[:, bank + q, :].rearrange("p (n t) -> p n t", t=P),
                                                        four(blocks[:, lev, :]), ALU.mult).then_inc(*DV.did(f"{m}{lev}_{q}"))
                    for j in range(3):
                        dve.wait_ge(*PE.by(f"s{j}", i))
                        for d in range(2):
                            nc.vector.tensor_scalar(S[:, d, :], ps[:, 7, d * HEAD:(d + 1) * HEAD], em[:, d, j:j + 1], None,
                                                    ALU.mult).then_inc(*DV.did(f"s{j}_{d}"))
                    dve.wait_ge(*AC.by("yf", i))
                    nc.vector.tensor_tensor(y, y, ps[:, 6, SEQ:TOK], ALU.add).then_inc(*DV.did("y"))
                    dve.wait_ge(*DV.by("y", i))
                    dve.wait_ge(*PE.by("mean", i))
                    nc.vector.tensor_tensor(yc, y, ps[:, 0, 0:SEQ], ALU.subtract).then_inc(*DV.did("yc"))
                    dve.wait_ge(*AC.by("std", i))
                    nc.vector.reciprocal(rs, rs).then_inc(*DV.did("rec"))
                    dve.wait_ge(*DV.by("rec", i))
                    nc.vector.tensor_tensor(yc, yc, rs, ALU.mult).then_inc(*DV.did("yn"))
                    dve.wait_ge(*DV.by("yn", i))
                    nc.vector.tensor_scalar(yc, yc, pcol("ln_w"), pcol("ln_b"), ALU.mult, ALU.add).then_inc(*DV.did("yl"))
                    dve.wait_ge(*DV.by("yl", i))
                    nc.vector.tensor_tensor(yc, yc, bonus[:, :], ALU.add).then_inc(*DV.did("yb"))
                    dve.wait_ge(*DV.by("yb", i))
                    nc.vector.tensor_tensor(yaT[:, ds(i, 1), :].rearrange("p a t -> p (a t)"), yc, gate[:, :],
                                            ALU.mult).then_inc(*DV.did("out"))
                DV.end()

            @block.tensor
            def _(pe):
                PE.open(pe)
                mm = nc.tensor.matmul
                with pe.Fori(0, PAIRS) as i:
                    pe.wait_ge(lw_sem, i * 64 + 64)
                    pe.wait_ge(*DV.before("yc", i))
                    pe.wait_ge(*AC.before("std", i))
                    for d in range(2):
                        for n in range(NT):
                            last = mm(ps[:, d, n * P:(n + 1) * P], tanh_w[:, d, n * P:(n + 1) * P], lw2[:, d, :],
                                      start=True, stop=True)
                        last.then_inc(*PE.did(f"u{d}"))
                    for d in range(2):
                        mm(ps[:, 2 + d, :], la2[:, d, :], low_a[:, d, :], start=True, stop=True).then_inc(*PE.did(f"a{d}"))
                    for k in range(2):
                        last = mm(ps[:, 7, 0:SEQ], lg2[:, k, :], gate_g[:, k, :], start=(k == 0), stop=(k == 1))
                    last.then_inc(*PE.did("gate"))
                    pe.wait_ge(w_sem, i * 48 + 48)
                    for n in range(3):
                        t0 = SEQ if n == 2 else 0
                        for k in range(KC):
                            last = mm(ps[:, 4 + n, t0:TOK], w[:, n, k, :], hT[:, k, t0:TOK], start=(k == 0), stop=(k == KC - 1))
                        last.then_inc(*PE.did("kvr"[n]))
                    for d in range(2):
                        pe.wait_ge(*AC.by("rate1", i))
                        for n in range(NT):
                            last = mm(ps[:, 2 * d + n // 2, (n % 2) * 2 * P:(n % 2 + 1) * 2 * P], sg[:, d, n, :],
                                      tri[:, d, :, :].rearrange("p e t -> p (e t)"), start=True, stop=True)
                        last.then_inc(*PE.did(f"cs{d}"))
                    pe.wait_ge(*AC.by("sq", i))
                    mm(ps[:, 4, :], head_ones[:, :], sq[:, :], start=True, stop=True).then_inc(*PE.did("kss"))

                    def turn(name, bank, src, after):
                        pe.wait_ge(*after)
                        for n in range(NT):
                            last = nc.tensor.transpose(ps[:, bank, n * P:(n + 1) * P], src[:, n * P:(n + 1) * P], ident[:, :])
                        last.then_inc(*PE.did(name))

                    flat = lambda m: m.rearrange("p n t -> p (n t)")
                    turn("vt", 5, v_s, DV.by("shift1", i))
                    pe.wait_ge(*DV.by("shift2", i))
                    turn("kt0", 6, flat(Kh[:, 0, :, :]), DV.by("Kh0", i))
                    pe.wait_ge(*AC.by("gate", i))
                    turn("at0", 7, flat(Ah[:, 0, :, :]), DV.by("Ah0", i))
                    pe.wait_ge(*AC.by("norm", i))
                    turn("kt1", 4, flat(Kh[:, 1, :, :]), DV.by("Kh1", i))
                    pe.wait_ge(*AC.by("vt", i))
                    turn("at1", 5, flat(Ah[:, 1, :, :]), DV.by("Ah1", i))
                    pe.wait_ge(*AC.by("neg1", i))
                    pe.wait_ge(*DV.by("rk", i))
                    pe.wait_ge(*AC.by("kt0", i))
                    mm(ps[:, 6, SEQ:TOK], head_ones[:, :], bonus[:, :], start=True, stop=True).then_inc(*PE.did("bonus"))
                    pe.wait_ge(*PO.by("rr1", i))
                    for q, (d, h) in enumerate(QS):
                        hs = head(h)
                        ring = lambda n: (3 * q + n) % 4

                        def bank_free(n):
                            c = 3 * q + n - 4
                            if c >= 0:
                                pe.wait_ge(*DV.by(f"g{c // 3}{'cxz'[c % 3]}", i))
                        bank_free(0)
                        for n in range(2):
                            for e, src in enumerate((Ah, Kh)):
                                c = (2 * n + e) * P
                                last = mm(ps[:, ring(0), c:c + P], src[hs, d, n, :], KR[hs, d, n, 0, :], start=True, stop=True)
                        last.then_inc(*PE.did(f"g{q}c"))
                        for n in range(2):
                            bank_free(1 + n)
                            for e, src in enumerate((Ah, Kh)):
                                last = mm(ps[:, ring(1 + n), e * 2 * P:(e + 1) * 2 * P], src[hs, d, 2 + n, :],
                                          KR[hs, d, 2 + n, :, :].rearrange("p e t -> p (e t)"), start=True, stop=True)
                            last.then_inc(*PE.did(f"g{q}{'xz'[n]}"))
                    for q in range(4):
                        pe.wait_ge(*PO.by(f"at{q}x", i))
                        pe.wait_ge(*AC.by("at1", i))
                        if q == 2:
                            pe.wait_ge(*DV.by("bv", i))
                        for n in range(NT):
                            last = nc.tensor.transpose(ps[:, 4 + q, n * P:(n + 1) * P], XT[:, q, n, :], ident[:, :])
                        last.then_inc(*PE.did(f"x1_{q}"))
                    for lev in LEVELS:
                        for q in range(4):
                            pe.wait_ge(*(AC.by(f"x1_{q}", i) if lev == 1 else DV.by(f"T{lev - 1}_{q}", i)))
                            if lev == 1:
                                pe.wait_ge(*DV.by("g3z", i))
                            for n in range(NT):
                                last = mm(ps[:, q, n * P:(n + 1) * P], A_T(q, n), X[:, q, n, :], start=True, stop=True)
                            last.then_inc(*PE.did(f"E{lev}_{q}"))
                        if lev < 6:
                            for q in range(4):
                                pe.wait_ge(*DV.by(f"F{lev}_{q}", i))
                                for n in range(NT):
                                    last = mm(ps[:, 4 + q, n * P:(n + 1) * P], XT[:, q, n, :], F[:, q, n, :], start=True, stop=True)
                                last.then_inc(*PE.did(f"X{lev}_{q}"))
                        for q in range(4):
                            pe.wait_ge(*DV.by(f"F{lev}_{q}", i))
                            for n in range(NT):
                                last = mm(ps[:, q, n * P:(n + 1) * P], F[:, q, n, :], XT[:, q, n, :], start=True, stop=True)
                            last.then_inc(*PE.did(f"T{lev}_{q}"))
                    pe.wait_ge(*AC.by("xt_3", i))
                    pe.wait_ge(*DV.by("X5_3", i))
                    for j in range(4):
                        if j:
                            pe.wait_ge(*DV.by(f"s{j - 1}_1", i))
                        for q, (d, h) in enumerate(QS):
                            n, hs = order[d][j], head(h)
                            if j:
                                mm(ps[:, 4 + h, d * HEAD:(d + 1) * HEAD], KR[hs, d, n, 0, :], S[hs, d, :], start=True, stop=False)
                            last = mm(ps[:, 4 + h, d * HEAD:(d + 1) * HEAD], B1(q, n), Vt[:, n, hs], start=(j == 0), stop=True)
                        last.then_inc(*PE.did(f"rhs{j}"))
                        pe.wait_ge(*AC.by(f"rhs{j}", i))
                        for q, (d, h) in enumerate(QS):
                            last = mm(ps[:, 0, q * HEAD:(q + 1) * HEAD], XT[:, q, order[d][j], :], rhs[:, q, :], start=True, stop=True)
                        last.then_inc(*PE.did(f"sa{j}"))
                        pe.wait_ge(*AC.by(f"sa{j}", i))
                        if j >= 2:
                            for q, (d, h) in enumerate(QS):
                                n, hs = order[d][j], head(h)
                                c = d * SEQ + (n - 2) * P
                                mm(ps[hs, 6, c:c + P], Vt[:, n, hs], Gx[:, q, n - 2, 3, :], start=True, stop=False)
                                mm(ps[hs, 6, c:c + P], S[hs, d, :], KR[hs, d, n, 1, :], start=False, stop=False)
                                last = mm(ps[hs, 6, c:c + P], nsa[:, q, :], Gx[:, q, n - 2, 1, :], start=False, stop=True)
                            last.then_inc(*PE.did(f"y{j}"))
                        if j < 3:
                            for q, (d, h) in enumerate(QS):
                                n, hs = order[d][j], head(h)
                                o = ps[hs, 7, d * HEAD:(d + 1) * HEAD]
                                mm(o, Kt[:, d, n, hs], Vt[:, n, hs], start=True, stop=False)
                                if j:
                                    mm(o, ident[hs, hs], S[hs, d, :], start=False, stop=False)
                                last = mm(o, At[:, d, n, hs], nsa[:, q, :], start=False, stop=True)
                            last.then_inc(*PE.did(f"s{j}"))
                    pe.wait_ge(*DV.by("y", i))
                    mm(ps[:, 0, 0:SEQ], head_mean[:, :], y, start=True, stop=True).then_inc(*PE.did("mean"))
                    pe.wait_ge(*AC.by("ysq", i))
                    mm(ps[:, 1, 0:SEQ], head_mean[:, :], ysq, start=True, stop=True).then_inc(*PE.did("var"))
                PE.end()


MASKS = [0]


def ssd(nc, sb, sem, ps, a, ident, ones, below, par, col, SKIP_D, hT, ybT):
    with ExitStack() as stage:
        def t(name, *shape):
            return sb(name, list(shape), ctx=stage)

        w_dt, by_head, by_head_done = t("w_dt", P, KC, 2 * SH), t("dt_by_head", 2 * SH, TOK), sem("dt_by_head_done")
        dt_bias, a_exp = t("dt_bias", P, 2 * SH), t("a_exp", P, 2 * SH)
        raw, lin, soft = t("dt_raw", P, NT, 2 * SH), t("dt_lin", P, NT, 2 * SH), t("dt_soft", P, NT, 2 * SH)
        heads = t("heads", P, 5, NT, 2 * SH)
        LOGA, CUM, STEP, END, WHOLE = range(5)
        per_group = t("per_group", P, GROUPS, 28)
        w_sem, rows_sem, proj, sums, dv, ac = (sem(x) for x in ("dt_w", "dt_rows", "dt_proj", "dt_sums", "dt_dve", "dt_act"))
        w_in = a["w_in"].rearrange("l (k p) n -> (l p) k n", p=P)
        in_columns = lambda m: m.rearrange("p (r w) -> p w r", r=GRID_R)
        with nc.Block() as block:

            @block.sync
            def _(sp):
                sp.dma_start(w_dt[:, :, :], w_in[:, :, DT0:GA0]).then_inc(w_sem, 16)
                sp.dma_start(dt_bias[:, :], a["ssm_dt_bias"].rearrange("l d h -> l (d h)").broadcast_to([P, 2 * SH])).then_inc(rows_sem, 16)
                sp.dma_start(a_exp[:, :], a["ssm_a_log"].rearrange("l d h -> l (d h)").broadcast_to([P, 2 * SH])).then_inc(rows_sem, 16)

            @block.tensor
            def _(pe):
                pe.wait_ge(w_sem, 16)
                for k in range(KC):
                    last = nc.tensor.matmul(ps[0:2 * SH, 4, :], w_dt[:, k, :], hT[:, k, :], start=(k == 0), stop=(k == KC - 1))
                last.then_inc(proj, 1)
                pe.wait_ge(by_head_done, 2)
                for n in range(NT):
                    last = nc.tensor.transpose(ps[:, 0, n * 2 * SH:(n + 1) * 2 * SH], by_head[:, n * P:(n + 1) * P],
                                               ident[0:2 * SH, 0:2 * SH])
                last.then_inc(proj, 1)
                pe.wait_ge(dv, 4 + 1)
                for d in range(2):
                    x = heads[:, LOGA, :, d * SH:(d + 1) * SH]
                    nc.tensor.matmul(ps[:, 1 + d, 0:P], below[:, 1 - d, 0, :], x, start=True, stop=True)
                    nc.tensor.matmul(ps[:, 1 + d, P:2 * P], below[:, d, 1, :], x, start=True, stop=True)
                    last = nc.tensor.matmul(ps[:, 1 + d, 2 * P:3 * P], ones[:, :], x, start=True, stop=True)
                last.then_inc(sums, 1)

            @block.scalar
            def _(act):
                act.wait_ge(proj, 1)
                nc.scalar.activation(by_head[:, 0:SEQ], ps[0:2 * SH, 4, 0:SEQ], ACT.Copy).then_inc(by_head_done, 1)
                nc.scalar.activation(by_head[:, SEQ:TOK].rearrange("p (w r) -> p w r", r=GRID_R),
                                     in_columns(ps[0:2 * SH, 4, SEQ:TOK]), ACT.Copy).then_inc(by_head_done, 1)
                act.wait_ge(rows_sem, 32)
                nc.scalar.activation(a_exp[:, :], a_exp[:, :], ACT.Exp).then_inc(ac, 1)
                act.wait_ge(dv, 1)
                nc.scalar.activation(soft[:, :, :], raw[:, :, :], ACT.Abs).then_inc(ac, 1)
                act.wait_ge(ac, 2)
                nc.scalar.activation(soft[:, :, :], soft[:, :, :], ACT.Exp, scale=-1.0).then_inc(ac, 1)
                act.wait_ge(ac, 3)
                nc.scalar.activation(soft[:, :, :], soft[:, :, :], ACT.Ln, bias=1.0).then_inc(ac, 1)
                act.wait_ge(sums, 1)
                for d in range(2):
                    for at, dst in ((0, END), (2 * P, WHOLE)):
                        nc.scalar.activation(heads[:, dst, :, d * SH:(d + 1) * SH],
                                             ps[:, 1 + d, at:at + P].rearrange("p (n h) -> p n h", h=SH), ACT.Exp).then_inc(ac, 1)

            @block.vector
            def _(dve):
                dve.wait_ge(proj, 2)
                dve.wait_ge(rows_sem, 32)
                nc.vector.tensor_tensor(raw[:, :, :], ps[:, 0, 0:NT * 2 * SH].rearrange("p (n h) -> p n h", h=2 * SH),
                                        dt_bias[:, :].unsqueeze(1).broadcast_to([P, NT, 2 * SH]), ALU.add).then_inc(dv, 1)
                dve.wait_ge(dv, 1)
                nc.vector.tensor_scalar(lin[:, :, :], raw[:, :, :], 0.0, None, ALU.max).then_inc(dv, 1)
                dve.wait_ge(dv, 2)
                dve.wait_ge(ac, 4)
                nc.vector.tensor_tensor(heads[:, STEP, :, :], lin[:, :, :], soft[:, :, :], ALU.add).then_inc(dv, 1)
                nc.vector.tensor_scalar(a_exp[:, :], a_exp[:, :], -1.0, None, ALU.mult).then_inc(dv, 1)
                dve.wait_ge(dv, 4)
                nc.vector.tensor_tensor(heads[:, LOGA, :, :], heads[:, STEP, :, :],
                                        a_exp[:, :].unsqueeze(1).broadcast_to([P, NT, 2 * SH]), ALU.mult).then_inc(dv, 1)
                cw, cb = col["conv_w"], col["conv_b"]
                XB = (D + 2 * GROUPS * STATE) // P
                for tap in range(CONV + 1):
                    c0 = cw + tap * XB if tap < CONV else cb
                    nc.vector.tensor_copy(per_group[:, :, 4 * tap:4 * tap + 2],
                                          par[:, c0:c0 + KC].rearrange("p (g e) -> p g e", e=2))
                    nc.vector.tensor_copy(per_group[:, :, 4 * tap + 2], par[:, c0 + KC:c0 + KC + GROUPS])
                    nc.vector.tensor_copy(per_group[:, :, 4 * tap + 3], par[:, c0 + KC + GROUPS:c0 + KC + 2 * GROUPS])
                for at, c0 in ((24, col["ssm_norm_w"]), (26, SKIP_D)):
                    nc.vector.tensor_copy(per_group[:, :, at:at + 2], par[:, c0:c0 + KC].rearrange("p (g e) -> p g e", e=2))
                dve.wait_ge(ac, 8)
                for d in range(2):
                    nc.vector.tensor_copy(heads[:, CUM, :, d * SH:(d + 1) * SH],
                                          ps[:, 1 + d, P:2 * P].rearrange("p (n h) -> p n h", h=SH))
                nc.vector.tensor_tensor(heads[:, END, :, :], heads[:, END, :, :], heads[:, STEP, :, :], ALU.mult).then_inc(dv, 1)

        w = t("w_group", P, 4, KC, P)
        wz = t("w_z", P, KC, GW)
        pg, hd = t("pg", P, 28), t("hd", P, 5, NT, 2, 4)
        pad = t("xbc_pad", P, 4, 2, SEQ + 4)
        cv = t("xbc_conv", P, 4, TOK)
        xt, bt = t("xt", P, NT, GW), t("bt", P, NT, STATE)
        cbm = t("cbm", P, 2, 2, P)
        seg = t("seg", P, 2, 4, 2, P)
        ecs = t("ecs", P, 2, 2, 2, P)
        xw = t("xw", P, 2, 3, 4, HEAD)
        H = t("H", P, 2, 3, 4, HEAD)
        sz = t("sz", P, 2, SEQ)
        y, ysq, inv = t("ys", P, 2, SEQ), t("ysq", P, 2, SEQ), t("inv", P, SEQ)
        eps_col = t("eps_col", P, 1)
        order = [(0, 1, 2, 3), (1, 0, 3, 2)]
        NS = [("%d_%d" % (j, d), j, d) for j in range(3) for d in range(2)]
        PE = Steps(sem("ss_pe"), "x0 x1 B C z tx0 tx1 tB cb cr0 cr1 cr2 cr3 ec0 ec1 " + " ".join("st" + s for s, _, _ in NS)
                   + " yd off0 off1 nrm", True)
        AC = Steps(sem("ss_act"), "p0 p1 p2 p3 z s0 s1 s2 s3 tx0 tx1 tB e0 e1 e2 e3 ec0 ec1 sq std", True)
        DV = Steps(sem("ss_dve"), "pg hd " + " ".join(f"c{n}_{k}" for n in range(4) for k in range(CONV))
                   + " cbm seg0 seg1 seg2 seg3 w0 w1 w2 w3 " + " ".join(
                       (f"hm{s} " if j else "") + f"h{s}" for s, j, d in NS)
                   + " y off0 off1 y0 y1 gate rec out", True)
        PO = Steps(sem("ss_pool"), "xw w", True)
        loads, zloads, consts = sem("ss_w"), sem("ss_wz"), sem("ss_consts")
        with nc.Block() as block:

            @block.sync
            def _(sp):
                with sp.Fori(0, GROUPS) as i:
                    sp.wait_ge(*PE.before("C", i))
                    sp.dma_start(w[:, 0, :, :], w_in[:, :, ds(i * GW + X0, P)]).then_inc(loads, 16)
                    sp.dma_start(w[:, 1, :, :], w_in[:, :, ds(i * GW + X0 + P, P)]).then_inc(loads, 16)
                    sp.dma_start(w[:, 2, :, :], w_in[:, :, ds(i * STATE + B0, STATE)]).then_inc(loads, 16)
                    sp.dma_start(w[:, 3, :, :], w_in[:, :, ds(i * STATE + C0, STATE)]).then_inc(loads, 16)
                    sp.wait_ge(*PE.before("z", i))
                    sp.dma_start(wz[:, :, :], w_in[:, :, ds(i * GW + Z0, GW)]).then_inc(zloads, 16)

            @block.gpsimd
            def _(pool):
                PO.open(pool)
                nc.gpsimd.memset(pad[:, :, :, :], 0.0).then_inc(consts, 1)
                nc.gpsimd.memset(eps_col[:, :], EPS).then_inc(consts, 1)
                with pool.Fori(0, GROUPS) as i:
                    pool.wait_ge(*AC.by("tx1", i))
                    pool.wait_ge(*DV.by("hd", i))
                    pool.wait_ge(*PE.before("off1", i))
                    for d in range(2):
                        for j in range(3):
                            n = order[d][j]
                            last = nc.gpsimd.tensor_tensor(xw[:, d, j, :, :], xt[:, n, :].rearrange("p (e c) -> p e c", c=HEAD),
                                                           hd[:, END, n, d, :].unsqueeze(2).broadcast_to([P, 4, HEAD]), ALU.mult)
                    last.then_inc(*PO.did("xw"))
                    pool.wait_ge(*DV.by("w3", i))
                    f = lambda m: m.rearrange("p e c t -> p (e c t)")
                    nc.gpsimd.tensor_tensor(f(seg[:, 0, :, :, :]), f(seg[:, 0, :, :, :]), f(seg[:, 1, :, :, :]),
                                            ALU.add).then_inc(*PO.did("w"))
                PO.end()

            @block.scalar
            def _(act):
                AC.open(act)
                act.wait_ge(consts, 2)
                with act.Fori(0, GROUPS) as i:
                    for n in range(4):
                        act.wait_ge(*PE.by(("x0", "x1", "B", "C")[n], i))
                        act.wait_ge(*DV.before(f"c{n}_4", i))
                        if n < 3:
                            nc.scalar.activation(pad[:, n, 0, 2:SEQ + 2], ps[:, n, 0:SEQ], ACT.Copy)
                        nc.scalar.activation(pad[:, n, 1, 2:SEQ + 2].rearrange("p (w r) -> p w r", r=GRID_R),
                                             in_columns(ps[:, n, SEQ:TOK]), ACT.Copy).then_inc(*AC.did(f"p{n}"))
                    act.wait_ge(*PE.by("z", i))
                    act.wait_ge(*DV.before("out", i))
                    nc.scalar.activation(sz[:, :, :], ps[:, 4, :].rearrange("p (e t) -> p e t", e=2), ACT.Silu).then_inc(*AC.did("z"))
                    for n in range(4):
                        t0 = SEQ if n == 3 else 0
                        act.wait_ge(*DV.by(f"c{n}_4", i))
                        nc.scalar.activation(cv[:, n, t0:TOK], cv[:, n, t0:TOK], ACT.Silu).then_inc(*AC.did(f"s{n}"))
                    for e in range(2):
                        act.wait_ge(*PE.by(f"tx{e}", i))
                        act.wait_ge(*PO.before("xw", i))
                        nc.scalar.activation(xt[:, :, e * P:(e + 1) * P], ps[:, 5 + e, :].rearrange("p (n c) -> p n c", c=P),
                                             ACT.Copy).then_inc(*AC.did(f"tx{e}"))
                    act.wait_ge(*PE.by("tB", i))
                    nc.scalar.activation(bt[:, :, :], ps[:, 7, :].rearrange("p (n c) -> p n c", c=P), ACT.Copy).then_inc(*AC.did("tB"))
                    for b in range(4):
                        d, e = divmod(b, 2)
                        act.wait_ge(*DV.by(f"seg{b}", i))
                        nc.scalar.activation(seg[:, d, 2 * e:2 * e + 2, :, :], seg[:, d, 2 * e:2 * e + 2, :, :],
                                             ACT.Exp).then_inc(*AC.did(f"e{b}"))
                    for d in range(2):
                        act.wait_ge(*PE.by(f"ec{d}", i))
                        act.wait_ge(*DV.before(f"off{d}", i))
                        nc.scalar.activation(ecs[:, d, :, :, :], ps[:, 5 + d, :].rearrange("p (e c t) -> p e c t", e=2, c=2),
                                             ACT.Exp).then_inc(*AC.did(f"ec{d}"))
                    act.wait_ge(*DV.by("gate", i))
                    nc.scalar.activation(ysq[:, :, :], sz[:, :, :], ACT.Square).then_inc(*AC.did("sq"))
                    act.wait_ge(*PE.by("nrm", i))
                    nc.scalar.activation(inv[:, :], ps[:, 4, 0:SEQ], ACT.Sqrt, scale=1.0 / GW, bias=eps_col[:, 0:1]).then_inc(*AC.did("std"))
                AC.end()

            @block.vector
            def _(dve):
                DV.open(dve)
                with dve.Fori(0, GROUPS) as i:
                    dve.wait_ge(*DV.before("out", i))
                    nc.vector.tensor_copy(pg[:, :], per_group[:, ds(i, 1), :].rearrange("p a n -> p (a n)")).then_inc(*DV.did("pg"))
                    dve.wait_ge(*PO.before("w", i))
                    dve.wait_ge(*PE.before("off1", i))
                    nc.vector.tensor_copy(hd[:, :, :, :, :].rearrange("p a n d e -> p (a n d) e"),
                                          heads[:, :, :, :].rearrange("p a n (d h) -> p (a n d) h", d=2)[:, :, ds(i * 4, 4)]
                                          ).then_inc(*DV.did("hd"))
                    dve.wait_ge(*DV.by("pg", i))
                    for n in range(4):
                        s0 = 1 if n == 3 else 0
                        dve.wait_ge(*AC.by(f"p{n}", i))
                        o = cv[:, n, s0 * SEQ:TOK].rearrange("p (s t) -> p s t", t=SEQ)
                        nc.vector.tensor_scalar(o, pad[:, n, s0:2, 0:SEQ], pg[:, n:n + 1], pg[:, 20 + n:21 + n], ALU.mult,
                                                ALU.add).then_inc(*DV.did(f"c{n}_0"))
                        for k in range(1, CONV):
                            dve.wait_ge(*DV.by(f"c{n}_{k - 1}", i))
                            nc.vector.scalar_tensor_tensor(o, pad[:, n, s0:2, k:k + SEQ], pg[:, 4 * k + n:4 * k + n + 1], o,
                                                           ALU.mult, ALU.add).then_inc(*DV.did(f"c{n}_{k}"))
                    dve.wait_ge(*PE.by("cb", i))
                    for d in range(2):
                        last = nc.vector.tensor_tensor(cbm[:, d, :, :], ps[:, 0, 0:SEQ].rearrange("p (c t) -> p c t", c=2),
                                                       below[:, d, 1:2, :].broadcast_to([P, 2, P]), ALU.mult)
                    last.then_inc(*DV.did("cbm"))
                    for b in range(4):
                        d = b // 2
                        dve.wait_ge(*PE.by(f"cr{b}", i))
                        dve.wait_ge(*PE.before("yd", i))
                        for e in range(2):
                            for c in range(2):
                                last = nc.vector.tensor_scalar(seg[:, d, 2 * (b % 2) + e, c, :], ps[:, 1 + b, (2 * e + c) * P:(2 * e + c + 1) * P],
                                                               hd[:, CUM, 2 + c, d, 2 * (b % 2) + e:2 * (b % 2) + e + 1], 0.0,
                                                               ALU.subtract, ALU.min)
                        last.then_inc(*DV.did(f"seg{b}"))
                    dve.wait_ge(*DV.by("cbm", i))
                    for b in range(4):
                        d = b // 2
                        dve.wait_ge(*AC.by(f"e{b}", i))
                        for e in range(2 * (b % 2), 2 * (b % 2) + 2):
                            for c in range(2):
                                last = nc.vector.scalar_tensor_tensor(seg[:, d, e, c, :], seg[:, d, e, c, :],
                                                                      hd[:, STEP, 2 + c, d, e:e + 1], cbm[:, d, c, :],
                                                                      ALU.mult, ALU.mult)
                        last.then_inc(*DV.did(f"w{b}"))
                    for s, j, d in NS:
                        n = order[d][j]
                        st = ps[:, (7, 0)[d], 0:GW].rearrange("p (e c) -> p e c", c=HEAD)
                        dve.wait_ge(*PE.by("st" + s, i))
                        if j:
                            dve.wait_ge(*DV.by(f"h{j - 1}_{d}", i))
                            nc.vector.tensor_tensor(H[:, d, j, :, :], H[:, d, j - 1, :, :],
                                                    hd[:, WHOLE, n, d, :].unsqueeze(2).broadcast_to([P, 4, HEAD]),
                                                    ALU.mult).then_inc(*DV.did("hm" + s))
                            dve.wait_ge(*DV.by("hm" + s, i))
                            nc.vector.tensor_tensor(H[:, d, j, :, :], H[:, d, j, :, :], st, ALU.add).then_inc(*DV.did("h" + s))
                        else:
                            nc.vector.tensor_copy(H[:, d, 0, :, :], st).then_inc(*DV.did("h" + s))
                    dve.wait_ge(*PE.by("yd", i))
                    dve.wait_ge(*AC.by("s1", i))
                    for e in range(2):
                        last = nc.vector.scalar_tensor_tensor(y[:, e, :], cv[:, e, SEQ:TOK], pg[:, 26 + e:27 + e],
                                                              ps[:, 3, e * SEQ:(e + 1) * SEQ], ALU.mult, ALU.add)
                    last.then_inc(*DV.did("y"))
                    for d in range(2):
                        dve.wait_ge(*PE.by(f"off{d}", i))
                        dve.wait_ge(*AC.by(f"ec{d}", i))
                        f = lambda m: m.rearrange("p e c t -> p (e c t)")
                        nc.vector.tensor_tensor(f(ecs[:, d, :, :, :]), f(ecs[:, d, :, :, :]), ps[:, 1 + d, :], ALU.mult).then_inc(*DV.did(f"off{d}"))
                    for d in range(2):
                        dve.wait_ge(*(DV.by("off1", i) if d == 0 else DV.by("y0", i)))
                        nc.vector.tensor_tensor(y[:, :, :], y[:, :, :], ecs[:, d, :, :, :].rearrange("p e c t -> p e (c t)"),
                                                ALU.add).then_inc(*DV.did(f"y{d}"))
                    dve.wait_ge(*DV.by("y1", i))
                    dve.wait_ge(*AC.by("z", i))
                    for e in range(2):
                        last = nc.vector.tensor_tensor(sz[:, e, :].rearrange("p (r w) -> p r w", r=GRID_R),
                                                       y[:, e, :].rearrange("p (w r) -> p r w", r=GRID_R),
                                                       sz[:, e, :].rearrange("p (r w) -> p r w", r=GRID_R), ALU.mult)
                    last.then_inc(*DV.did("gate"))
                    dve.wait_ge(*AC.by("std", i))
                    nc.vector.reciprocal(inv[:, :], inv[:, :]).then_inc(*DV.did("rec"))
                    dve.wait_ge(*DV.by("rec", i))
                    for e in range(2):
                        last = nc.vector.scalar_tensor_tensor(ybT[:, ds(i * 2 + e, 1), :].rearrange("p a t -> p (a t)"), sz[:, e, :],
                                                              pg[:, 24 + e:25 + e], inv[:, :], ALU.mult, ALU.mult)
                    last.then_inc(*DV.did("out"))
                DV.end()

            @block.tensor
            def _(pe):
                PE.open(pe)
                mm = nc.tensor.matmul
                with pe.Fori(0, GROUPS) as i:
                    pe.wait_ge(loads, i * 64 + 64)
                    pe.wait_ge(*DV.before("off1", i))
                    pe.wait_ge(*AC.before("std", i))
                    for n in range(4):
                        t0 = SEQ if n == 3 else 0
                        for k in range(KC):
                            last = mm(ps[:, n, t0:TOK], w[:, n, k, :], hT[:, k, t0:TOK], start=(k == 0), stop=(k == KC - 1))
                        last.then_inc(*PE.did(("x0", "x1", "B", "C")[n]))
                    pe.wait_ge(zloads, i * 16 + 16)
                    for e in range(2):
                        for k in range(KC):
                            last = mm(ps[:, 4, e * SEQ:(e + 1) * SEQ], wz[:, k, e * P:(e + 1) * P], hT[:, k, SEQ:TOK],
                                      start=(k == 0), stop=(k == KC - 1))
                    last.then_inc(*PE.did("z"))
                    for m, name in enumerate(("tx0", "tx1", "tB")):
                        pe.wait_ge(*AC.by(f"s{m}", i))
                        for n in range(NT):
                            last = nc.tensor.transpose(ps[:, 5 + m, n * P:(n + 1) * P], cv[:, m, n * P:(n + 1) * P], ident[:, :])
                        last.then_inc(*PE.did(name))
                    pe.wait_ge(*AC.by("s3", i))
                    for c in range(2):
                        x = slice(SEQ + c * P, SEQ + (c + 1) * P)
                        last = mm(ps[:, 0, c * P:(c + 1) * P], cv[:, 2, x], cv[:, 3, x], start=True, stop=True)
                    last.then_inc(*PE.did("cb"))
                    for b in range(4):
                        d = b // 2
                        for e in range(2):
                            for c in range(2):
                                at = (2 * e + c) * P
                                last = mm(ps[:, 1 + b, at:at + P],
                                          hd[:, LOGA, 2 + c, d, 2 * (b % 2) + e:2 * (b % 2) + e + 1].broadcast_to([P, P]),
                                          below[:, d, 1, :], start=True, stop=True)
                        last.then_inc(*PE.did(f"cr{b}"))
                    for d in range(2):
                        pe.wait_ge(*AC.by(f"tx{d}", i))
                        for e in range(2):
                            for c in range(2):
                                at = (2 * e + c) * P
                                for h in range(2):
                                    last = mm(ps[h * HEAD:(h + 1) * HEAD, 5 + d, at:at + P],
                                              hd[:, LOGA, 2 + c, d, 2 * e + h:2 * e + h + 1].broadcast_to([P, HEAD]),
                                              below[:, d, 1, :], start=True, stop=True)
                        last.then_inc(*PE.did(f"ec{d}"))
                    pe.wait_ge(*PO.by("xw", i))
                    pe.wait_ge(*AC.by("tB", i))
                    pe.wait_ge(*DV.by("cbm", i))
                    for s, j, d in NS:
                        if j:
                            pe.wait_ge(*DV.by(f"h{j - 1}_{d}", i))
                        mm(ps[:, (7, 0)[d], 0:GW], bt[:, order[d][j], :],
                           xw[:, d, j, :, :].rearrange("p e c -> p (e c)"), start=True, stop=True).then_inc(*PE.did("st" + s))
                    pe.wait_ge(*PO.by("w", i))
                    for e in range(4):
                        for c in range(2):
                            r0 = (e % 2) * HEAD
                            at = (e // 2) * SEQ + c * P
                            last = mm(ps[r0:r0 + HEAD, 3, at:at + P], xt[:, 2 + c, e * HEAD:(e + 1) * HEAD], seg[:, 0, e, c, :],
                                      start=True, stop=True)
                    last.then_inc(*PE.did("yd"))
                    for d in range(2):
                        pe.wait_ge(*DV.by(f"h2_{d}", i))
                        for e in range(2):
                            for c in range(2):
                                j = 1 + (c if d == 0 else 1 - c)
                                last = mm(ps[:, 1 + d, e * SEQ + c * P:e * SEQ + (c + 1) * P],
                                          H[:, d, j, 2 * e:2 * e + 2, :].rearrange("p e c -> p (e c)"),
                                          cv[:, 3, SEQ + c * P:SEQ + (c + 1) * P], start=True, stop=True)
                        last.then_inc(*PE.did(f"off{d}"))
                    pe.wait_ge(*AC.by("sq", i))
                    for e in range(2):
                        last = mm(ps[:, 4, 0:SEQ], ones[:, :], ysq[:, e, :], start=(e == 0), stop=(e == 1))
                    last.then_inc(*PE.did("nrm"))
                PE.end()


def merge(nc, sb, sem, ps, a, ident, ones, par, col, modT, hT, yaT, ybT, xT):
    with ExitStack() as stage:
        def t(name, *shape):
            return sb(name, list(shape), ctx=stage)

        w = t("w_merge", P, 2, KC, 512)
        mT = t("mT", P, KC, SEQ)
        sga, sgb = t("sga", P, 4, SEQ), t("sgb", P, 4, SEQ)
        x_rows = t("x_rows", P, 2, D)
        g1, gain2, rstd, eps_col = t("g1", P, KC), t("gain2", P, KC), t("rstd", P, SEQ), t("m_eps", P, 1)
        mixT, h2T, sqT = ybT, yaT, mT
        w_in = [sem("mg_w0"), sem("mg_w1")]
        x_in, consts, out_mm, out_cp = sem("mg_x"), sem("mg_consts"), sem("mg_out_mm"), sem("mg_out_cp")
        PE = Steps(sem("mg_pe"), "ga gb A B", True)
        AC = Steps(sem("mg_act"), "ga gb", True)
        DV = Steps(sem("mg_dve"), "A B m", True)
        passed = sem("mg_passed")
        dv2, pe2, ac2 = sem("mg_dve2"), sem("mg_pe2"), sem("mg_act2")
        cols = lambda name: a[name].rearrange("l (k p) n -> (l p) k n", p=P)
        win, wa, wb, wo = cols("w_in"), cols("w_branch_a"), cols("w_branch_b"), cols("w_out")
        BL = 4
        half = lambda b: ps[:, 2 * b:2 * b + 2, :].rearrange("p b (c t) -> p (b c) t", t=SEQ)
        with nc.Block() as block:

            @block.sync
            def _(sp):
                sp.dma_start(x_rows[:, :, :], a["x"].rearrange("l (n p) d -> (l p) n d", p=P)).then_inc(x_in, 16)
                with sp.Fori(0, BL) as i:
                    at, at_a, at_b = (sp.snap(i * 512 + c) for c in (0, GA0, GA0 + D))
                    wait_alone(sp, passed, *PE.before("A", i))
                    sp.dma_start(w[:, 0, :, :], win[:, :, ds(at_a, 512)]).then_inc(w_in[0], 16)
                    wait_alone(sp, passed, *PE.before("B", i))
                    sp.dma_start(w[:, 1, :, :], win[:, :, ds(at_b, 512)]).then_inc(w_in[1], 16)
                    wait_alone(sp, passed, *PE.by("ga", i))
                    sp.dma_start(w[:, 0, :, :], wa[:, :, ds(at, 512)]).then_inc(w_in[0], 16)
                    wait_alone(sp, passed, *PE.by("gb", i))
                    sp.dma_start(w[:, 1, :, :], wb[:, :, ds(at, 512)]).then_inc(w_in[1], 16)
                for n in range(BL):
                    sp.wait_ge(*(PE.by("AB"[n], BL - 1) if n < 2 else (out_mm, n - 1)))
                    sp.dma_start(w[:, n % 2, :, :], wo[:, :, n * 512:(n + 1) * 512]).then_inc(w_in[n % 2], 16)

            @block.tensor
            def _(pe):
                PE.open(pe)

                def product(slot, rhs, bank):
                    for c in range(4):
                        for k in range(KC):
                            last = nc.tensor.matmul(ps[:, bank + c // 2, (c % 2) * SEQ:(c % 2 + 1) * SEQ],
                                                    w[:, slot, k, c * P:(c + 1) * P], rhs[:, k, :], start=(k == 0), stop=(k == KC - 1))
                    return last

                with pe.Fori(0, BL) as i:
                    pe.wait_ge(w_in[0], i * 32 + 16)
                    pe.wait_ge(*AC.before("ga", i))
                    product(0, hT[:, :, SEQ:TOK], 0).then_inc(*PE.did("ga"))
                    pe.wait_ge(w_in[1], i * 32 + 16)
                    pe.wait_ge(*AC.before("gb", i))
                    product(1, hT[:, :, SEQ:TOK], 2).then_inc(*PE.did("gb"))
                    pe.wait_ge(w_in[0], i * 32 + 32)
                    pe.wait_ge(*DV.before("A", i))
                    product(0, yaT, 4).then_inc(*PE.did("A"))
                    pe.wait_ge(w_in[1], i * 32 + 32)
                    pe.wait_ge(*DV.before("B", i))
                    product(1, ybT, 6).then_inc(*PE.did("B"))
                PE.end()
                pe.wait_ge(*DV.by("m", BL - 1))
                for n in range(BL):
                    pe.wait_ge(w_in[n % 2], 32 * BL + 16 * (n // 2 + 1))
                    if n >= 2:
                        pe.wait_ge(out_cp, n - 1)
                    product(n % 2, mT, 2 * (n % 2)).then_inc(out_mm, 1)
                pe.wait_ge(x_in, 16)
                for j in range(KC):
                    if j == 8:
                        pe.wait_ge(dv2, 2 + 1)
                    for n in range(2):
                        last = nc.tensor.transpose(ps[:, 4 + (j % 8) // 2, (j % 2) * SEQ + n * P:(j % 2) * SEQ + (n + 1) * P],
                                                   x_rows[:, n, j * P:(j + 1) * P], ident[:, :])
                    if j % 8 == 7:
                        last.then_inc(pe2, 1)
                for r in range(2):
                    pe.wait_ge(ac2, 1 + 2 * r)
                    for k in range(KC):
                        last = nc.tensor.matmul(ps[:, r, 0:SEQ], ones[:, :], sqT[:, k, :], start=(k == 0), stop=(k == KC - 1))
                    last.then_inc(pe2, 1)

            @block.gpsimd
            def _(pool):
                nc.gpsimd.memset(eps_col[:, :], EPS).then_inc(consts, 1)

            @block.scalar
            def _(act):
                AC.open(act)
                with act.Fori(0, BL) as i:
                    act.wait_ge(*PE.by("ga", i))
                    act.wait_ge(*DV.before("m", i))
                    nc.scalar.activation(sga[:, :, :], half(0), ACT.Sigmoid).then_inc(*AC.did("ga"))
                    act.wait_ge(*PE.by("gb", i))
                    nc.scalar.activation(sgb[:, :, :], half(1), ACT.Sigmoid).then_inc(*AC.did("gb"))
                AC.end()
                for n in range(BL):
                    act.wait_ge(out_mm, n + 1)
                    nc.scalar.activation(mixT[:, 4 * n:4 * n + 4, :], half(n % 2), ACT.Copy).then_inc(out_cp, 1)
                act.wait_ge(out_cp, BL)
                act.wait_ge(consts, 1)
                for r, src in enumerate((mixT, xT)):
                    if r:
                        act.wait_ge(dv2, 8)
                    nc.scalar.activation(sqT[:, :, :], src[:, :, :], ACT.Square).then_inc(ac2, 1)
                    act.wait_ge(pe2, 3 + r)
                    nc.scalar.activation(rstd[:, :], ps[:, r, 0:SEQ], ACT.Sqrt, scale=1.0 / D, bias=eps_col[:, 0:1]).then_inc(ac2, 1)

            @block.vector
            def _(dve):
                DV.open(dve)
                with dve.Fori(0, BL) as i:
                    dve.wait_ge(*AC.by("ga", i))
                    dve.wait_ge(*PE.by("A", i))
                    nc.vector.tensor_tensor(sga[:, :, :], sga[:, :, :], half(2), ALU.mult).then_inc(*DV.did("A"))
                    dve.wait_ge(*AC.by("gb", i))
                    dve.wait_ge(*PE.by("B", i))
                    nc.vector.tensor_tensor(sgb[:, :, :], sgb[:, :, :], half(3), ALU.mult).then_inc(*DV.did("B"))
                    dve.wait_ge(*DV.by("B", i))
                    nc.vector.tensor_tensor(mT[:, ds(i * 4, 4), :], sga[:, :, :], sgb[:, :, :], ALU.add).then_inc(*DV.did("m"))
                DV.end()
                row = lambda m: m.unsqueeze(1).broadcast_to([P, 8, SEQ])
                nc.vector.tensor_tensor(g1[:, :], modT[:, 2 * KC:3 * KC, 0], par[:, col["norm_post1"]:col["norm_post1"] + KC],
                                        ALU.mult).then_inc(dv2, 1)
                nc.vector.scalar_tensor_tensor(gain2[:, :], modT[:, 4 * KC:5 * KC, 0], 1.0,
                                               par[:, col["norm_pre2"]:col["norm_pre2"] + KC], ALU.add, ALU.mult).then_inc(dv2, 1)
                for h in range(2):
                    dve.wait_ge(pe2, h + 1)
                    nc.vector.tensor_copy(xT[:, 8 * h:8 * h + 8, :], ps[:, 4:8, :].rearrange("p b (c t) -> p (b c) t", t=SEQ)).then_inc(dv2, 1)
                dve.wait_ge(ac2, 2)
                nc.vector.reciprocal(rstd[:, :], rstd[:, :]).then_inc(dv2, 1)
                dve.wait_ge(dv2, 5)
                for j in range(KC):
                    last = nc.vector.scalar_tensor_tensor(mixT[:, j, :], mixT[:, j, :], g1[:, j:j + 1], rstd[:, :], ALU.mult, ALU.mult)
                last.then_inc(dv2, 1)
                dve.wait_ge(dv2, 6)
                for h in range(2):
                    s = slice(8 * h, 8 * h + 8)
                    nc.vector.tensor_tensor(xT[:, s, :], xT[:, s, :], mixT[:, s, :], ALU.add).then_inc(dv2, 1)
                dve.wait_ge(ac2, 4)
                nc.vector.reciprocal(rstd[:, :], rstd[:, :]).then_inc(dv2, 1)
                dve.wait_ge(dv2, 9)
                for j in range(KC):
                    last = nc.vector.scalar_tensor_tensor(h2T[:, j, :], xT[:, j, :], gain2[:, j:j + 1], rstd[:, :], ALU.mult, ALU.mult)
                last.then_inc(dv2, 1)
                dve.wait_ge(dv2, 10)
                for j in range(KC):
                    last = nc.vector.tensor_scalar(h2T[:, j, :], h2T[:, j, :], modT[:, 3 * KC + j, 0:1], None, ALU.add)
                last.then_inc(dv2, 1)


def peer(nc, sb, sem, ps, a, out, ident, ones, par, col, modT, hT, h2T, qT, xT):
    with ExitStack() as outer:
        idx = sb("idx", [P, 2 * SLOTS], U32, ctx=outer)
        gates = sb("gates", [P, 2 * SLOTS], ctx=outer)
        rows = hT[:, :, :].rearrange("p k t -> p (k t)").rearrange("p (a n d) -> p a n d", a=2, n=2)
        h2_rows, x_rows = rows[:, 0, :, :], rows[:, 1, :, :]
        g2_rows = sb("g2_rows", [P, D], ctx=outer)
        route(nc, sb, sem, ps, a, ident, ones, par, col, modT, h2T, xT, qT, idx, gates, h2_rows, x_rows, g2_rows)
        experts(nc, sb, sem, ps, a, out, ident, idx, gates, h2_rows, x_rows, g2_rows)


def route(nc, sb, sem, ps, a, ident, ones, par, col, modT, h2T, xT, qT, idx, gates, h2_rows, x_rows, g2_rows):
    with ExitStack() as stage:
        def t(name, shape, dt=F32):
            return sb(name, list(shape), dt, ctx=stage)

        w = t("w_q", [P, 2, KC, 512])
        keys, keysT = t("keys", [P, KC, PK]), t("keysT", [P, KC, PK])
        g2, diag = t("g2", [P, KC]), t("diag_g2", [P, 4, P])
        sc, sc2 = t("sc", [P, 2, 2, PK]), t("sc2", [P, 2, 2, PK])
        top_s, top_i, top_f = t("top_s", [P, 2, 2, TOPK]), t("top_i", [P, 2, 2, TOPK], U32), t("top_f", [P, 2, 2, TOPK])
        cand, cand2 = t("cand", [P, 2, TOPK, TOPK]), t("cand2", [P, 2, TOPK, TOPK])
        best_s, best_j = t("best_s", [P, 2, TOPK]), t("best_j", [P, 2, TOPK], U32)
        part_i, part_f = t("part_i", [P, 2, 2, TOPK], U32), t("part_f", [P, 2, 2, TOPK])
        iota_i, iota_f = t("iota_i", [P, TOPK], U32), t("iota_f", [P, TOPK])
        hot = t("hot", [P, 2, TOPK, TOPK])
        ex, ef = t("ex", [P, 2, 2, TOPK]), t("ef", [P, 2, TOPK])
        soft, total = t("soft", [P, 2, TOPK]), t("total", [P, 2])
        w_in = [sem("q_w0"), sem("q_w1")]
        k_in, q_mm, q_cp, k_tr, k_cp, s_mm, iotas = (sem(x) for x in ("k_in", "q_mm", "q_cp", "k_tr", "k_cp", "s_mm", "iotas"))
        r_tr, r_cp, g_dg, g_mm, g_cp, g2_done = (sem(x) for x in ("r_tr", "r_cp", "g_dg", "g_mm", "g_cp", "g2_done"))
        passed = sem("rt_passed")
        LISTS = [(n, s) for n in range(2) for s in range(2)]
        DV = Steps(sem("rt_dve"), " ".join(
            ["sc"] + [f"{m}{n}{s}" for m in ("m1", "i1", "mr", "m2", "i2") for n, s in LISTS] + ["tf", "cand"]
            + [f"{m}{n}" for m in ("b1", "j1", "br", "b2", "j2") for n in range(2)]
            + ["hi", "lo", "pf", "eq0", "mul0", "red0", "eq1", "mul1", "red1", "ef", "idx", "diff", "sum", "rec", "gates"]), True)
        AC = Steps(sem("rt_act"), "exp", True)
        wq = a["peer_wq"].rearrange("l (k p) n -> (l p) k n", p=P)
        with nc.Block() as block:

            @block.sync
            def _(sp):
                for j in range(KC):
                    sp.dma_start(keys[:, j, :], a["peer_subkeys"][0, j // 2, j % 2, :, :]).then_inc(k_in, 16)
                for n in range(4):
                    if n >= 2:
                        sp.wait_ge(q_mm, n - 1)
                    sp.dma_start(w[:, n % 2, :, :], wq[:, :, n * 512:(n + 1) * 512]).then_inc(w_in[n % 2], 16)

            @block.gpsimd
            def _(pool):
                nc.gpsimd.iota(iota_i[:, :], [[1, TOPK]], base=0, channel_multiplier=0).then_inc(iotas, 1)

            @block.tensor
            def _(pe):
                pe.wait_ge(k_in, 16 * KC)
                for g in range(4):
                    for c in range(4):
                        last = nc.tensor.transpose(ps[:, 4 + g, c * P:(c + 1) * P], keys[:, 4 * g + c, :], ident[:, :])
                    last.then_inc(k_tr, 1)
                for n in range(4):
                    pe.wait_ge(w_in[n % 2], 16 * (n // 2 + 1))
                    if n >= 2:
                        pe.wait_ge(q_cp, n - 1)
                    for c in range(4):
                        for k in range(KC):
                            last = nc.tensor.matmul(ps[:, 2 * (n % 2) + c // 2, (c % 2) * SEQ:(c % 2 + 1) * SEQ],
                                                    w[:, n % 2, k, c * P:(c + 1) * P], h2T[:, k, :], start=(k == 0), stop=(k == KC - 1))
                    last.then_inc(q_mm, 1)
                for g in range(16):
                    pe.wait_ge(k_cp, 4)
                    if g >= 4:
                        pe.wait_ge(r_cp, g - 3)
                    src, n, j0 = (h2T, xT)[g // 8], (g % 8) // 4, (g % 4) * 4
                    for c in range(4):
                        last = nc.tensor.transpose(ps[:, 4 + g % 4, c * P:(c + 1) * P], src[:, j0 + c, n * P:(n + 1) * P], ident[:, :])
                    last.then_inc(r_tr, 1)
                for g in range(4):
                    pe.wait_ge(g_dg, g + 1)
                    pe.wait_ge(r_cp, 13 + g)
                    nc.tensor.matmul(ps[:, 4 + g, :], ones[:, :], diag[:, :, :].rearrange("p c t -> p (c t)"),
                                     start=True, stop=True).then_inc(g_mm, 1)
                pe.wait_ge(q_cp, 4)
                pe.wait_ge(g_cp, 4)
                for n in range(2):
                    for j in range(KC):
                        last = nc.tensor.matmul(ps[:, 4 * n + j // 4, (j % 4) * PK:(j % 4 + 1) * PK], qT[:, j, n * P:(n + 1) * P],
                                                keysT[:, j, :], start=True, stop=True)
                last.then_inc(s_mm, 1)

            @block.scalar
            def _(act):
                for g in range(4):
                    act.wait_ge(k_tr, g + 1)
                    nc.scalar.activation(keysT[:, 4 * g:4 * g + 4, :], ps[:, 4 + g, :].rearrange("p (c k) -> p c k", k=PK),
                                         ACT.Copy).then_inc(k_cp, 1)
                for n in range(4):
                    act.wait_ge(q_mm, n + 1)
                    b = 2 * (n % 2)
                    nc.scalar.activation(qT[:, 4 * n:4 * n + 4, :], ps[:, b:b + 2, :].rearrange("p b (c t) -> p (b c) t", t=SEQ),
                                         ACT.Copy).then_inc(q_cp, 1)
                for g in range(16):
                    act.wait_ge(r_tr, g + 1)
                    dst, n, j0 = (h2_rows, x_rows)[g // 8], (g % 8) // 4, (g % 4) * 4
                    nc.scalar.activation(dst[:, n, j0 * P:(j0 + 4) * P], ps[:, 4 + g % 4, :], ACT.Copy).then_inc(r_cp, 1)
                for g in range(4):
                    act.wait_ge(g_mm, g + 1)
                    nc.scalar.activation(g2_rows[:, g * 512:(g + 1) * 512], ps[:, 4 + g, :], ACT.Copy).then_inc(g_cp, 1)
                AC.open(act)
                with act.Fori(0, PH) as i:
                    act.wait_ge(*DV.by("diff", i))
                    nc.scalar.activation(soft[:, :, :], soft[:, :, :], ACT.Exp).then_inc(*AC.did("exp"))
                AC.end()

            @block.vector
            def _(dve):
                nc.vector.tensor_tensor(g2[:, :], modT[:, 5 * KC:6 * KC, 0], par[:, col["norm_post2"]:col["norm_post2"] + KC],
                                        ALU.mult).then_inc(g2_done, 1)
                dve.wait_ge(g2_done, 1)
                for g in range(4):
                    if g:
                        dve.wait_ge(g_mm, g)
                    for c in range(4):
                        last = nc.vector.tensor_scalar(diag[:, c, :], ident[:, :], g2[:, 4 * g + c:4 * g + c + 1], None, ALU.mult)
                    last.then_inc(g_dg, 1)
                dve.wait_ge(iotas, 1)
                nc.vector.tensor_copy(iota_f[:, :], iota_i[:, :]).then_inc(g2_done, 1)
                dve.wait_ge(g2_done, 2)
                dve.wait_ge(s_mm, 1)
                DV.open(dve)
                scores = ps[:, :, :].rearrange("p (n b) (c k) -> p n (b c) k", n=2, c=4)

                with dve.Fori(0, PH) as i:
                    dve.wait_ge(*DV.before("gates", i))
                    nc.vector.tensor_copy(sc[:, :, :, :], scores[:, :, ds(i * 2, 2), :]).then_inc(*DV.did("sc"))
                    wait_alone(dve, passed, *DV.by("sc", i))
                    for n, s in LISTS:
                        nc.vector.max(top_s[:, n, s, 0:8], sc[:, n, s, :]).then_inc(*DV.did(f"m1{n}{s}"))
                    for n, s in LISTS:
                        wait_alone(dve, passed, *DV.by(f"m1{n}{s}", i))
                        nc.vector.max_index(top_i[:, n, s, 0:8], top_s[:, n, s, 0:8], sc[:, n, s, :]).then_inc(*DV.did(f"i1{n}{s}"))
                    for n, s in LISTS:
                        nc.vector.match_replace(sc2[:, n, s, :], top_s[:, n, s, 0:8], sc[:, n, s, :], -3.0e38).then_inc(*DV.did(f"mr{n}{s}"))
                    for n, s in LISTS:
                        wait_alone(dve, passed, *DV.by(f"mr{n}{s}", i))
                        nc.vector.max(top_s[:, n, s, 8:16], sc2[:, n, s, :]).then_inc(*DV.did(f"m2{n}{s}"))
                    for n, s in LISTS:
                        wait_alone(dve, passed, *DV.by(f"m2{n}{s}", i))
                        nc.vector.max_index(top_i[:, n, s, 8:16], top_s[:, n, s, 8:16], sc2[:, n, s, :]).then_inc(*DV.did(f"i2{n}{s}"))
                    dve.wait_ge(*DV.by("i211", i))
                    nc.vector.tensor_copy(top_f[:, :, :, :], top_i[:, :, :, :]).then_inc(*DV.did("tf"))
                    nc.vector.tensor_tensor(cand[:, :, :, :], top_s[:, :, 0, :].unsqueeze(3).broadcast_to([P, 2, TOPK, TOPK]),
                                            top_s[:, :, 1, :].unsqueeze(2).broadcast_to([P, 2, TOPK, TOPK]), ALU.add).then_inc(*DV.did("cand"))
                    wait_alone(dve, passed, *DV.by("cand", i))
                    flat = lambda m, n: m[:, n, :, :].rearrange("p a b -> p (a b)")
                    for n in range(2):
                        nc.vector.max(best_s[:, n, 0:8], flat(cand, n)).then_inc(*DV.did(f"b1{n}"))
                    for n in range(2):
                        wait_alone(dve, passed, *DV.by(f"b1{n}", i))
                        nc.vector.max_index(best_j[:, n, 0:8], best_s[:, n, 0:8], flat(cand, n)).then_inc(*DV.did(f"j1{n}"))
                    for n in range(2):
                        nc.vector.match_replace(flat(cand2, n), best_s[:, n, 0:8], flat(cand, n), -3.0e38).then_inc(*DV.did(f"br{n}"))
                    for n in range(2):
                        wait_alone(dve, passed, *DV.by(f"br{n}", i))
                        nc.vector.max(best_s[:, n, 8:16], flat(cand2, n)).then_inc(*DV.did(f"b2{n}"))
                    for n in range(2):
                        wait_alone(dve, passed, *DV.by(f"b2{n}", i))
                        nc.vector.max_index(best_j[:, n, 8:16], best_s[:, n, 8:16], flat(cand2, n)).then_inc(*DV.did(f"j2{n}"))
                    dve.wait_ge(*DV.by("j21", i))
                    nc.vector.tensor_scalar(part_i[:, 0, :, :], best_j[:, :, :], 4, None, ALU.logical_shift_right).then_inc(*DV.did("hi"))
                    nc.vector.tensor_scalar(part_i[:, 1, :, :], best_j[:, :, :], TOPK - 1, None, ALU.bitwise_and).then_inc(*DV.did("lo"))
                    dve.wait_ge(*DV.by("lo", i))
                    nc.vector.tensor_copy(part_f[:, :, :, :], part_i[:, :, :, :]).then_inc(*DV.did("pf"))
                    dve.wait_ge(*DV.by("pf", i))
                    for s in range(2):
                        if s:
                            dve.wait_ge(*DV.by("red0", i))
                        nc.vector.tensor_tensor(hot[:, :, :, :], part_f[:, s, :, :].unsqueeze(3).broadcast_to([P, 2, TOPK, TOPK]),
                                                iota_f[:, :].unsqueeze(1).unsqueeze(1).broadcast_to([P, 2, TOPK, TOPK]),
                                                ALU.is_equal).then_inc(*DV.did(f"eq{s}"))
                        dve.wait_ge(*DV.by(f"eq{s}", i))
                        nc.vector.tensor_tensor(hot[:, :, :, :], hot[:, :, :, :],
                                                top_f[:, :, s, :].unsqueeze(2).broadcast_to([P, 2, TOPK, TOPK]), ALU.mult).then_inc(*DV.did(f"mul{s}"))
                        dve.wait_ge(*DV.by(f"mul{s}", i))
                        nc.vector.tensor_reduce(ex[:, s, :, :], hot[:, :, :, :], AX, ALU.add).then_inc(*DV.did(f"red{s}"))
                    dve.wait_ge(*DV.by("red1", i))
                    nc.vector.scalar_tensor_tensor(ef[:, :, :], ex[:, 0, :, :], float(PK), ex[:, 1, :, :], ALU.mult, ALU.add).then_inc(*DV.did("ef"))
                    dve.wait_ge(*DV.by("ef", i))
                    nc.vector.tensor_copy(idx[:, :].rearrange("p (n h) -> p n h", n=2)[:, :, ds(i * TOPK, TOPK)], ef[:, :, :]).then_inc(*DV.did("idx"))
                    nc.vector.tensor_tensor(soft[:, :, :], best_s[:, :, :], best_s[:, :, 0:1].broadcast_to([P, 2, TOPK]),
                                            ALU.subtract).then_inc(*DV.did("diff"))
                    dve.wait_ge(*AC.by("exp", i))
                    nc.vector.tensor_reduce(total[:, :], soft[:, :, :], AX, ALU.add).then_inc(*DV.did("sum"))
                    dve.wait_ge(*DV.by("sum", i))
                    nc.vector.reciprocal(total[:, :], total[:, :]).then_inc(*DV.did("rec"))
                    dve.wait_ge(*DV.by("rec", i))
                    nc.vector.tensor_tensor(gates[:, :].rearrange("p (n h) -> p n h", n=2)[:, :, ds(i * TOPK, TOPK)], soft[:, :, :],
                                            total[:, :].unsqueeze(2).broadcast_to([P, 2, TOPK]), ALU.mult).then_inc(*DV.did("gates"))
                DV.end()


def experts(nc, sb, sem, ps, a, out, ident, idx, gates, h2_rows, x_rows, g2_rows):
    with ExitStack() as stage:
        def t(name, shape, dt=F32):
            return sb(name, list(shape), dt, ctx=stage)

        NB = 4
        TURNS = 2 * PH
        ub, vb = [t(f"ub{b}", [P, D]) for b in range(NB)], [t(f"vb{b}", [P, D]) for b in range(NB)]
        junk, fin = t("junk", [P, D]), t("fin", [P, D])
        fin2 = ub[0]
        ixu, ixv = t("ixu", [P, TOPK], U32), t("ixv", [P, TOPK], U32)
        dots, acts, coef = t("dots", [P, TOPK]), t("acts", [P, TOPK]), t("coef", [P, TOPK])
        diag = t("diag", [P, 2, P])
        zero, eps_col = t("zero", [P, P]), t("x_eps", [P, 1])
        ssq, rstd = t("x_ssq", [P, 2]), t("x_rstd", [P, 2])
        u_in, v_in = [sem(f"u_in{b}") for b in range(NB)], [sem(f"v_in{b}") for b in range(NB)]
        consts, opened, stored = sem("x_consts"), sem("x_open"), sem("x_stored")
        u_tab = a["peer_u"].rearrange("l e d -> (l e) d")
        v_tab = a["peer_v"].rearrange("l e d -> (l e) d")
        DU = Steps(sem("x_du"), "ix " + " ".join(f"dot{k}" for k in range(TOPK)))
        GE = Steps(sem("x_ge"), "gelu")
        DC = Steps(sem("x_dc"), "ix coef")
        DG = Steps(sem("x_dg"), " ".join(f"dg{k}" for k in range(TOPK)))
        PV = Steps(sem("x_pv"), " ".join(f"v{k}" for k in range(TOPK)), True)
        passed = sem("x_passed")
        done, fin_a = sem("x_fin"), sem("x_fin_a")

        def program(emit_u, emit_v, engine, first=None):
            emit_u(0, 0)
            for n in range(2):
                lo = n * PH
                with engine.Fori(lo, lo + PH - 1) as i:
                    emit_v(i, n, i + 1, n)
                emit_v(lo + PH - 1, n, lo + PH if n == 0 else None, 1)

        def fresh(steps):
            steps.at = 0

        with nc.Block() as block:

            @block.gpsimd
            def _(pool):
                nc.gpsimd.memset(zero[:, :], 0.0).then_inc(consts, 1)
                nc.gpsimd.memset(eps_col[:, :], EPS).then_inc(consts, 1)

                def gather_u(u, k):
                    b = k % NB
                    if k == 0:
                        wait_alone(pool, passed, *DU.by("ix", u))
                    if k >= NB:
                        wait_alone(pool, passed, *DU.by(f"dot{k - NB}", u))
                    nc.gpsimd.indirect_dma_start(ub[b][:, :], None, u_tab, bass.IndirectOffsetOnAxis(ap=ixu[:, k:k + 1], axis=0)
                                                 ).then_inc(u_in[b], 16)

                def gather_v(v, k):
                    b = k % NB
                    if k == 0:
                        wait_alone(pool, passed, *DC.by("ix", v))
                    wait_alone(pool, passed, *(PV.by(f"v{k - NB}", v) if k >= NB else PV.before(f"v{TOPK - NB + k}", v)))
                    nc.gpsimd.indirect_dma_start(vb[b][:, :], None, v_tab, bass.IndirectOffsetOnAxis(ap=ixv[:, k:k + 1], axis=0)
                                                 ).then_inc(v_in[b], 16)

                def emit_u(u, n):
                    for k in range(TOPK):
                        gather_u(u, k)

                def emit_v(v, n, u, un):
                    for k in range(TOPK):
                        gather_v(v, k)
                        if u is not None:
                            gather_u(u, k)

                program(emit_u, emit_v, pool)

            @block.vector
            def _(dve):
                def dot(u, n, k):
                    dve.wait_ge(u_in[k % NB], u * (16 * TOPK // NB) + 16 * (k // NB + 1))
                    if k:
                        dve.wait_ge(*DU.by(f"dot{k - 1}", u))
                    else:
                        dve.wait_ge(*DU.by("ix", u))
                    nc.vector.scalar_tensor_tensor(junk[:, :], ub[k % NB][:, :], 1.0, h2_rows[:, n, :], ALU.mult, ALU.mult,
                                                   accum_out=dots[:, k:k + 1]).then_inc(*DU.did(f"dot{k}"))

                def emit_u(u, n):
                    fresh(DU)
                    nc.vector.tensor_copy(ixu[:, :], idx[:, ds(u * TOPK, TOPK)]).then_inc(*DU.did("ix"))
                    for k in range(TOPK):
                        dot(u, n, k)

                def emit_v(v, n, u, un):
                    fresh(DC)
                    dve.wait_ge(*PV.before(f"v{TOPK - 1}", v))
                    nc.vector.tensor_copy(ixv[:, :], idx[:, ds(v * TOPK, TOPK)]).then_inc(*DC.did("ix"))
                    dve.wait_ge(*GE.by("gelu", v))
                    nc.vector.tensor_tensor(coef[:, :], acts[:, :], gates[:, ds(v * TOPK, TOPK)], ALU.mult).then_inc(*DC.did("coef"))
                    if u is not None:
                        dve.wait_ge(*DU.by(f"dot{TOPK - 1}", v))
                        emit_u(u, un)

                program(emit_u, emit_v, dve)
                for n in range(2):
                    dve.wait_ge(done, 4 * n + 2)
                    nc.vector.reciprocal(rstd[:, n:n + 1], rstd[:, n:n + 1]).then_inc(done, 1)
                    dve.wait_ge(done, 4 * n + 3)
                    if n:
                        dve.wait_ge(stored, 16)
                    nc.vector.scalar_tensor_tensor(fin[:, :], ps[:, 4 * n:4 * n + 4, :].rearrange("p b t -> p (b t)"), rstd[:, n:n + 1],
                                                   g2_rows[:, :], ALU.mult, ALU.mult).then_inc(fin_a, 1)
                    dve.wait_ge(fin_a, n + 1)
                    nc.vector.tensor_tensor(fin[:, :], fin[:, :], x_rows[:, n, :], ALU.add).then_inc(done, 1)

            @block.scalar
            def _(act):
                def emit_u(u, n):
                    return

                def emit_v(v, n, u, un):
                    fresh(GE)
                    fresh(DG)
                    act.wait_ge(*DU.by(f"dot{TOPK - 1}", v))
                    nc.scalar.activation(acts[:, :], dots[:, :], ACT.Gelu).then_inc(*GE.did("gelu"))
                    act.wait_ge(*DC.by("coef", v))
                    for k in range(TOPK):
                        act.wait_ge(*(PV.by(f"v{k - 2}", v) if k >= 2 else PV.before(f"v{TOPK - 2 + k}", v)))
                        nc.scalar.activation(diag[:, k % 2, :], ident[:, :], ACT.Copy, scale=coef[:, k:k + 1]).then_inc(*DG.did(f"dg{k}"))

                program(emit_u, emit_v, act)
                act.wait_ge(consts, 2)
                act.wait_ge(*PV.by(f"v{TOPK - 1}", TURNS - 1))
                act.wait_ge(opened, 2)
                for n in range(2):
                    if n:
                        act.wait_ge(done, 4)
                    nc.scalar.activation(fin2[:, :], ps[:, 4 * n:4 * n + 4, :].rearrange("p b t -> p (b t)"), ACT.Square,
                                         accum_out=ssq[:, n:n + 1]).then_inc(done, 1)
                    act.wait_ge(done, 4 * n + 1)
                    nc.scalar.activation(rstd[:, n:n + 1], ssq[:, n:n + 1], ACT.Sqrt, scale=1.0 / D, bias=eps_col[:, 0:1]).then_inc(done, 1)

            @block.tensor
            def _(pe):
                PV.open(pe)
                pe.wait_ge(consts, 1)

                def emit_u(u, n):
                    for m in range(2):
                        for c in range(4):
                            nc.tensor.matmul(ps[:, 4 * m + c, :], zero[:, :], g2_rows[:, c * 512:(c + 1) * 512], start=True, stop=False)

                def emit_v(v, n, u, un):
                    fresh(PV)
                    for k in range(TOPK):
                        pe.wait_ge(*DG.by(f"dg{k}", v))
                        pe.wait_ge(v_in[k % NB], v * (16 * TOPK // NB) + 16 * (k // NB + 1))
                        for c in range(4):
                            last = nc.tensor.matmul(ps[:, 4 * n + c, :], diag[:, k % 2, :], vb[k % NB][:, c * 512:(c + 1) * 512],
                                                    start=False, stop=False)
                        last.then_inc(*PV.did(f"v{k}"))

                program(emit_u, emit_v, pe)
                for m in range(2):
                    for c in range(4):
                        last = nc.tensor.matmul(ps[:, 4 * m + c, :], zero[:, :], g2_rows[:, c * 512:(c + 1) * 512], start=False, stop=True)
                    last.then_inc(opened, 1)

            @block.sync
            def _(sp):
                for n in range(2):
                    sp.wait_ge(done, 4 * n + 4)
                    sp.dma_start(out[0, n * P:(n + 1) * P, :], fin[:, :]).then_inc(stored, 16)
                sp.wait_ge(stored, 32)


_NAMES = ["x", "c", "ctx", "c_ctx", "w_mod", "b_mod", "norm_pre1", "norm_post1", "norm_pre2", "norm_post2", "w_in",
          "rw_mu", "rw_w0", "rw_w2", "rw_a0", "rw_a2", "rw_g2", "rw_k_k", "rw_k_a", "rw_r_k", "rw_ln_w", "rw_ln_b",
          "ssm_conv_w", "ssm_conv_b", "ssm_dt_bias", "ssm_a_log", "ssm_d", "ssm_norm_w", "w_branch_a", "w_branch_b",
          "w_out", "peer_wq", "peer_subkeys", "peer_u", "peer_v"]


def kernel(**inputs):
    import numpy as np
    import concourse.bacc as bacc
    from concourse.bass_utils import run_bass_kernel_spmd

    nc = bacc.Bacc("TRN2", target_bir_lowering=False, num_devices=1)
    arrays, aps = {}, {}
    for name in _NAMES:
        v = np.ascontiguousarray(inputs[name])
        arrays[f"in_{name}"] = v
        aps[name] = nc.dram_tensor(f"in_{name}", v.shape, mybir.dt.from_np(v.dtype), kind="ExternalInput").ap()
    out = nc.dram_tensor("out_x", (1, SEQ, D), F32, kind="ExternalOutput").ap()
    hybrid_block(nc, aps, out)
    r = run_bass_kernel_spmd(nc, [arrays], core_ids=[0])
    return r.results[0]["out_x"]
```

```python
from contextlib import ExitStack

import concourse.bass as bass
from concourse import mybir

F32 = mybir.dt.float32
U32 = mybir.dt.uint32
ALU = mybir.AluOpType
ACT = mybir.ActivationFunctionType
AX = mybir.AxisListType.X
ds = bass.ds

P = 128
D = 2048
KC = D // P
SEQ = 256
TOK = 2 * SEQ
NT = TOK // P
GRID_W = 64
GRID_R = SEQ // GRID_W
EPS = 1e-6
HEAD = 64
PAIRS = D // P
LW, LA, LG = 96, 96, 256
LN_X_EPS = 64e-5
GROUPS = 8
GW = D // GROUPS
STATE = 128
CONV = 5
SH = 32
R0, K0, V0, L0 = 0, D, 2 * D, 3 * D
RW_COLS = 3 * D + 2 * LW + 2 * LA + LG
Z0 = RW_COLS
X0 = Z0 + D
B0 = X0 + D
C0 = B0 + GROUPS * STATE
DT0 = C0 + GROUPS * STATE
GA0 = DT0 + 2 * SH
N_MOD = 6
PH, PK, TOPK = 8, 128, 16
SLOTS = PH * TOPK
DECAY = -0.6065306597126334


class Steps:

    def __init__(self, sem, names, loop=False):
        self.sem, self.names, self.at = sem, names.split(), 0
        assert len(set(self.names)) == len(self.names), [n for n in self.names if self.names.count(n) > 1]
        self.n = len(self.names)
        self.base = self.n if loop else 0
        self.left_out = 0

    def open(self, engine):
        engine.sem_inc(self.sem, self.n)

    def did(self, name):
        assert self.at < self.n and self.names[self.at] == name, (name, self.names[self.at:self.at + 2])
        self.at += 1
        count, self.left_out = 1 + self.left_out, 0
        return self.sem, count

    def skip(self, *names):
        for name in names:
            assert self.names[self.at] == name, (name, self.names[self.at])
            self.at += 1
            self.left_out += 1

    def by(self, name, turn=0):
        return self.sem, turn * self.n + (self.base + self.names.index(name) + 1)

    def before(self, name, turn):
        return self.sem, turn * self.n + (self.names.index(name) + 1)

    def end(self):
        assert self.at == self.n and not self.left_out, self.names[self.at:]


def wait_alone(engine, passed, sem, value):
    engine.wait_ge(sem, value)
    engine.sem_inc(passed, 1)


def vector_rows(a):
    rows, at = {}, 0

    def add(name, ap, n, width=P):
        nonlocal at
        rows[name] = (at, ap, n, width)
        at += n

    for name in ("norm_pre1", "norm_post1", "norm_pre2", "norm_post2"):
        add(name, a[name].rearrange("l (j p) -> (l j) p", p=P), KC)
    add("a0", a["rw_a0"].rearrange("l d (j p) -> (l d j) p", p=P), 2 * KC)
    for name in ("rw_k_k", "rw_k_a", "rw_ln_w", "rw_ln_b", "ssm_norm_w"):
        add(name, a[name].rearrange("l (j p) -> (l j) p", p=P), KC)
    add("rw_r_k", a["rw_r_k"].rearrange("l (j e) k -> (l j) (e k)", e=2), KC)
    add("mu", a["rw_mu"][:, 0:L0].rearrange("l (j p) -> (l j) p", p=P), L0 // P)
    add("mu_l", a["rw_mu"][:, L0:L0 + 4 * LW].rearrange("l (j p) -> (l j) p", p=LW), 4, LW)
    add("mu_g", a["rw_mu"][:, L0 + 4 * LW:RW_COLS].rearrange("l (j p) -> (l j) p", p=P), 2)
    add("conv_w", a["ssm_conv_w"].rearrange("l t (j p) -> (l t j) p", p=P), CONV * (D + 2 * GROUPS * STATE) // P)
    add("conv_b", a["ssm_conv_b"].rearrange("l (j p) -> (l j) p", p=P), (D + 2 * GROUPS * STATE) // P)
    add("b_mod", a["b_mod"].rearrange("l (j p) -> (l j) p", p=P), N_MOD * KC)
    add("c", a["c"].rearrange("l (j p) -> (l j) p", p=P), KC)
    add("c_ctx", a["c_ctx"].rearrange("(j p) -> j p", p=P), KC)
    return rows, at


def hybrid_block(nc, a, out):
    rows, n_rows = vector_rows(a)
    tiles = (n_rows + P - 1) // P
    col = {name: r[0] for name, r in rows.items()}

    with ExitStack() as whole:
        whole.enter_context(nc.allow_non_contiguous_dma("weights are read in slices of columns"))
        def sb(name, shape, dt=F32, ctx=whole):
            return ctx.enter_context(nc.sbuf_tensor(name, shape, dt))

        def sem(name):
            return whole.enter_context(nc.semaphore(name))

        ps = whole.enter_context(nc.psum_tensor("ps", [P, 8, 512], F32))
        ident = sb("ident", [P, P])
        ones = sb("ones", [P, P])
        head_ones = sb("head_ones", [P, P])
        head_mean = sb("head_mean", [P, P])
        tri = sb("tri", [P, 2, 2, P])
        below = sb("below", [P, 2, 2, P])
        par = sb("par", [P, (tiles + 1) * P])
        modT = sb("modT", [P, N_MOD * KC, 2])
        silu_c = sb("silu_c", [P, KC, 2])
        hT = sb("hT", [P, KC, TOK])
        yaT = sb("yaT", [P, KC, SEQ])
        minus_half = sb("minus_half", [P, 1])
        pc = lambda name, j=0, n=1: par[:, col[name] + j:col[name] + j + n]
        SKIP_D = tiles * P

        setup(nc, sb, sem, ps, a, rows, tiles, ident, ones, head_ones, head_mean, tri, below, minus_half, par, silu_c, modT)
        norm_in(nc, sb, sem, ps, a, ident, minus_half, par, col, modT, hT)
        rwkv(nc, sb, sem, ps, a, ident, head_ones, head_mean, tri, below, par, col, hT, yaT)
        ybT = sb("ybT", [P, KC, SEQ])
        ssd(nc, sb, sem, ps, a, ident, ones, below, par, col, SKIP_D, silu_c, modT, hT, ybT)
        xT = sb("xT", [P, KC, SEQ])
        merge(nc, sb, sem, ps, a, ident, ones, par, col, modT, hT, yaT, ybT, xT)
        peer(nc, sb, sem, ps, a, out, ident, ones, par, col, modT, hT, yaT, ybT, xT)


def setup(nc, sb, sem, ps, a, rows, tiles, ident, ones, head_ones, head_mean, tri, below, minus_half, par, silu_c, modT):
    with ExitStack() as stage:
        raw = sb("raw", [P, tiles + 1, P], ctx=stage)
        skip = sb("skip", [KC, 2], ctx=stage)
        sig_c = sb("sig_c", [P, KC, 2], ctx=stage)
        w = sb("w_mod_ring", [P, 2, KC, 512], ctx=stage)
        mod_row = sb("mod_row", [2, 2, 512], ctx=stage)
        consts = sem("consts")
        raw_clear, raw_in = sem("raw_clear"), sem("raw_in")
        w_in = [sem("w_mod_in0"), sem("w_mod_in1")]
        par_tr, par_done, c_sig, c_done = sem("par_tr"), sem("par_done"), sem("c_sig"), sem("c_done")
        skip_done = sem("skip_done")
        row_mm, row_copied, row_tr, mod_done = sem("row_mm"), sem("row_copied"), sem("row_tr"), sem("mod_done")
        w_mod = a["w_mod"].rearrange("l (k p) n -> (l p) k n", p=P)
        BLOCKS = 2 * D // 512
        pieces = []
        for name, (at, ap, n, width) in rows.items():
            done = 0
            while done < n:
                tile, row = divmod(at + done, P)
                k = min(n - done, P - row)
                pieces.append((tile, row, k, width, ap[done:done + k, :]))
                done += k

        with nc.Block() as block:

            @block.gpsimd
            def _(pool):
                nc.gpsimd.memset(raw[:, :, :], 0.0).then_inc(raw_clear, 1)
                count = [0]

                def const(ins):
                    count[0] += 1
                    ins.then_inc(consts, 1)
                    pool.wait_ge(consts, count[0])

                def sel(ap, cmp, fill, base, cm, pattern):
                    const(nc.gpsimd.affine_select(out=ap, in_=ap, compare_op=cmp, fill=fill, base=base,
                                                  pattern=pattern, channel_multiplier=cm))

                const(nc.gpsimd.memset(minus_half[:, :], -0.5))
                const(nc.gpsimd.memset(ident[:, :], 0.0))
                sel(ident[:, :], ALU.not_equal, 1.0, 0, 1, [[-1, P]])
                const(nc.gpsimd.memset(ones[:, :], 1.0))
                for t, v in ((head_ones, 1.0), (head_mean, 1.0 / HEAD)):
                    const(nc.gpsimd.memset(t[:, :], 0.0))
                    const(nc.gpsimd.memset(t[0:HEAD, 0:HEAD], v))
                    const(nc.gpsimd.memset(t[HEAD:P, HEAD:P], v))
                const(nc.gpsimd.memset(tri[:, :, :, :], 0.5))
                const(nc.gpsimd.memset(below[:, :, :, :], 1.0))
                for d, sign in ((0, 1), (1, -1)):
                    for e, base in ((0, 0), (1, -1)):
                        sel(tri[:, d, e, :], ALU.is_ge, -0.5, base, -sign, [[sign, P]])
                    for e, base in ((0, -1), (1, 0)):
                        sel(below[:, d, e, :], ALU.is_ge, 0.0, base, -sign, [[sign, P]])
                CONSTS[0] = count[0]

            @block.sync
            def _(sp):
                for n in range(2):
                    sp.dma_start(w[:, n, :, :], w_mod[:, :, n * 512:(n + 1) * 512]).then_inc(w_in[n], 16)
                with sp.Fori(1, BLOCKS // 2) as i:
                    for n in range(2):
                        sp.wait_ge(row_mm, i * 2 + n - 1)
                        sp.dma_start(w[:, n, :, :],
                                     w_mod[:, :, ds(i * 1024 + n * 512, 512)]).then_inc(w_in[n], 16)

            @block.scalar
            def _(act):
                act.dma_start(skip[:, :], a["ssm_d"].rearrange("l (j e) -> (l j) e", e=2)).then_inc(raw_in, 16)
                act.wait_ge(raw_clear, 1)
                for tile, row, k, width, src in pieces:
                    act.dma_start(raw[row:row + k, tile, 0:width], src).then_inc(raw_in, 16)
                act.wait_ge(par_done, 2)
                c0 = rows["c"][0]
                for e in range(2):
                    nc.scalar.activation(sig_c[:, :, e], par[:, c0 + e * KC:c0 + (e + 1) * KC],
                                         ACT.Sigmoid).then_inc(c_sig, 1)
                with act.Fori(0, BLOCKS // 2) as i:
                    for n in range(2):
                        act.wait_ge(row_mm, i * 2 + n + 1)
                        nc.scalar.activation(mod_row[:, n, :], ps[0:2, n, :], ACT.Copy).then_inc(row_copied, 1)

            @block.vector
            def _(dve):
                dve.wait_ge(raw_in, 16 * (len(pieces) + 1))
                for e in range(2):
                    nc.vector.tensor_copy(raw[0:KC, tiles, e * HEAD:(e + 1) * HEAD],
                                          skip[:, e:e + 1].broadcast_to([KC, HEAD])).then_inc(skip_done, 1)
                for half in range(2):
                    lo, hi = half * 4, min(tiles + 1, half * 4 + 4)
                    dve.wait_ge(par_tr, hi)
                    nc.vector.tensor_copy(par[:, lo * P:hi * P], ps[:, 2 + half, 0:(hi - lo) * P]).then_inc(par_done, 1)
                dve.wait_ge(c_sig, 2)
                c0 = rows["c"][0]
                for e in range(2):
                    nc.vector.tensor_tensor(silu_c[:, :, e], sig_c[:, :, e], par[:, c0 + e * KC:c0 + (e + 1) * KC],
                                            ALU.mult).then_inc(c_done, 1)
                b0 = rows["b_mod"][0]
                dve.sem_inc(mod_done, 2)
                with dve.Fori(0, BLOCKS // 2) as i:
                    for n in range(2):
                        dve.wait_ge(row_tr, i * 2 + n + 1)
                        nc.vector.tensor_tensor(
                            modT[:, ds(i * 8 + n * 4, 4), :],
                            ps[:, 4 + n, 0:8].rearrange("p (j e) -> p j e", e=2),
                            par[:, ds(i * 8 + b0 + n * 4, 4)].unsqueeze(2).broadcast_to([P, 4, 2]),
                            ALU.add).then_inc(mod_done, 1)

            @block.tensor
            def _(pe):
                pe.wait_ge(consts, CONSTS[0])
                pe.wait_ge(raw_in, 16 * (len(pieces) + 1))
                pe.wait_ge(skip_done, 2)
                for t in range(tiles + 1):
                    nc.tensor.transpose(ps[:, 2 + t // 4, (t % 4) * P:(t % 4 + 1) * P], raw[:, t, :],
                                        ident[:, :]).then_inc(par_tr, 1)
                pe.wait_ge(c_done, 2)

                def turn_rows(count, n, guard):
                    pe.wait_ge(row_copied, count + 1)
                    pe.wait_ge(mod_done, guard)
                    for j in range(4):
                        last = nc.tensor.matmul(ps[:, 4 + n, 2 * j:2 * j + 2], mod_row[:, n, j * P:(j + 1) * P],
                                                ident[0:2, 0:2], start=True, stop=True)
                    last.then_inc(row_tr, 1)

                with pe.Fori(0, BLOCKS // 2) as i:
                    for n in range(2):
                        pe.wait_ge(w_in[n], i * 16 + 16)
                        for k in range(KC):
                            last = nc.tensor.matmul(ps[0:2, n, :], silu_c[:, k, :], w[:, n, k, :],
                                                    start=(k == 0), stop=(k == KC - 1))
                        last.then_inc(row_mm, 1)
                    for n in range(2):
                        turn_rows(i * 2 + n, n, i * 2 + 2)


CONSTS = [0]


def norm_in(nc, sb, sem, ps, a, ident, minus_half, par, col, modT, hT):
    with ExitStack() as stage:
        rows = sb("in_rows", [P, NT, D], ctx=stage)
        junk = sb("in_sq", [P, D], ctx=stage)
        ssq = sb("in_ssq", [P, NT], ctx=stage)
        rstd = sb("in_rstd", [P, NT], ctx=stage)
        gain = sb("in_gain", [P, KC, 2], ctx=stage)
        rows_in = [sem(f"rows_in{t}") for t in range(NT)]
        sq_done, rstd_done, gain_done, scaled, turned, h_done = (
            sem(x) for x in ("in_sq_done", "in_rstd_done", "in_gain_done", "in_scaled", "in_turned", "h_done"))
        srcs = [a["ctx"], a["ctx"], a["x"], a["x"]]
        with nc.Block() as block:

            @block.sync
            def _(sp):
                for t in range(NT):
                    lo = (t % 2) * P
                    sp.dma_start(rows[:, t, :], srcs[t][0, lo:lo + P, :]).then_inc(rows_in[t], 16)

            @block.scalar
            def _(act):
                for t in range(NT):
                    act.wait_ge(rows_in[t], 16)
                    if t:
                        act.wait_ge(sq_done, t)
                    nc.scalar.activation(junk[:, :], rows[:, t, :], ACT.Square,
                                         accum_out=ssq[:, t:t + 1]).then_inc(sq_done, 1)

            @block.gpsimd
            def _(pool):
                pool.wait_ge(sq_done, NT)
                nc.gpsimd.tensor_scalar(rstd[:, :], ssq[:, :], 1.0 / D, EPS, ALU.mult, ALU.add).then_inc(rstd_done, 1)
                pool.wait_ge(rstd_done, 1)
                nc.gpsimd.tensor_tensor(rstd[:, :], rstd[:, :], minus_half[:, 0:1].broadcast_to([P, NT]),
                                        ALU.pow).then_inc(rstd_done, 1)

            @block.vector
            def _(dve):
                g0 = col["norm_pre1"]
                nc.vector.scalar_tensor_tensor(gain[:, :, :], modT[:, KC:2 * KC, :], 1.0,
                                               par[:, g0:g0 + KC].unsqueeze(2).broadcast_to([P, KC, 2]),
                                               ALU.add, ALU.mult).then_inc(gain_done, 1)
                dve.wait_ge(rstd_done, 2)
                for t in range(NT):
                    nc.vector.tensor_scalar(rows[:, t, :], rows[:, t, :], rstd[:, t:t + 1], None,
                                            ALU.mult).then_inc(scaled, 1)
                dve.wait_ge(gain_done, 1)
                for j in range(KC):
                    dve.wait_ge(turned, j + 1)
                    for s, e in ((0, 1), (1, 0)):
                        nc.vector.tensor_scalar(hT[:, j, s * SEQ:(s + 1) * SEQ], ps[:, j % 4, s * SEQ:(s + 1) * SEQ],
                                                gain[:, j, e:e + 1], modT[:, j, e:e + 1],
                                                ALU.mult, ALU.add).then_inc(h_done, 1)

            @block.tensor
            def _(pe):
                pe.wait_ge(scaled, NT)
                for j in range(KC):
                    if j >= 4:
                        pe.wait_ge(h_done, 2 * (j - 3))
                    for t in range(NT):
                        last = nc.tensor.transpose(ps[:, j % 4, t * P:(t + 1) * P], rows[:, t, j * P:(j + 1) * P],
                                                   ident[:, :])
                    last.then_inc(turned, 1)


PP = ["k_k", "k_a", "om_ka", "r_k", "ln_w", "ln_b"]


def lora(nc, sb, sem, ps, a, par, col, hT, per_pair, shifts, tanh_w, low_a, gate_g):
    with ExitStack() as stage:
        w = sb("w_lora", [P, KC, 4 * LW + LG], ctx=stage)
        om = sb("lora_om", [P, 54], ctx=stage)
        hm = sb("lora_hm", [P, 54], ctx=stage)
        pad = sb("lora_pad", [P, 6, 2, SEQ + 2], ctx=stage)
        kept = sb("lora_kept", [P, 6, TOK], ctx=stage)
        near = sb("lora_near", [P, 6, TOK], ctx=stage)
        w_in, proj, padded, keeps, added, shifted, mus, pads, funcs = (
            sem(x) for x in ("lora_w", "lora_proj", "lora_padded", "lora_keeps", "lora_added", "lora_shifted",
                             "lora_mus", "lora_pads", "lora_funcs"))
        src = a["w_in"].rearrange("l (k p) n -> (l p) k n", p=P)
        m0 = col["mu"]
        parts = [(j * LW, LW, 0) for j in range(4)] + [(4 * LW + j * P, P, SEQ) for j in range(2)]
        with nc.Block() as block:

            @block.sync
            def _(sp):
                sp.dma_start(w[:, :, :], src[:, :, L0:RW_COLS]).then_inc(w_in, 16)

            @block.gpsimd
            def _(pool):
                nc.gpsimd.memset(pad[:, :, :, :], 0.0).then_inc(pads, 1)
                pool.wait_ge(pads, 1)
                nc.gpsimd.memset(tanh_w[LW:LW + 1, :, :], 1.0).then_inc(pads, 1)

            @block.tensor
            def _(pe):
                pe.wait_ge(w_in, 16)
                for n, (c, m, t0) in enumerate(parts):
                    for k in range(KC):
                        last = nc.tensor.matmul(ps[0:m, n, t0:TOK], w[:, k, c:c + m], hT[:, k, t0:TOK],
                                                start=(k == 0), stop=(k == KC - 1))
                    last.then_inc(proj, 1)

            @block.scalar
            def _(act):
                act.wait_ge(pads, 1)
                act.wait_ge(mus, 2)
                for n, (c, m, t0) in enumerate(parts):
                    act.wait_ge(proj, n + 1)
                    s0 = t0 // SEQ
                    nc.scalar.activation(pad[0:m, n, s0:2, 1:SEQ + 1],
                                         ps[0:m, n, t0:TOK].rearrange("p (s t) -> p s t", t=SEQ),
                                         ACT.Copy).then_inc(padded, 1)
                    nc.scalar.activation(kept[0:m, n, t0:TOK], ps[0:m, n, t0:TOK], ACT.Copy,
                                         scale=om[0:m, 48 + n:49 + n]).then_inc(keeps, 1)
                for d in range(2):
                    act.wait_ge(shifted, d + 1)
                    nc.scalar.activation(tanh_w[0:LW, d, :], near[0:LW, d, :], ACT.Tanh).then_inc(funcs, 1)
                for j in range(2):
                    act.wait_ge(shifted, 5 + j)
                    nc.scalar.activation(gate_g[:, j, :], near[:, 4 + j, SEQ:TOK], ACT.Sigmoid).then_inc(funcs, 1)

            @block.vector
            def _(dve):
                nc.vector.tensor_scalar(om[:, :], par[:, m0:m0 + 54], -1.0, 1.0, ALU.mult, ALU.add).then_inc(mus, 1)
                nc.vector.tensor_scalar(hm[:, :], par[:, m0:m0 + 54], 0.5, None, ALU.mult).then_inc(mus, 1)
                dve.wait_ge(mus, 2)
                cols = {"k_k": col["rw_k_k"], "k_a": col["rw_k_a"], "r_k": col["rw_r_k"], "ln_w": col["rw_ln_w"], "ln_b": col["rw_ln_b"]}
                for n, name in enumerate(PP):
                    if name in cols:
                        c = cols[name]
                        nc.vector.tensor_copy(per_pair[:, :, n], par[:, c:c + KC])
                    elif name == "om_ka":
                        c = col["rw_k_a"]
                        nc.vector.tensor_scalar(per_pair[:, :, n], par[:, c:c + KC], -1.0, 1.0, ALU.mult, ALU.add)
                for n, c in enumerate((KC, 2 * KC, 0)):
                    nc.vector.tensor_copy(shifts[:, :, 2 * n], om[:, c:c + KC])
                    nc.vector.tensor_copy(shifts[:, :, 2 * n + 1], hm[:, c:c + KC])
                for d in range(2):
                    c = col["a0"] + d * KC
                    nc.vector.tensor_copy(shifts[:, :, 6 + d], par[:, c:c + KC])
                for n, (c, m, t0) in enumerate(parts):
                    dve.wait_ge(padded, n + 1)
                    s0 = t0 // SEQ
                    view = near[0:m, n, t0:TOK].rearrange("p (s t) -> p s t", t=SEQ)
                    nc.vector.tensor_tensor(view, pad[0:m, n, s0:2, 0:SEQ], pad[0:m, n, s0:2, 2:SEQ + 2],
                                            ALU.add).then_inc(added, 1)
                    dve.wait_ge(added, n + 1)
                    dve.wait_ge(keeps, n + 1)
                    out = low_a[:, n - 2, :] if n in (2, 3) else near[0:m, n, t0:TOK]
                    nc.vector.scalar_tensor_tensor(out, near[0:m, n, t0:TOK], hm[0:m, 48 + n:49 + n],
                                                   kept[0:m, n, t0:TOK], ALU.mult, ALU.add).then_inc(shifted, 1)


def rwkv(nc, sb, sem, ps, a, ident, head_ones, head_mean, tri, below, par, col, hT, yaT):
    with ExitStack() as stage:
        def t(name, *shape):
            return sb(name, list(shape), ctx=stage)

        per_pair = t("per_pair", P, PAIRS, len(PP))
        tanh_w = t("tanh_w", LW + 1, 2, TOK)
        low_a = t("low_a", LA, 2, TOK)
        gate_g = t("gate_g", P, 2, SEQ)
        shifts = t("shifts", P, PAIRS, 8)
        lora(nc, sb, sem, ps, a, par, col, hT, per_pair, shifts, tanh_w, low_a, gate_g)

        w = t("w_pair", P, 3, KC, P)
        lw2, la2, lg2 = t("lw2", LW + 1, 2, P), t("la2", LA, 2, P), t("lg2", P, 2, P)
        pp, pn = t("pp", P, len(PP)), t("pn", P, 8)
        blocks = t("blocks", P, 6, P)
        neg2 = t("neg2", P, 2, P)
        ident2 = t("ident2", P, P)
        ln_eps = t("ln_eps", P, 1)
        pad = t("pad", P, 3, 2, SEQ + 2)
        near = t("near", P, 3, TOK)
        kvr = t("kvr", P, 3, TOK)
        k_s, v_s, r_s = kvr[:, 0, :], kvr[:, 1, :], kvr[:, 2, SEQ:TOK]
        X, F = t("X", P, 4, NT, P), t("F", P, 4, NT, P)
        early = X[:, :, :, :].rearrange("p q n t -> p (q n t)")
        rate = early[:, 0:2 * TOK].rearrange("p (d t) -> p d t", d=2)
        rn, kk = early[:, 2 * TOK:3 * TOK], early[:, 3 * TOK:4 * TOK]
        sg, e_ng = F[:, 0:2, :, :], F[:, 2:4, :, :]
        sq, kd = t("sq", P, TOK), t("kd", P, 2, TOK)
        e_in = t("e_in", P, 2, NT, P)
        KR = t("KR", P, 2, NT, 2, P)
        Kh, Ah = t("Kh", P, 2, NT, P), t("Ah", P, 2, NT, P)
        em = t("em", P, 2, 3)
        Vt, Kt, At = t("Vt", P, NT, P), t("Kt", P, 2, NT, P), t("At", P, 2, NT, P)
        Gc, Gx = t("Gc", P, 4, 2, 2, P), t("Gx", P, 4, 2, 4, P)
        XT = t("XT", P, 4, NT, P)
        rhs, nsa, S = t("rhs", P, 4, HEAD), t("nsa", P, 4, HEAD), t("S", P, 2, HEAD)
        gate = t("gate", P, SEQ)
        y, yc, bonus = sq[:, 0:SEQ], sq[:, SEQ:TOK], t("bonus", P, SEQ)
        ysq, rs = rn[:, 0:SEQ], rn[:, SEQ:TOK]
        low = F[:, 0, :, :].rearrange("p n t -> p (n t)")
        passed, passed_pe = sem("rw_passed"), sem("rw_passed_pe")
        LEVELS = range(1, 6)
        K_SHARES = (4, 6, 8, 10, 12, 14, 16)
        QS = [(d, h) for d in range(2) for h in range(2)]
        order = [(0, 1, 2, 3), (1, 0, 3, 2)]

        w_sem = {n: sem("rw_w_in_" + "kvr"[n]) for n in range(3)}
        lw_sem, lg_sem, m_sem = sem("rw_lw_in"), sem("rw_lg_in"), sem("rw_masks")
        first_pe, first_act, first_dve = sem("rw_first_pe"), sem("rw_first_act"), sem("rw_first_dve")
        J = [(m, j) for j in range(4) for m in ("rhs", "sa", "y", "s") if not (m == "s" and j == 3 or m == "y" and j < 2)]
        PE = Steps(sem("rw_pe"), " ".join(
            ["cs0", "cs1", "kss", "gate", "vt", "r", "kt0", "at0", "kt1", "at1", "bonus"]
            + [f"g{q}{x}" for q in range(4) for x in "cxz"]
            + [n for lev in LEVELS for n in [f"{m}{lev}_{q}" for m in "EX" for q in range(4)] + (["k"] if lev == 3 else [])]
            + [f"T5_{q}" for q in range(4)] + ["P6_0", "P6_1", "Q6_0", "Q6_1"]
            + [n for m, j in J for n in [f"{m}{j}"] + {"rhs0": ["u0"], "sa0": ["u1"], "rhs1": ["a0"], "sa1": ["a1"]}.get(f"{m}{j}", [])]
            + ["v", "mean", "var"]), True)
        AC = Steps(sem("rw_act"), " ".join(
            [f"{x}{d}" for d in range(2) for x in ("exc", "inc", "neg")]
            + ["sq", "norm", "gate", "vt", "kt0", "at0", "kt1", "at1", "pad2", "keep2", "pad0", "keep0"]
            + [f"T5_{q}" for q in range(4)] + ["P6_0", "P6_1", "Q6_0", "Q6_1"]
            + ["rhs0", "sa0", "sg0", "rhs1", "sg1", "sa1", "rate0", "rhs2", "rate1", "sa2", "rhs3", "sa3", "yf", "pad1", "keep1", "ysq", "std"]), True)
        DV = Steps(sem("rw_dve"), " ".join(
            ["pp", "nmax", "nrec", "kk"] + [f"{x}{d}" for d in range(2) for x in ("kdf", "kd", "KK", "Kh", "Ah")]
            + ["em0", "em1", "em2", "rk", "bv"] + [f"g{q}{x}" for q in range(4) for x in "cxz"]
            + ["pn"] + [f"x1_{q}" for q in range(4)]
            + [n for lev in LEVELS for n in [f"F{lev}_{q}" for q in range(4)]
               + [x for q in range(4) for x in [f"X{lev}_{q}"] + ([f"T{lev}_{q}"] if lev < 5 else [])]
               + (["near2", "shift2"] if lev == 1 else ["near0", "shift0"] if lev == 4 else [])]
            + [f"s{j}_{d}" for j in range(3) for d in range(2)]
            + ["y", "yc", "near1", "shift1", "rec", "yn", "yl", "yb", "out"]), True)
        PO = Steps(sem("rw_pool"), " ".join(
            ["aa0", "rr0", "aa1", "rr1", "kfb", "rkk"]
            + [f"{x}{q}{y}" for q in range(4) for y in "cx" for x in ("m2", "i2", "at")]), True)

        w_in = a["w_in"].rearrange("l (k p) n -> (l p) k n", p=P)
        w2, w0 = a["rw_w2"].rearrange("l d c n -> (l c) d n"), a["rw_w0"]
        a2 = a["rw_a2"].rearrange("l d c n -> (l c) d n")
        g2 = a["rw_g2"].rearrange("l (k p) n -> (l p) k n", p=P)
        head = lambda h: slice(h * HEAD, (h + 1) * HEAD)
        A_T = lambda q, n: Gc[:, q, n, 0, :] if n < 2 else Gx[:, q, n - 2, 0, :]
        B1 = lambda q, n: Gc[:, q, n, 1, :] if n < 2 else Gx[:, q, n - 2, 2, :]
        early_half, late_half = (slice(0, 64), slice(64, 128)), (slice(64, 128), slice(0, 64))

        def turns(engine, steps, turn):
            with engine.Fori(0, PAIRS - 1) as i:
                turn(i, False)
            steps.end()
            steps.at = 0
            turn(PAIRS - 1, True)
            steps.end()

        with nc.Block() as block:

            @block.sync
            def _(sp):
                def low_rank(at):
                    sp.dma_start(lw2[0:LW, :, :], w2[:, :, at]).then_inc(lw_sem, 16)
                    sp.dma_start(lw2[LW:LW + 1, :, :], w0[:, :, at]).then_inc(lw_sem, 16)
                    sp.dma_start(la2[:, :, :], a2[:, :, at]).then_inc(lw_sem, 16)

                low_rank(slice(0, P))
                for n, c0 in enumerate((K0, V0, R0)):
                    sp.dma_start(w[:, n, :, :], w_in[:, :, c0:c0 + P]).then_inc(w_sem[n], 16)
                sp.dma_start(lg2[:, :, :], g2[:, :, 0:P]).then_inc(lg_sem, 16)
                sp.wait_ge(first_pe, 7)
                with sp.Fori(0, PAIRS - 1) as i:
                    for n, c0, name in ((2, R0, "r"), (0, K0, "k"), (1, V0, "v")):
                        if name == "v":
                            wait_alone(sp, passed, *PE.before("a1", i))
                            low_rank(ds(i * P + P, P))
                        wait_alone(sp, passed, *PE.before(name, i))
                        sp.dma_start(w[:, n, :, :], w_in[:, :, ds(i * P + (c0 + P), P)]).then_inc(w_sem[n], 16)
                    wait_alone(sp, passed, *PE.by("gate", i))
                    sp.dma_start(lg2[:, :, :], g2[:, :, ds(i * P + P, P)]).then_inc(lg_sem, 16)

            @block.gpsimd
            def _(pool):
                count = [0]

                def const(ins):
                    count[0] += 1
                    ins.then_inc(m_sem, 1)
                    pool.wait_ge(m_sem, count[0])

                PO.open(pool)
                const(nc.gpsimd.memset(blocks[:, :, :], 1.0))
                const(nc.gpsimd.memset(pad[:, :, :, :], 0.0))
                const(nc.gpsimd.memset(ln_eps[:, :], LN_X_EPS))
                for n in range(6):
                    b = 2 << n
                    v = blocks[:, n, :].rearrange("p (j b) -> p j b", b=b)
                    for base, cm, step in ((0, 1, -b), (b - 1, -1, b)):
                        const(nc.gpsimd.affine_select(out=v, in_=v, compare_op=ALU.is_ge, fill=0.0, base=base,
                                                      pattern=[[step, P // b], [0, b]], channel_multiplier=cm))
                for d in range(2):
                    const(nc.gpsimd.tensor_tensor(neg2[:, d, :], blocks[:, 0, :], below[:, d, 0, :], ALU.mult))
                    const(nc.gpsimd.tensor_scalar(neg2[:, d, :], neg2[:, d, :], -1.0, None, ALU.mult))
                const(nc.gpsimd.tensor_scalar(ident2[:, :], ident[:, :], 2.0, None, ALU.mult))
                MASKS[0] = count[0]

                def turn(i, last_turn):
                    for d in range(2):
                        pool.wait_ge(*DV.by("kk", i))
                        pool.wait_ge(*DV.by(f"kdf{d}", i))
                        nc.gpsimd.tensor_tensor(rate[:, d, :], rate[:, d, :], kk, ALU.mult).then_inc(*PO.did(f"aa{d}"))
                        pool.wait_ge(*AC.by(f"inc{d}", i))
                        pool.wait_ge(*PE.before("y3", i))
                        nc.gpsimd.tensor_tensor(KR[:, d, 2:4, 1, :], e_in[:, d, 2:4, :],
                                                r_s.rearrange("p (n t) -> p n t", t=P), ALU.mult).then_inc(*PO.did(f"rr{d}"))
                    pool.wait_ge(*DV.by("kd1", i))
                    pool.wait_ge(*DV.before("yb", i))
                    nc.gpsimd.tensor_tensor(bonus[:, :], kd[:, 0, SEQ:TOK], kd[:, 1, SEQ:TOK], ALU.add).then_inc(*PO.did("kfb"))
                    pool.wait_ge(*PO.by("kfb", i))
                    nc.gpsimd.tensor_tensor(bonus[:, :], bonus[:, :], r_s, ALU.mult).then_inc(*PO.did("rkk"))
                    for q, (d, h) in enumerate(QS):
                        for part, src, lo in (("c", Gc, 0), ("x", Gx, 2)):
                            pool.wait_ge(*DV.by(f"g{q}" + ("c" if part == "c" else "z"), i))
                            pool.wait_ge(*PE.before("sa3", i))
                            u = src[:, q, :, 0, :]
                            v = XT[:, q, lo:lo + 2, :]
                            wide = lambda m: m.unsqueeze(1).broadcast_to([P, 2, P])
                            nc.gpsimd.tensor_tensor(v, u, wide(neg2[:, d, :]), ALU.mult).then_inc(*PO.did(f"m2{q}{part}"))
                            pool.wait_ge(*PO.by(f"m2{q}{part}", i))
                            nc.gpsimd.tensor_tensor(v, v, wide(ident[:, :]), ALU.add).then_inc(*PO.did(f"i2{q}{part}"))
                            nc.gpsimd.tensor_tensor(u, u, wide(ident[:, :]), ALU.add).then_inc(*PO.did(f"at{q}{part}"))

                turns(pool, PO, turn)

            @block.scalar
            def _(act):
                AC.open(act)
                act.wait_ge(m_sem, MASKS[0])

                def sigmoids(d, bank, ready, mark):
                    act.wait_ge(*ready)
                    nc.scalar.activation(sg[:, d, :, :], ps[:, bank, :].rearrange("p (n c) -> p n c", c=P),
                                         ACT.Sigmoid).then_inc(*mark)

                def rates(d, bank, ready, params, mark):
                    act.wait_ge(*ready)
                    nc.scalar.activation(rate[:, d, :], ps[:, bank, :], ACT.Sigmoid, bias=params[:, 6 + d:7 + d]).then_inc(*mark)

                def padded(n, ready, mark_pad, mark_keep):
                    s0 = 1 if n == 2 else 0
                    act.wait_ge(*ready)
                    nc.scalar.activation(pad[:, n, s0:2, 1:SEQ + 1],
                                         ps[:, 4 + n, s0 * SEQ:TOK].rearrange("p (s t) -> p s t", t=SEQ),
                                         ACT.Copy).then_inc(*mark_pad)
                    nc.scalar.activation(kvr[:, n, s0 * SEQ:TOK], ps[:, 4 + n, s0 * SEQ:TOK], ACT.Copy,
                                         scale=pn[:, 2 * n:2 * n + 1]).then_inc(*mark_keep)

                act.wait_ge(first_dve, 1)
                for d in range(2):
                    sigmoids(d, d, (first_pe, d + 1), (first_act, 1))
                for d in range(2):
                    rates(d, 2 + d, (first_pe, 3 + d), pn, (first_act, 1))
                for n in range(3):
                    padded(n, (first_pe, 5 + n), (first_act, 1), (first_act, 1))

                def turn(i, last_turn):
                    for d in range(2):
                        act.wait_ge(*PE.by(f"cs{d}", i))
                        if d == 0:
                            act.wait_ge(*PE.before("y3", i))
                            act.wait_ge(*DV.before("s2_1", i))
                        c = ps[:, 2 * d:2 * d + 2, :].rearrange("p b (n e t) -> p (b n) e t", n=2, e=2)
                        nc.scalar.activation(KR[:, d, :, 0, :], c[:, :, 1, :], ACT.Exp, scale=DECAY).then_inc(*AC.did(f"exc{d}"))
                        nc.scalar.activation(e_in[:, d, :, :], c[:, :, 0, :], ACT.Exp, scale=DECAY).then_inc(*AC.did(f"inc{d}"))
                        nc.scalar.activation(e_ng[:, d, :, :], c[:, :, 0, :], ACT.Exp, scale=-DECAY).then_inc(*AC.did(f"neg{d}"))
                    act.wait_ge(*DV.by("pp", i))
                    c = PP.index("k_k")
                    nc.scalar.activation(sq[:, :], k_s, ACT.Square, scale=pp[:, c:c + 1]).then_inc(*AC.did("sq"))
                    act.wait_ge(*PE.by("kss", i))
                    nc.scalar.activation(rn, ps[:, 7, :], ACT.Sqrt).then_inc(*AC.did("norm"))
                    act.wait_ge(*PE.by("gate", i))
                    nc.scalar.activation(gate[:, :], ps[:, 4, 0:SEQ], ACT.Copy).then_inc(*AC.did("gate"))
                    for name, bank, dst in (("vt", 5, Vt[:, :, :]), ("kt0", 0, Kt[:, 0, :, :]), ("at0", 1, At[:, 0, :, :]),
                                            ("kt1", 2, Kt[:, 1, :, :]), ("at1", 3, At[:, 1, :, :])):
                        act.wait_ge(*PE.by(name, i))
                        nc.scalar.activation(dst, ps[:, bank, :].rearrange("p (n c) -> p n c", c=P),
                                             ACT.Copy).then_inc(*AC.did(name))
                    if last_turn:
                        AC.skip("pad2", "keep2", "pad0", "keep0")
                    else:
                        act.wait_ge(*DV.by("pn", i))
                        act.wait_ge(*PO.by("rkk", i))
                        padded(2, PE.by("r", i), AC.did("pad2"), AC.did("keep2"))
                        padded(0, PE.by("k", i), AC.did("pad0"), AC.did("keep0"))
                    for q in range(4):
                        act.wait_ge(*PE.by(f"T5_{q}", i))
                        nc.scalar.activation(XT[:, q, :, :], ps[:, q, :].rearrange("p (n c) -> p n c", c=P),
                                             ACT.Copy).then_inc(*AC.did(f"T5_{q}"))
                    for d in range(2):
                        act.wait_ge(*PE.by(f"P6_{d}", i))
                        nc.scalar.activation(low[late_half[d], :], ps[late_half[d], d, :], ACT.Copy).then_inc(*AC.did(f"P6_{d}"))
                    for d in range(2):
                        act.wait_ge(*PE.by(f"Q6_{d}", i))
                        nc.scalar.activation(XT[early_half[d], 2 * d:2 * d + 2, :, late_half[d]].rearrange("p q n c -> p (q n) c"),
                                             ps[early_half[d], 2 + d, :].rearrange("p (u c) -> p u c", c=64),
                                             ACT.Copy, scale=-1.0).then_inc(*AC.did(f"Q6_{d}"))
                    for j in range(4):
                        act.wait_ge(*PE.by(f"rhs{j}", i))
                        nc.scalar.activation(rhs[:, :, :].rearrange("p (d h) v -> p h d v", h=2),
                                             ps[:, 0:2, 0:2 * HEAD].rearrange("p h (d v) -> p h d v", v=HEAD),
                                             ACT.Copy).then_inc(*AC.did(f"rhs{j}"))
                        if j in (1, 2):
                            if last_turn:
                                AC.skip(("sg1", "rate1")[j - 1])
                            elif j == 1:
                                sigmoids(1, 6, PE.by("u1", i), AC.did("sg1"))
                            else:
                                rates(1, 6, PE.by("a1", i), pn, AC.did("rate1"))
                        act.wait_ge(*PE.by(f"sa{j}", i))
                        nc.scalar.activation(nsa[:, :, :], ps[:, 2, 0:4 * HEAD].rearrange("p (q v) -> p q v", v=HEAD),
                                             ACT.Copy, scale=-1.0).then_inc(*AC.did(f"sa{j}"))
                        if j in (0, 1):
                            if last_turn:
                                AC.skip(("sg0", "rate0")[j])
                            elif j == 0:
                                sigmoids(0, 4, PE.by("u0", i), AC.did("sg0"))
                            else:
                                rates(0, 4, PE.by("a0", i), pn, AC.did("rate0"))
                    act.wait_ge(*PE.by("y3", i))
                    nc.scalar.activation(y, ps[:, 3, 0:SEQ], ACT.Copy).then_inc(*AC.did("yf"))
                    if last_turn:
                        AC.skip("pad1", "keep1")
                    else:
                        padded(1, PE.by("v", i), AC.did("pad1"), AC.did("keep1"))
                    act.wait_ge(*DV.by("yc", i))
                    nc.scalar.activation(ysq, yc, ACT.Square).then_inc(*AC.did("ysq"))
                    act.wait_ge(*PE.by("var", i))
                    nc.scalar.activation(rs, ps[:, 7, 0:SEQ], ACT.Sqrt, bias=ln_eps[:, 0:1]).then_inc(*AC.did("std"))

                turns(act, AC, turn)

            @block.vector
            def _(dve):
                DV.open(dve)
                dve.wait_ge(m_sem, MASKS[0])
                pcol = lambda name: pp[:, PP.index(name):PP.index(name) + 1]

                def shift(n, ready, kept, mark_near, wait_near, mark_shift):
                    s0 = 1 if n == 2 else 0
                    dve.wait_ge(*ready)
                    nc.vector.tensor_tensor(near[:, n, s0 * SEQ:TOK].rearrange("p (s t) -> p s t", t=SEQ),
                                            pad[:, n, s0:2, 0:SEQ], pad[:, n, s0:2, 2:SEQ + 2], ALU.add).then_inc(*mark_near)
                    dve.wait_ge(*wait_near)
                    dve.wait_ge(*kept)
                    nc.vector.scalar_tensor_tensor(kvr[:, n, s0 * SEQ:TOK], near[:, n, s0 * SEQ:TOK], pn[:, 2 * n + 1:2 * n + 2],
                                                   kvr[:, n, s0 * SEQ:TOK], ALU.mult, ALU.add).then_inc(*mark_shift)

                nc.vector.tensor_copy(pn[:, :], shifts[:, 0, :]).then_inc(first_dve, 1)
                for n in range(3):
                    shift(n, (first_act, 5 + 2 * n), (first_act, 6 + 2 * n), (first_dve, 1), (first_dve, 2 + 2 * n), (first_dve, 1))

                def turn(i, last_turn):
                    dve.wait_ge(*AC.before("std", i))
                    dve.wait_ge(*DV.before("out", i))
                    if last_turn:
                        nc.vector.tensor_copy(pp[:, :], per_pair[:, PAIRS - 1, :]).then_inc(*DV.did("pp"))
                    else:
                        nc.vector.tensor_copy(pp[:, :], per_pair[:, ds(i, 1), :].rearrange("p a n -> p (a n)")).then_inc(*DV.did("pp"))
                    dve.wait_ge(*DV.by("pp", i))
                    dve.wait_ge(*AC.by("norm", i))
                    nc.vector.tensor_scalar(rn, rn, 1e-12, None, ALU.max).then_inc(*DV.did("nmax"))
                    dve.wait_ge(*DV.by("nmax", i))
                    nc.vector.reciprocal(rn, rn).then_inc(*DV.did("nrec"))
                    dve.wait_ge(*DV.by("nrec", i))
                    nc.vector.scalar_tensor_tensor(kk, k_s, pcol("k_k"), rn, ALU.mult, ALU.mult).then_inc(*DV.did("kk"))
                    dve.wait_ge(*DV.by("kk", i))
                    flat = lambda m: m.rearrange("p n t -> p (n t)")
                    for d in range(2):
                        dve.wait_ge(*PO.before("kfb", i))
                        nc.vector.tensor_scalar(kd[:, d, :], rate[:, d, :], pcol("k_a"), pcol("om_ka"), ALU.mult,
                                                ALU.add).then_inc(*DV.did(f"kdf{d}"))
                        dve.wait_ge(*DV.by(f"kdf{d}", i))
                        nc.vector.tensor_tensor(kd[:, d, :], kd[:, d, :], k_s, ALU.mult).then_inc(*DV.did(f"kd{d}"))
                        dve.wait_ge(*AC.by(f"neg{d}", i))
                        nc.vector.tensor_tensor(KR[:, d, :, 0, :], KR[:, d, :, 0, :],
                                                kk.rearrange("p (n t) -> p n t", t=P), ALU.mult).then_inc(*DV.did(f"KK{d}"))
                        dve.wait_ge(*DV.by(f"kd{d}", i))
                        nc.vector.tensor_tensor(flat(Kh[:, d, :, :]), kd[:, d, :], flat(e_ng[:, d, :, :]),
                                                ALU.mult).then_inc(*DV.did(f"Kh{d}"))
                        dve.wait_ge(*PO.by(f"aa{d}", i))
                        nc.vector.tensor_tensor(flat(Ah[:, d, :, :]), rate[:, d, :], flat(e_ng[:, d, :, :]),
                                                ALU.mult).then_inc(*DV.did(f"Ah{d}"))
                    nc.vector.tensor_tensor(em[:, 0, :], e_in[:, 0, 0:3, P - 1], e_in[:, 0, 1:4, P - 1],
                                            ALU.mult).then_inc(*DV.did("em0"))
                    nc.vector.tensor_tensor(em[:, 1, 0:3:2], e_in[:, 1, 1:4:2, 0], e_in[:, 1, 0:3:2, 0],
                                            ALU.mult).then_inc(*DV.did("em1"))
                    nc.vector.tensor_tensor(em[:, 1, 1:2], e_in[:, 1, 0, 0:1], e_in[:, 1, 3, 0:1],
                                            ALU.mult).then_inc(*DV.did("em2"))
                    dve.wait_ge(*PO.by("rkk", i))
                    nc.vector.tensor_scalar(bonus[:, :], bonus[:, :], pcol("r_k"), None, ALU.mult).then_inc(*DV.did("rk"))
                    dve.wait_ge(*PE.by("bonus", i))
                    nc.vector.tensor_tensor(bonus[:, :], ps[:, 7, 0:SEQ], v_s[:, SEQ:TOK],
                                            ALU.mult).then_inc(*DV.did("bv"))
                    for q, (d, h) in enumerate(QS):
                        dve.wait_ge(*PE.by(f"g{q}c", i))
                        nc.vector.tensor_tensor(Gc[:, q, :, :, :].rearrange("p n e t -> p (n e) t"),
                                                ps[:, (3 * q) % 4, :].rearrange("p (n t) -> p n t", t=P),
                                                below[:, d, 0:1, :].broadcast_to([P, 4, P]), ALU.mult).then_inc(*DV.did(f"g{q}c"))
                        for n, x in ((0, "x"), (1, "z")):
                            dve.wait_ge(*PE.by(f"g{q}{x}", i))
                            nc.vector.tensor_tensor(Gx[:, q, n, :, :].rearrange("p (k e) t -> p k e t", e=2),
                                                    ps[:, (3 * q + 1 + n) % 4, :].rearrange("p (k e t) -> p k e t", k=2, e=2),
                                                    below[:, d, :, :].unsqueeze(1).broadcast_to([P, 2, 2, P]),
                                                    ALU.mult).then_inc(*DV.did(f"g{q}{x}"))
                    if last_turn:
                        DV.skip("pn")
                    else:
                        dve.wait_ge(*AC.before("keep1", i))
                        nc.vector.tensor_copy(pn[:, :], shifts[:, ds(i + 1, 1), :].rearrange("p a n -> p (a n)")).then_inc(*DV.did("pn"))
                    four = lambda m: m.unsqueeze(1).broadcast_to([P, NT, P])
                    line = lambda m, q: m[:, q, :, :].rearrange("p n t -> p (n t)")
                    for q in range(4):
                        dve.wait_ge(*PO.by(f"i2{q}x", i))
                        nc.vector.transpose(line(X, q), line(XT, q)).then_inc(*DV.did(f"x1_{q}"))
                    for lev in LEVELS:
                        for q in range(4):
                            dve.wait_ge(*PE.by(f"E{lev}_{q}", i))
                            nc.vector.scalar_tensor_tensor(F[:, q, :, :], ps[:, q, :].rearrange("p (n t) -> p n t", t=P), -1.0,
                                                           four(ident2[:, :]), ALU.mult, ALU.add).then_inc(*DV.did(f"F{lev}_{q}"))
                        for q in range(4):
                            dve.wait_ge(*PE.by(f"X{lev}_{q}", i))
                            nc.vector.tensor_tensor(X[:, q, :, :], ps[:, q, :].rearrange("p (n t) -> p n t", t=P),
                                                    four(blocks[:, lev, :]), ALU.mult).then_inc(*DV.did(f"X{lev}_{q}"))
                            if lev < 5:
                                dve.wait_ge(*DV.by(f"X{lev}_{q}", i))
                                nc.vector.transpose(line(XT, q), line(X, q)).then_inc(*DV.did(f"T{lev}_{q}"))
                        if lev in (1, 4):
                            n = {1: 2, 4: 0}[lev]
                            if last_turn:
                                DV.skip(f"near{n}", f"shift{n}")
                            else:
                                shift(n, AC.by(f"pad{n}", i), AC.by(f"keep{n}", i), DV.did(f"near{n}"), DV.by(f"near{n}", i),
                                      DV.did(f"shift{n}"))
                    for j in range(3):
                        dve.wait_ge(*PE.by(f"s{j}", i))
                        for d in range(2):
                            nc.vector.tensor_scalar(S[:, d, :], ps[:, 7, d * HEAD:(d + 1) * HEAD], em[:, d, j:j + 1], None,
                                                    ALU.mult).then_inc(*DV.did(f"s{j}_{d}"))
                    dve.wait_ge(*AC.by("yf", i))
                    nc.vector.tensor_tensor(y, y, ps[:, 3, SEQ:TOK], ALU.add).then_inc(*DV.did("y"))
                    dve.wait_ge(*DV.by("y", i))
                    dve.wait_ge(*PE.by("mean", i))
                    nc.vector.tensor_tensor(yc, y, ps[:, 6, 0:SEQ], ALU.subtract).then_inc(*DV.did("yc"))
                    if last_turn:
                        DV.skip("near1", "shift1")
                    else:
                        shift(1, AC.by("pad1", i), AC.by("keep1", i), DV.did("near1"), DV.by("near1", i), DV.did("shift1"))
                    dve.wait_ge(*AC.by("std", i))
                    nc.vector.reciprocal(rs, rs).then_inc(*DV.did("rec"))
                    dve.wait_ge(*DV.by("rec", i))
                    nc.vector.tensor_tensor(yc, yc, rs, ALU.mult).then_inc(*DV.did("yn"))
                    dve.wait_ge(*DV.by("yn", i))
                    nc.vector.tensor_scalar(yc, yc, pcol("ln_w"), pcol("ln_b"), ALU.mult, ALU.add).then_inc(*DV.did("yl"))
                    dve.wait_ge(*DV.by("yl", i))
                    nc.vector.tensor_tensor(yc, yc, bonus[:, :], ALU.add).then_inc(*DV.did("yb"))
                    dve.wait_ge(*DV.by("yb", i))
                    dst = yaT[:, PAIRS - 1, :] if last_turn else yaT[:, ds(i, 1), :].rearrange("p a t -> p (a t)")
                    nc.vector.tensor_tensor(dst, yc, gate[:, :], ALU.mult).then_inc(*DV.did("out"))

                turns(dve, DV, turn)

            @block.tensor
            def _(pe):
                PE.open(pe)
                mm = nc.tensor.matmul

                def decay_logit(d, bank, mark):
                    for n in range(NT):
                        last = mm(ps[:, bank, n * P:(n + 1) * P], tanh_w[:, d, n * P:(n + 1) * P], lw2[:, d, :],
                                  start=True, stop=True)
                    last.then_inc(*mark)

                def rate_logit(d, bank, mark):
                    mm(ps[:, bank, :], la2[:, d, :], low_a[:, d, :], start=True, stop=True).then_inc(*mark)

                def project(n, k0, k1):
                    t0 = SEQ if n == 2 else 0
                    for k in range(k0, k1):
                        last = mm(ps[:, 4 + n, t0:TOK], w[:, n, k, :], hT[:, k, t0:TOK], start=(k == 0), stop=(k == KC - 1))
                    return last

                pe.wait_ge(lw_sem, 48)
                for d in range(2):
                    decay_logit(d, d, (first_pe, 1))
                for d in range(2):
                    rate_logit(d, 2 + d, (first_pe, 1))
                for n in range(3):
                    pe.wait_ge(w_sem[n], 16)
                    project(n, 0, KC).then_inc(first_pe, 1)
                pe.wait_ge(first_act, 10)
                pe.wait_ge(first_dve, 7)

                def turn(i, last_turn):
                    nxt = not last_turn
                    for d in range(2):
                        pe.wait_ge(*AC.before("rate1", i))
                        pe.wait_ge(*(AC.before("yf", i) if d == 0 else DV.before("y", i)))
                        for n in range(NT):
                            last = mm(ps[:, 2 * d + n // 2, (n % 2) * 2 * P:(n % 2 + 1) * 2 * P], sg[:, d, n, :],
                                      tri[:, d, :, :].rearrange("p e t -> p (e t)"), start=True, stop=True)
                        last.then_inc(*PE.did(f"cs{d}"))
                    if nxt:
                        pe.wait_ge(*DV.before("yc", i))
                        pe.wait_ge(w_sem[2], i * 16 + 32)
                        project(2, 0, 8)
                    pe.wait_ge(*AC.by("sq", i))
                    mm(ps[:, 7, :], head_ones[:, :], sq[:, :], start=True, stop=True).then_inc(*PE.did("kss"))
                    if last_turn:
                        pe.wait_ge(lg_sem, 16 * PAIRS)
                    else:
                        pe.wait_ge(lg_sem, i * 16 + 16)
                    for k in range(2):
                        last = mm(ps[:, 4, 0:SEQ], lg2[:, k, :], gate_g[:, k, :], start=(k == 0), stop=(k == 1))
                    last.then_inc(*PE.did("gate"))

                    def turned(name, bank, src, after):
                        pe.wait_ge(*after)
                        for n in range(NT):
                            last = nc.tensor.transpose(ps[:, bank, n * P:(n + 1) * P], src[:, n * P:(n + 1) * P], ident[:, :])
                        last.then_inc(*PE.did(name))

                    flat = lambda m: m.rearrange("p n t -> p (n t)")
                    pe.wait_ge(*AC.by("neg1", i))
                    turned("vt", 5, v_s, DV.before("shift1", i))
                    if nxt:
                        project(2, 8, KC).then_inc(*PE.did("r"))
                        pe.wait_ge(*AC.by("gate", i))
                        pe.wait_ge(w_sem[0], i * 16 + 32)
                        project(0, 0, K_SHARES[0])
                    else:
                        PE.skip("r")
                    turned("kt0", 0, flat(Kh[:, 0, :, :]), DV.by("Kh0", i))
                    turned("at0", 1, flat(Ah[:, 0, :, :]), DV.by("Ah0", i))
                    turned("kt1", 2, flat(Kh[:, 1, :, :]), DV.by("Kh1", i))
                    turned("at1", 3, flat(Ah[:, 1, :, :]), DV.by("Ah1", i))
                    pe.wait_ge(*DV.by("rk", i))
                    mm(ps[:, 7, 0:SEQ], head_ones[:, :], bonus[:, :], start=True, stop=True).then_inc(*PE.did("bonus"))
                    pe.wait_ge(*PO.by("rr1", i))
                    for q, (d, h) in enumerate(QS):
                        hs = head(h)
                        ring = lambda n: (3 * q + n) % 4

                        def bank_free(n):
                            c = 3 * q + n - 4
                            if c >= 0:
                                pe.wait_ge(*DV.by(f"g{c // 3}{'cxz'[c % 3]}", i))
                            else:
                                pe.wait_ge(*AC.by(("kt0", "at0", "kt1", "at1")[ring(n)], i))
                        bank_free(0)
                        for n in range(2):
                            for e, src in enumerate((Ah, Kh)):
                                c = (2 * n + e) * P
                                last = mm(ps[:, ring(0), c:c + P], src[hs, d, n, :], KR[hs, d, n, 0, :], start=True, stop=True)
                        last.then_inc(*PE.did(f"g{q}c"))
                        for n in range(2):
                            bank_free(1 + n)
                            for e, src in enumerate((Ah, Kh)):
                                last = mm(ps[:, ring(1 + n), e * 2 * P:(e + 1) * 2 * P], src[hs, d, 2 + n, :],
                                          KR[hs, d, 2 + n, :, :].rearrange("p e t -> p (e t)"), start=True, stop=True)
                            last.then_inc(*PE.did(f"g{q}{'xz'[n]}"))
                    def share(lev, half):
                        if nxt:
                            at = 2 * lev - 2 + half
                            if at == 6:
                                pe.wait_ge(w_sem[1], i * 16 + 32)
                            k0, k1 = K_SHARES[at:at + 2] if at < 6 else (2 * at - 12, 2 * at - 10)
                            last = project(int(at >= 6), k0, k1)
                            if at == 5:
                                last.then_inc(*PE.did("k"))
                        elif (lev, half) == (3, 1):
                            PE.skip("k")

                    v_done = [8]

                    def some_v():
                        if nxt:
                            v_done[0] += 1
                            return project(1, v_done[0] - 1, v_done[0])

                    for lev in LEVELS:
                        for q in range(4):
                            if lev == 1:
                                pe.wait_ge(*DV.by(f"x1_{q}", i))
                                pe.wait_ge(*PO.by(f"at{q}x", i))
                            else:
                                pe.wait_ge(*DV.by(f"T{lev - 1}_{q}", i))
                            for n in range(NT):
                                last = mm(ps[:, q, n * P:(n + 1) * P], A_T(q, n), X[:, q, n, :], start=True, stop=True)
                            last.then_inc(*PE.did(f"E{lev}_{q}"))
                        share(lev, 0)
                        for q in range(4):
                            pe.wait_ge(*DV.by(f"F{lev}_{q}", i))
                            for n in range(NT):
                                last = mm(ps[:, q, n * P:(n + 1) * P], XT[:, q, n, :], F[:, q, n, :], start=True, stop=True)
                            last.then_inc(*PE.did(f"X{lev}_{q}"))
                        share(lev, 1)
                    for q in range(4):
                        pe.wait_ge(*DV.by(f"X5_{q}", i))
                        for n in range(NT):
                            last = nc.tensor.transpose(ps[:, q, n * P:(n + 1) * P], X[:, q, n, :], ident[:, :])
                        last.then_inc(*PE.did(f"T5_{q}"))
                    units = [(q, n) for q in range(2) for n in range(NT)]
                    for d in range(2):
                        wait_alone(pe, passed_pe, *AC.by(f"T5_{2 * d + 1}", i))
                        for u, (q, n) in enumerate(units):
                            last = mm(ps[late_half[d], d, u * 64:(u + 1) * 64], A_T(2 * d + q, n)[early_half[d], late_half[d]],
                                      X[early_half[d], 2 * d + q, n, early_half[d]], start=True, stop=True)
                        last.then_inc(*PE.did(f"P6_{d}"))
                    for d in range(2):
                        wait_alone(pe, passed_pe, *AC.by("T5_3", i))
                        wait_alone(pe, passed_pe, *AC.by(f"P6_{d}", i))
                        for u, (q, n) in enumerate(units):
                            last = mm(ps[early_half[d], 2 + d, u * 64:(u + 1) * 64], low[late_half[d], u * 64:(u + 1) * 64],
                                      XT[late_half[d], 2 * d + q, n, late_half[d]], start=True, stop=True)
                        last.then_inc(*PE.did(f"Q6_{d}"))
                    pe.wait_ge(*AC.by("P6_1", i))
                    if nxt:
                        pe.wait_ge(lw_sem, i * 48 + 96)
                        pe.wait_ge(*AC.by("keep0", i))
                    for j in range(4):
                        if j:
                            pe.wait_ge(*DV.by(f"s{j - 1}_1", i))
                        for q, (d, h) in enumerate(QS):
                            n, hs = order[d][j], head(h)
                            if j:
                                mm(ps[:, h, d * HEAD:(d + 1) * HEAD], KR[hs, d, n, 0, :], S[hs, d, :], start=True, stop=False)
                            last = mm(ps[:, h, d * HEAD:(d + 1) * HEAD], B1(q, n), Vt[:, n, hs], start=(j == 0), stop=True)
                        last.then_inc(*PE.did(f"rhs{j}"))
                        if j >= 2:
                            some_v()
                        if j < 2:
                            if last_turn:
                                PE.skip(("u0", "a0")[j])
                            elif j == 0:
                                decay_logit(0, 4, PE.did("u0"))
                            else:
                                pe.wait_ge(*AC.by("sg0", i))
                                rate_logit(0, 4, PE.did("a0"))
                        pe.wait_ge(*AC.by("Q6_1", i))
                        pe.wait_ge(*AC.by(f"rhs{j}", i))
                        for q, (d, h) in enumerate(QS):
                            last = mm(ps[:, 2, q * HEAD:(q + 1) * HEAD], XT[:, q, order[d][j], :], rhs[:, q, :], start=True, stop=True)
                        last.then_inc(*PE.did(f"sa{j}"))
                        if j >= 2:
                            some_v()
                        if j < 2:
                            if last_turn:
                                PE.skip(("u1", "a1")[j])
                            elif j == 0:
                                decay_logit(1, 6, PE.did("u1"))
                            else:
                                pe.wait_ge(*AC.by("sg1", i))
                                rate_logit(1, 6, PE.did("a1"))
                        pe.wait_ge(*AC.by(f"sa{j}", i))
                        if j >= 2:
                            for q, (d, h) in enumerate(QS):
                                n, hs = order[d][j], head(h)
                                c = d * SEQ + (n - 2) * P
                                mm(ps[hs, 3, c:c + P], Vt[:, n, hs], Gx[:, q, n - 2, 3, :], start=True, stop=False)
                                mm(ps[hs, 3, c:c + P], S[hs, d, :], KR[hs, d, n, 1, :], start=False, stop=False)
                                last = mm(ps[hs, 3, c:c + P], nsa[:, q, :], Gx[:, q, n - 2, 1, :], start=False, stop=True)
                            last.then_inc(*PE.did(f"y{j}"))
                        if j < 3:
                            for q, (d, h) in enumerate(QS):
                                n, hs = order[d][j], head(h)
                                o = ps[hs, 7, d * HEAD:(d + 1) * HEAD]
                                mm(o, Kt[:, d, n, hs], Vt[:, n, hs], start=True, stop=False)
                                if j:
                                    mm(o, ident[hs, hs], S[hs, d, :], start=False, stop=False)
                                last = mm(o, At[:, d, n, hs], nsa[:, q, :], start=False, stop=True)
                            last.then_inc(*PE.did(f"s{j}"))
                            some_v()
                    if nxt:
                        some_v().then_inc(*PE.did("v"))
                        assert v_done[0] == KC
                        pe.wait_ge(*AC.by("rate1", i))
                    else:
                        PE.skip("v")
                    pe.wait_ge(*DV.by("y", i))
                    mm(ps[:, 6, 0:SEQ], head_mean[:, :], y, start=True, stop=True).then_inc(*PE.did("mean"))
                    pe.wait_ge(*AC.by("ysq", i))
                    mm(ps[:, 7, 0:SEQ], head_mean[:, :], ysq, start=True, stop=True).then_inc(*PE.did("var"))

                turns(pe, PE, turn)


MASKS = [0]


def ssd(nc, sb, sem, ps, a, ident, ones, below, par, col, SKIP_D, silu_c, modT, hT, ybT):
    with ExitStack() as stage:
        def t(name, *shape):
            return sb(name, list(shape), ctx=stage)

        w_dt, by_head, by_head_done = t("w_dt", P, KC, 2 * SH), t("dt_by_head", 2 * SH, TOK), sem("dt_by_head_done")
        dt_bias, a_exp = t("dt_bias", P, 2 * SH), t("a_exp", P, 2 * SH)
        raw, lin, soft = t("dt_raw", P, NT, 2 * SH), t("dt_lin", P, NT, 2 * SH), t("dt_soft", P, NT, 2 * SH)
        heads = t("heads", P, 5, NT, 2 * SH)
        LOGA, CUM, STEP, END, WHOLE = range(5)
        per_group = t("per_group", P, GROUPS, 28)
        w_sem, rows_sem, proj, sums, dv, ac = (sem(x) for x in ("dt_w", "dt_rows", "dt_proj", "dt_sums", "dt_dve", "dt_act"))
        w_in = a["w_in"].rearrange("l (k p) n -> (l p) k n", p=P)
        in_columns = lambda m: m.rearrange("p (r w) -> p w r", r=GRID_R)
        with nc.Block() as block:

            @block.sync
            def _(sp):
                sp.dma_start(w_dt[:, :, :], w_in[:, :, DT0:GA0]).then_inc(w_sem, 16)
                sp.dma_start(dt_bias[:, :], a["ssm_dt_bias"].rearrange("l d h -> l (d h)").broadcast_to([P, 2 * SH])).then_inc(rows_sem, 16)
                sp.dma_start(a_exp[:, :], a["ssm_a_log"].rearrange("l d h -> l (d h)").broadcast_to([P, 2 * SH])).then_inc(rows_sem, 16)

            @block.tensor
            def _(pe):
                pe.wait_ge(w_sem, 16)
                for k in range(KC):
                    last = nc.tensor.matmul(ps[0:2 * SH, 4, :], w_dt[:, k, :], hT[:, k, :], start=(k == 0), stop=(k == KC - 1))
                last.then_inc(proj, 1)
                pe.wait_ge(by_head_done, 2)
                for n in range(NT):
                    last = nc.tensor.transpose(ps[:, 0, n * 2 * SH:(n + 1) * 2 * SH], by_head[:, n * P:(n + 1) * P],
                                               ident[0:2 * SH, 0:2 * SH])
                last.then_inc(proj, 1)
                pe.wait_ge(dv, 4 + 1)
                for d in range(2):
                    x = heads[:, LOGA, :, d * SH:(d + 1) * SH]
                    nc.tensor.matmul(ps[:, 1 + d, 0:P], below[:, 1 - d, 0, :], x, start=True, stop=True)
                    nc.tensor.matmul(ps[:, 1 + d, P:2 * P], below[:, d, 1, :], x, start=True, stop=True)
                    last = nc.tensor.matmul(ps[:, 1 + d, 2 * P:3 * P], ones[:, :], x, start=True, stop=True)
                last.then_inc(sums, 1)

            @block.scalar
            def _(act):
                act.wait_ge(proj, 1)
                nc.scalar.activation(by_head[:, 0:SEQ], ps[0:2 * SH, 4, 0:SEQ], ACT.Copy).then_inc(by_head_done, 1)
                nc.scalar.activation(by_head[:, SEQ:TOK].rearrange("p (w r) -> p w r", r=GRID_R),
                                     in_columns(ps[0:2 * SH, 4, SEQ:TOK]), ACT.Copy).then_inc(by_head_done, 1)
                act.wait_ge(rows_sem, 32)
                nc.scalar.activation(a_exp[:, :], a_exp[:, :], ACT.Exp).then_inc(ac, 1)
                act.wait_ge(dv, 1)
                nc.scalar.activation(soft[:, :, :], raw[:, :, :], ACT.Abs).then_inc(ac, 1)
                act.wait_ge(ac, 2)
                nc.scalar.activation(soft[:, :, :], soft[:, :, :], ACT.Exp, scale=-1.0).then_inc(ac, 1)
                act.wait_ge(ac, 3)
                nc.scalar.activation(soft[:, :, :], soft[:, :, :], ACT.Ln, bias=1.0).then_inc(ac, 1)
                act.wait_ge(sums, 1)
                for d in range(2):
                    for at, dst in ((0, END), (2 * P, WHOLE)):
                        nc.scalar.activation(heads[:, dst, :, d * SH:(d + 1) * SH],
                                             ps[:, 1 + d, at:at + P].rearrange("p (n h) -> p n h", h=SH), ACT.Exp).then_inc(ac, 1)

            @block.vector
            def _(dve):
                dve.wait_ge(proj, 2)
                dve.wait_ge(rows_sem, 32)
                nc.vector.tensor_tensor(raw[:, :, :], ps[:, 0, 0:NT * 2 * SH].rearrange("p (n h) -> p n h", h=2 * SH),
                                        dt_bias[:, :].unsqueeze(1).broadcast_to([P, NT, 2 * SH]), ALU.add).then_inc(dv, 1)
                dve.wait_ge(dv, 1)
                nc.vector.tensor_scalar(lin[:, :, :], raw[:, :, :], 0.0, None, ALU.max).then_inc(dv, 1)
                dve.wait_ge(dv, 2)
                dve.wait_ge(ac, 4)
                nc.vector.tensor_tensor(heads[:, STEP, :, :], lin[:, :, :], soft[:, :, :], ALU.add).then_inc(dv, 1)
                nc.vector.tensor_scalar(a_exp[:, :], a_exp[:, :], -1.0, None, ALU.mult).then_inc(dv, 1)
                dve.wait_ge(dv, 4)
                nc.vector.tensor_tensor(heads[:, LOGA, :, :], heads[:, STEP, :, :],
                                        a_exp[:, :].unsqueeze(1).broadcast_to([P, NT, 2 * SH]), ALU.mult).then_inc(dv, 1)
                cw, cb = col["conv_w"], col["conv_b"]
                XB = (D + 2 * GROUPS * STATE) // P
                for tap in range(CONV + 1):
                    c0 = cw + tap * XB if tap < CONV else cb
                    nc.vector.tensor_copy(per_group[:, :, 4 * tap:4 * tap + 2],
                                          par[:, c0:c0 + KC].rearrange("p (g e) -> p g e", e=2))
                    nc.vector.tensor_copy(per_group[:, :, 4 * tap + 2], par[:, c0 + KC:c0 + KC + GROUPS])
                    nc.vector.tensor_copy(per_group[:, :, 4 * tap + 3], par[:, c0 + KC + GROUPS:c0 + KC + 2 * GROUPS])
                for at, c0 in ((24, col["ssm_norm_w"]), (26, SKIP_D)):
                    nc.vector.tensor_copy(per_group[:, :, at:at + 2], par[:, c0:c0 + KC].rearrange("p (g e) -> p g e", e=2))
                dve.wait_ge(ac, 8)
                for d in range(2):
                    nc.vector.tensor_copy(heads[:, CUM, :, d * SH:(d + 1) * SH],
                                          ps[:, 1 + d, P:2 * P].rearrange("p (n h) -> p n h", h=SH))
                nc.vector.tensor_tensor(heads[:, END, :, :], heads[:, END, :, :], heads[:, STEP, :, :], ALU.mult).then_inc(dv, 1)

        w = t("w_group", P, 4, KC, P)
        wz = t("w_z", P, KC, GW)
        pg, hd = t("pg", P, 28), t("hd", P, 5, NT, 2, 4)
        pad = t("xbc_pad", P, 4, 2, SEQ + 4)
        cv = t("xbc_conv", P, 4, TOK)
        xt, bt = t("xt", P, NT, GW), t("bt", P, NT, STATE)
        cbm = t("cbm", P, 2, 2, P)
        seg = t("seg", P, 2, 4, 2, P)
        ecs = t("ecs", P, 2, 2, 2, P)
        xw = t("xw", P, 2, 3, 4, HEAD)
        H = t("H", P, 2, 3, 4, HEAD)
        sz = t("sz", P, 2, SEQ)
        y, ysq, inv = t("ys", P, 2, SEQ), t("ysq", P, 2, SEQ), t("inv", P, SEQ)
        eps_col = t("eps_col", P, 1)
        w_mod = a["w_mod"].rearrange("l (k p) n -> (l p) k n", p=P)
        wm = t("w_mod_piece", P, 2, 2, 512)
        by_row = t("mod_by_row", P, 2, 512)
        MOD0, MOD_PER = 2 * KC, 4 * KC // GROUPS
        PIECES = MOD_PER // 4 * KC // 2
        order = [(0, 1, 2, 3), (1, 0, 3, 2)]
        NS = [("%d_%d" % (j, d), j, d) for j in range(3) for d in range(2)]
        PE = Steps(sem("ss_pe"), "x0 x1 B C tx0 tx1 tB z cb cr0 cr1 cr2 cr3 ec0 ec1 " + " ".join("st" + s for s, _, _ in NS)
                   + " yd off0 off1 nrm mod", True)
        AC = Steps(sem("ss_act"), "p0 p1 s0 p2 s1 p3 s2 tx0 tx1 s3 z tB e0 e1 e2 e3 ec0 ec1 sq std", True)
        DV = Steps(sem("ss_dve"), "pg hd " + " ".join(
            [x for n in range(4) for x in [f"c{n}_{k}" for k in range(CONV)] + [f"m{m}" for m in range(n * 8, n * 8 + 8)]])
                   + " cbm seg0 seg1 seg2 seg3 w0 w1 w2 w3 " + " ".join(
                       (f"hm{s} " if j else "") + f"h{s}" for s, j, d in NS)
                   + " y off0 off1 y0 y1 gate rec out mod", True)
        PO = Steps(sem("ss_pool"), "xw w", True)
        mod_in = [sem("ss_w_mod0"), sem("ss_w_mod1")]
        loads, zloads, consts = sem("ss_w"), sem("ss_wz"), sem("ss_consts")
        with nc.Block() as block:

            @block.sync
            def _(sp):
                with sp.Fori(0, GROUPS) as i:
                    sp.wait_ge(*PE.before("C", i))
                    sp.dma_start(w[:, 0, :, :], w_in[:, :, ds(i * GW + X0, P)]).then_inc(loads, 16)
                    sp.dma_start(w[:, 1, :, :], w_in[:, :, ds(i * GW + X0 + P, P)]).then_inc(loads, 16)
                    sp.dma_start(w[:, 2, :, :], w_in[:, :, ds(i * STATE + B0, STATE)]).then_inc(loads, 16)
                    sp.dma_start(w[:, 3, :, :], w_in[:, :, ds(i * STATE + C0, STATE)]).then_inc(loads, 16)
                    sp.wait_ge(*PE.before("z", i))
                    sp.dma_start(wz[:, :, :], w_in[:, :, ds(i * GW + Z0, GW)]).then_inc(zloads, 16)
                    for m in range(PIECES):
                        sp.wait_ge(*(DV.by(f"m{2 * m - 3}", i) if m >= 2 else DV.before(f"m{2 * (PIECES + m) - 3}", i)))
                        b, k = divmod(2 * m, KC)
                        sp.dma_start(wm[:, m % 2, :, :], w_mod[:, k:k + 2, ds(i * (MOD_PER * P) + (MOD0 * P + b * 512), 512)]
                                     ).then_inc(mod_in[m % 2], 16)

            @block.gpsimd
            def _(pool):
                PO.open(pool)
                nc.gpsimd.memset(pad[:, :, :, :], 0.0).then_inc(consts, 1)
                nc.gpsimd.memset(eps_col[:, :], EPS).then_inc(consts, 1)
                with pool.Fori(0, GROUPS) as i:
                    pool.wait_ge(*AC.by("tx1", i))
                    pool.wait_ge(*DV.by("hd", i))
                    pool.wait_ge(*PE.before("off1", i))
                    for d in range(2):
                        for j in range(3):
                            n = order[d][j]
                            last = nc.gpsimd.tensor_tensor(xw[:, d, j, :, :], xt[:, n, :].rearrange("p (e c) -> p e c", c=HEAD),
                                                           hd[:, END, n, d, :].unsqueeze(2).broadcast_to([P, 4, HEAD]), ALU.mult)
                    last.then_inc(*PO.did("xw"))
                    pool.wait_ge(*DV.by("w3", i))
                    f = lambda m: m.rearrange("p e c t -> p (e c t)")
                    nc.gpsimd.tensor_tensor(f(seg[:, 0, :, :, :]), f(seg[:, 0, :, :, :]), f(seg[:, 1, :, :, :]),
                                            ALU.add).then_inc(*PO.did("w"))
                PO.end()

            @block.scalar
            def _(act):
                AC.open(act)
                act.wait_ge(consts, 2)
                with act.Fori(0, GROUPS) as i:
                    def silu(n):
                        t0 = SEQ if n == 3 else 0
                        act.wait_ge(*DV.by(f"c{n}_4", i))
                        nc.scalar.activation(cv[:, n, t0:TOK], cv[:, n, t0:TOK], ACT.Silu).then_inc(*AC.did(f"s{n}"))

                    for n in range(4):
                        act.wait_ge(*PE.by(("x0", "x1", "B", "C")[n], i))
                        act.wait_ge(*DV.before(f"c{n}_4", i))
                        if n < 3:
                            nc.scalar.activation(pad[:, n, 0, 2:SEQ + 2], ps[:, n, 0:SEQ], ACT.Copy)
                        nc.scalar.activation(pad[:, n, 1, 2:SEQ + 2].rearrange("p (w r) -> p w r", r=GRID_R),
                                             in_columns(ps[:, n, SEQ:TOK]), ACT.Copy).then_inc(*AC.did(f"p{n}"))
                        if n:
                            silu(n - 1)
                    for e in range(2):
                        act.wait_ge(*PE.by(f"tx{e}", i))
                        act.wait_ge(*PO.before("xw", i))
                        nc.scalar.activation(xt[:, :, e * P:(e + 1) * P], ps[:, 5 + e, :].rearrange("p (n c) -> p n c", c=P),
                                             ACT.Copy).then_inc(*AC.did(f"tx{e}"))
                    silu(3)
                    act.wait_ge(*PE.by("z", i))
                    act.wait_ge(*DV.before("out", i))
                    nc.scalar.activation(sz[:, :, :], ps[:, 4, :].rearrange("p (e t) -> p e t", e=2), ACT.Silu).then_inc(*AC.did("z"))
                    act.wait_ge(*PE.by("tB", i))
                    nc.scalar.activation(bt[:, :, :], ps[:, 7, :].rearrange("p (n c) -> p n c", c=P), ACT.Copy).then_inc(*AC.did("tB"))
                    for b in range(4):
                        d, e = divmod(b, 2)
                        act.wait_ge(*DV.by(f"seg{b}", i))
                        nc.scalar.activation(seg[:, d, 2 * e:2 * e + 2, :, :], seg[:, d, 2 * e:2 * e + 2, :, :],
                                             ACT.Exp).then_inc(*AC.did(f"e{b}"))
                    for d in range(2):
                        act.wait_ge(*PE.by(f"ec{d}", i))
                        act.wait_ge(*DV.before(f"off{d}", i))
                        nc.scalar.activation(ecs[:, d, :, :, :], ps[:, 5 + d, :].rearrange("p (e c t) -> p e c t", e=2, c=2),
                                             ACT.Exp).then_inc(*AC.did(f"ec{d}"))
                    act.wait_ge(*DV.by("gate", i))
                    nc.scalar.activation(ysq[:, :, :], sz[:, :, :], ACT.Square).then_inc(*AC.did("sq"))
                    act.wait_ge(*PE.by("nrm", i))
                    nc.scalar.activation(inv[:, :], ps[:, 4, 0:SEQ], ACT.Sqrt, scale=1.0 / GW, bias=eps_col[:, 0:1]).then_inc(*AC.did("std"))
                AC.end()

            @block.vector
            def _(dve):
                DV.open(dve)
                with dve.Fori(0, GROUPS) as i:
                    dve.wait_ge(*DV.before("out", i))
                    nc.vector.tensor_copy(pg[:, :], per_group[:, ds(i, 1), :].rearrange("p a n -> p (a n)")).then_inc(*DV.did("pg"))
                    dve.wait_ge(*PO.before("w", i))
                    dve.wait_ge(*PE.before("off1", i))
                    nc.vector.tensor_copy(hd[:, :, :, :, :].rearrange("p a n d e -> p (a n d) e"),
                                          heads[:, :, :, :].rearrange("p a n (d h) -> p (a n d) h", d=2)[:, :, ds(i * 4, 4)]
                                          ).then_inc(*DV.did("hd"))
                    dve.wait_ge(*DV.by("pg", i))
                    for n in range(4):
                        s0 = 1 if n == 3 else 0
                        dve.wait_ge(*AC.by(f"p{n}", i))
                        o = cv[:, n, s0 * SEQ:TOK].rearrange("p (s t) -> p s t", t=SEQ)
                        nc.vector.tensor_scalar(o, pad[:, n, s0:2, 0:SEQ], pg[:, n:n + 1], pg[:, 20 + n:21 + n], ALU.mult,
                                                ALU.add).then_inc(*DV.did(f"c{n}_0"))
                        for k in range(1, CONV):
                            dve.wait_ge(*DV.by(f"c{n}_{k - 1}", i))
                            nc.vector.scalar_tensor_tensor(o, pad[:, n, s0:2, k:k + SEQ], pg[:, 4 * k + n:4 * k + n + 1], o,
                                                           ALU.mult, ALU.add).then_inc(*DV.did(f"c{n}_{k}"))
                        for m in range(8 * n, 8 * n + 8):
                            b, k = divmod(m, KC)
                            piece, part = m // 2, wm[:, m // 2 % 2, m % 2, :]
                            if m % 2 == 0:
                                dve.wait_ge(mod_in[piece % 2], i * (8 * PIECES) + 16 * (piece // 2 + 1))
                            if k == 0:
                                nc.vector.tensor_scalar(by_row[:, b, :], part, silu_c[:, 0, 0:1], None, ALU.mult).then_inc(*DV.did(f"m{m}"))
                            else:
                                dve.wait_ge(*DV.by(f"m{m - 1}", i))
                                nc.vector.scalar_tensor_tensor(by_row[:, b, :], part, silu_c[:, k, 0:1], by_row[:, b, :],
                                                               ALU.mult, ALU.add).then_inc(*DV.did(f"m{m}"))
                    dve.wait_ge(*PE.by("cb", i))
                    for d in range(2):
                        last = nc.vector.tensor_tensor(cbm[:, d, :, :], ps[:, 0, 0:SEQ].rearrange("p (c t) -> p c t", c=2),
                                                       below[:, d, 1:2, :].broadcast_to([P, 2, P]), ALU.mult)
                    last.then_inc(*DV.did("cbm"))
                    for b in range(4):
                        d = b // 2
                        dve.wait_ge(*PE.by(f"cr{b}", i))
                        dve.wait_ge(*PE.before("yd", i))
                        for e in range(2):
                            for c in range(2):
                                last = nc.vector.tensor_scalar(seg[:, d, 2 * (b % 2) + e, c, :], ps[:, 1 + b, (2 * e + c) * P:(2 * e + c + 1) * P],
                                                               hd[:, CUM, 2 + c, d, 2 * (b % 2) + e:2 * (b % 2) + e + 1], 0.0,
                                                               ALU.subtract, ALU.min)
                        last.then_inc(*DV.did(f"seg{b}"))
                    dve.wait_ge(*DV.by("cbm", i))
                    for b in range(4):
                        d = b // 2
                        dve.wait_ge(*AC.by(f"e{b}", i))
                        for e in range(2 * (b % 2), 2 * (b % 2) + 2):
                            for c in range(2):
                                last = nc.vector.scalar_tensor_tensor(seg[:, d, e, c, :], seg[:, d, e, c, :],
                                                                      hd[:, STEP, 2 + c, d, e:e + 1], cbm[:, d, c, :],
                                                                      ALU.mult, ALU.mult)
                        last.then_inc(*DV.did(f"w{b}"))
                    for s, j, d in NS:
                        n = order[d][j]
                        st = ps[:, (7, 0)[d], 0:GW].rearrange("p (e c) -> p e c", c=HEAD)
                        dve.wait_ge(*PE.by("st" + s, i))
                        if j:
                            dve.wait_ge(*DV.by(f"h{j - 1}_{d}", i))
                            nc.vector.tensor_tensor(H[:, d, j, :, :], H[:, d, j - 1, :, :],
                                                    hd[:, WHOLE, n, d, :].unsqueeze(2).broadcast_to([P, 4, HEAD]),
                                                    ALU.mult).then_inc(*DV.did("hm" + s))
                            dve.wait_ge(*DV.by("hm" + s, i))
                            nc.vector.tensor_tensor(H[:, d, j, :, :], H[:, d, j, :, :], st, ALU.add).then_inc(*DV.did("h" + s))
                        else:
                            nc.vector.tensor_copy(H[:, d, 0, :, :], st).then_inc(*DV.did("h" + s))
                    dve.wait_ge(*PE.by("yd", i))
                    dve.wait_ge(*AC.by("s1", i))
                    for e in range(2):
                        last = nc.vector.scalar_tensor_tensor(y[:, e, :], cv[:, e, SEQ:TOK], pg[:, 26 + e:27 + e],
                                                              ps[:, 3, e * SEQ:(e + 1) * SEQ], ALU.mult, ALU.add)
                    last.then_inc(*DV.did("y"))
                    for d in range(2):
                        dve.wait_ge(*PE.by(f"off{d}", i))
                        dve.wait_ge(*AC.by(f"ec{d}", i))
                        f = lambda m: m.rearrange("p e c t -> p (e c t)")
                        nc.vector.tensor_tensor(f(ecs[:, d, :, :, :]), f(ecs[:, d, :, :, :]), ps[:, 1 + d, :], ALU.mult).then_inc(*DV.did(f"off{d}"))
                    for d in range(2):
                        dve.wait_ge(*(DV.by("off1", i) if d == 0 else DV.by("y0", i)))
                        nc.vector.tensor_tensor(y[:, :, :], y[:, :, :], ecs[:, d, :, :, :].rearrange("p e c t -> p e (c t)"),
                                                ALU.add).then_inc(*DV.did(f"y{d}"))
                    dve.wait_ge(*DV.by("y1", i))
                    dve.wait_ge(*AC.by("z", i))
                    for e in range(2):
                        last = nc.vector.tensor_tensor(sz[:, e, :].rearrange("p (r w) -> p r w", r=GRID_R),
                                                       y[:, e, :].rearrange("p (w r) -> p r w", r=GRID_R),
                                                       sz[:, e, :].rearrange("p (r w) -> p r w", r=GRID_R), ALU.mult)
                    last.then_inc(*DV.did("gate"))
                    dve.wait_ge(*AC.by("std", i))
                    nc.vector.reciprocal(inv[:, :], inv[:, :]).then_inc(*DV.did("rec"))
                    dve.wait_ge(*DV.by("rec", i))
                    for e in range(2):
                        last = nc.vector.scalar_tensor_tensor(ybT[:, ds(i * 2 + e, 1), :].rearrange("p a t -> p (a t)"), sz[:, e, :],
                                                              pg[:, 24 + e:25 + e], inv[:, :], ALU.mult, ALU.mult)
                    last.then_inc(*DV.did("out"))
                    dve.wait_ge(*PE.by("mod", i))
                    nc.vector.tensor_tensor(modT[:, ds(i * MOD_PER + MOD0, MOD_PER), 0], ps[:, 7, 0:MOD_PER],
                                            par[:, ds(i * MOD_PER + (col["b_mod"] + MOD0), MOD_PER)], ALU.add).then_inc(*DV.did("mod"))
                DV.end()

            @block.tensor
            def _(pe):
                PE.open(pe)
                mm = nc.tensor.matmul
                with pe.Fori(0, GROUPS) as i:
                    pe.wait_ge(loads, i * 64 + 64)
                    pe.wait_ge(*DV.before("off1", i))
                    pe.wait_ge(*AC.before("std", i))
                    for n in range(4):
                        t0 = SEQ if n == 3 else 0
                        for k in range(KC):
                            last = mm(ps[:, n, t0:TOK], w[:, n, k, :], hT[:, k, t0:TOK], start=(k == 0), stop=(k == KC - 1))
                        last.then_inc(*PE.did(("x0", "x1", "B", "C")[n]))
                    def z_part(e):
                        for k in range(KC):
                            last = mm(ps[:, 4, e * SEQ:(e + 1) * SEQ], wz[:, k, e * P:(e + 1) * P], hT[:, k, SEQ:TOK],
                                      start=(k == 0), stop=(k == KC - 1))
                        return last

                    pe.wait_ge(zloads, i * 16 + 16)
                    for m, name in enumerate(("tx0", "tx1", "tB")):
                        if name == "tB":
                            z_part(0)
                            pe.wait_ge(*DV.before("mod", i))
                        pe.wait_ge(*AC.by(f"s{m}", i))
                        for n in range(NT):
                            last = nc.tensor.transpose(ps[:, 5 + m, n * P:(n + 1) * P], cv[:, m, n * P:(n + 1) * P], ident[:, :])
                        last.then_inc(*PE.did(name))
                    z_part(1).then_inc(*PE.did("z"))
                    pe.wait_ge(*AC.by("s3", i))
                    for c in range(2):
                        x = slice(SEQ + c * P, SEQ + (c + 1) * P)
                        last = mm(ps[:, 0, c * P:(c + 1) * P], cv[:, 2, x], cv[:, 3, x], start=True, stop=True)
                    last.then_inc(*PE.did("cb"))
                    for b in range(4):
                        d = b // 2
                        if b == 3:
                            pe.wait_ge(*AC.by("z", i))
                        for e in range(2):
                            for c in range(2):
                                at = (2 * e + c) * P
                                last = mm(ps[:, 1 + b, at:at + P],
                                          hd[:, LOGA, 2 + c, d, 2 * (b % 2) + e:2 * (b % 2) + e + 1].broadcast_to([P, P]),
                                          below[:, d, 1, :], start=True, stop=True)
                        last.then_inc(*PE.did(f"cr{b}"))
                    for d in range(2):
                        pe.wait_ge(*AC.by(f"tx{d}", i))
                        for e in range(2):
                            for c in range(2):
                                at = (2 * e + c) * P
                                for h in range(2):
                                    last = mm(ps[h * HEAD:(h + 1) * HEAD, 5 + d, at:at + P],
                                              hd[:, LOGA, 2 + c, d, 2 * e + h:2 * e + h + 1].broadcast_to([P, HEAD]),
                                              below[:, d, 1, :], start=True, stop=True)
                        last.then_inc(*PE.did(f"ec{d}"))
                    pe.wait_ge(*PO.by("xw", i))
                    pe.wait_ge(*AC.by("tB", i))
                    pe.wait_ge(*DV.by("cbm", i))
                    for s, j, d in NS:
                        if j:
                            pe.wait_ge(*DV.by(f"h{j - 1}_{d}", i))
                        mm(ps[:, (7, 0)[d], 0:GW], bt[:, order[d][j], :],
                           xw[:, d, j, :, :].rearrange("p e c -> p (e c)"), start=True, stop=True).then_inc(*PE.did("st" + s))
                    pe.wait_ge(*PO.by("w", i))
                    for e in range(4):
                        for c in range(2):
                            r0 = (e % 2) * HEAD
                            at = (e // 2) * SEQ + c * P
                            last = mm(ps[r0:r0 + HEAD, 3, at:at + P], xt[:, 2 + c, e * HEAD:(e + 1) * HEAD], seg[:, 0, e, c, :],
                                      start=True, stop=True)
                    last.then_inc(*PE.did("yd"))
                    for d in range(2):
                        pe.wait_ge(*DV.by(f"h2_{d}", i))
                        for e in range(2):
                            for c in range(2):
                                j = 1 + (c if d == 0 else 1 - c)
                                last = mm(ps[:, 1 + d, e * SEQ + c * P:e * SEQ + (c + 1) * P],
                                          H[:, d, j, 2 * e:2 * e + 2, :].rearrange("p e c -> p (e c)"),
                                          cv[:, 3, SEQ + c * P:SEQ + (c + 1) * P], start=True, stop=True)
                        last.then_inc(*PE.did(f"off{d}"))
                    pe.wait_ge(*AC.by("sq", i))
                    for e in range(2):
                        last = mm(ps[:, 4, 0:SEQ], ones[:, :], ysq[:, e, :], start=(e == 0), stop=(e == 1))
                    last.then_inc(*PE.did("nrm"))
                    for j in range(MOD_PER):
                        last = mm(ps[:, 7, j:j + 1], by_row[:, j // 4, j % 4 * P:(j % 4 + 1) * P], ones[:, 0:1], start=True, stop=True)
                    last.then_inc(*PE.did("mod"))
                PE.end()


def merge(nc, sb, sem, ps, a, ident, ones, par, col, modT, hT, yaT, ybT, xT):
    with ExitStack() as stage:
        def t(name, *shape):
            return sb(name, list(shape), ctx=stage)

        w = t("w_merge", P, 2, KC, 512)
        mT = t("mT", P, KC, SEQ)
        sga, sgb = t("sga", P, 4, SEQ), t("sgb", P, 4, SEQ)
        x_rows = t("x_rows", P, 2, D)
        g1, gain2, rstd, eps_col = t("g1", P, KC), t("gain2", P, KC), t("rstd", P, SEQ), t("m_eps", P, 1)
        mixT, h2T, sqT = ybT, yaT, mT
        w_in = [sem("mg_w0"), sem("mg_w1")]
        x_in, consts, out_mm, out_cp = sem("mg_x"), sem("mg_consts"), sem("mg_out_mm"), sem("mg_out_cp")
        PE = Steps(sem("mg_pe"), "ga gb A B", True)
        AC = Steps(sem("mg_act"), "ga gb", True)
        DV = Steps(sem("mg_dve"), "A B m", True)
        passed = sem("mg_passed")
        dv2, pe2, ac2 = sem("mg_dve2"), sem("mg_pe2"), sem("mg_act2")
        cols = lambda name: a[name].rearrange("l (k p) n -> (l p) k n", p=P)
        win, wa, wb, wo = cols("w_in"), cols("w_branch_a"), cols("w_branch_b"), cols("w_out")
        BL = 4
        half = lambda b: ps[:, 2 * b:2 * b + 2, :].rearrange("p b (c t) -> p (b c) t", t=SEQ)
        with nc.Block() as block:

            @block.sync
            def _(sp):
                with sp.Fori(0, BL) as i:
                    at, at_a, at_b = (sp.snap(i * 512 + c) for c in (0, GA0, GA0 + D))
                    wait_alone(sp, passed, *PE.before("A", i))
                    sp.dma_start(w[:, 0, :, :], win[:, :, ds(at_a, 512)]).then_inc(w_in[0], 16)
                    wait_alone(sp, passed, *PE.before("B", i))
                    sp.dma_start(w[:, 1, :, :], win[:, :, ds(at_b, 512)]).then_inc(w_in[1], 16)
                    wait_alone(sp, passed, *PE.by("ga", i))
                    sp.dma_start(w[:, 0, :, :], wa[:, :, ds(at, 512)]).then_inc(w_in[0], 16)
                    wait_alone(sp, passed, *PE.by("gb", i))
                    sp.dma_start(w[:, 1, :, :], wb[:, :, ds(at, 512)]).then_inc(w_in[1], 16)
                sp.dma_start(x_rows[:, :, :], a["x"].rearrange("l (n p) d -> (l p) n d", p=P)).then_inc(x_in, 16)
                for n in range(BL):
                    sp.wait_ge(*(PE.by("AB"[n], BL - 1) if n < 2 else (out_mm, n - 1)))
                    sp.dma_start(w[:, n % 2, :, :], wo[:, :, n * 512:(n + 1) * 512]).then_inc(w_in[n % 2], 16)

            @block.tensor
            def _(pe):
                PE.open(pe)

                def product(slot, rhs, bank):
                    for c in range(4):
                        for k in range(KC):
                            last = nc.tensor.matmul(ps[:, bank + c // 2, (c % 2) * SEQ:(c % 2 + 1) * SEQ],
                                                    w[:, slot, k, c * P:(c + 1) * P], rhs[:, k, :], start=(k == 0), stop=(k == KC - 1))
                    return last

                with pe.Fori(0, BL) as i:
                    pe.wait_ge(w_in[0], i * 32 + 16)
                    pe.wait_ge(*AC.before("ga", i))
                    product(0, hT[:, :, SEQ:TOK], 0).then_inc(*PE.did("ga"))
                    pe.wait_ge(w_in[1], i * 32 + 16)
                    pe.wait_ge(*AC.before("gb", i))
                    product(1, hT[:, :, SEQ:TOK], 2).then_inc(*PE.did("gb"))
                    pe.wait_ge(w_in[0], i * 32 + 32)
                    pe.wait_ge(*DV.before("A", i))
                    product(0, yaT, 4).then_inc(*PE.did("A"))
                    pe.wait_ge(w_in[1], i * 32 + 32)
                    pe.wait_ge(*DV.before("B", i))
                    product(1, ybT, 6).then_inc(*PE.did("B"))
                PE.end()
                pe.wait_ge(*DV.by("m", BL - 1))
                for n in range(BL):
                    pe.wait_ge(w_in[n % 2], 32 * BL + 16 * (n // 2 + 1))
                    if n >= 2:
                        pe.wait_ge(out_cp, n - 1)
                    product(n % 2, mT, 2 * (n % 2)).then_inc(out_mm, 1)
                pe.wait_ge(x_in, 16)
                for j in range(KC):
                    if j == 8:
                        pe.wait_ge(dv2, 2 + 1)
                    for n in range(2):
                        last = nc.tensor.transpose(ps[:, 4 + (j % 8) // 2, (j % 2) * SEQ + n * P:(j % 2) * SEQ + (n + 1) * P],
                                                   x_rows[:, n, j * P:(j + 1) * P], ident[:, :])
                    if j % 8 == 7:
                        last.then_inc(pe2, 1)
                for r in range(2):
                    pe.wait_ge(ac2, 1 + 2 * r)
                    for k in range(KC):
                        last = nc.tensor.matmul(ps[:, r, 0:SEQ], ones[:, :], sqT[:, k, :], start=(k == 0), stop=(k == KC - 1))
                    last.then_inc(pe2, 1)

            @block.gpsimd
            def _(pool):
                nc.gpsimd.memset(eps_col[:, :], EPS).then_inc(consts, 1)

            @block.scalar
            def _(act):
                AC.open(act)
                with act.Fori(0, BL) as i:
                    act.wait_ge(*PE.by("ga", i))
                    act.wait_ge(*DV.before("m", i))
                    nc.scalar.activation(sga[:, :, :], half(0), ACT.Sigmoid).then_inc(*AC.did("ga"))
                    act.wait_ge(*PE.by("gb", i))
                    nc.scalar.activation(sgb[:, :, :], half(1), ACT.Sigmoid).then_inc(*AC.did("gb"))
                AC.end()
                for n in range(BL):
                    act.wait_ge(out_mm, n + 1)
                    nc.scalar.activation(mixT[:, 4 * n:4 * n + 4, :], half(n % 2), ACT.Copy).then_inc(out_cp, 1)
                act.wait_ge(out_cp, BL)
                act.wait_ge(consts, 1)
                for r, src in enumerate((mixT, xT)):
                    if r:
                        act.wait_ge(dv2, 8)
                    nc.scalar.activation(sqT[:, :, :], src[:, :, :], ACT.Square).then_inc(ac2, 1)
                    act.wait_ge(pe2, 3 + r)
                    nc.scalar.activation(rstd[:, :], ps[:, r, 0:SEQ], ACT.Sqrt, scale=1.0 / D, bias=eps_col[:, 0:1]).then_inc(ac2, 1)

            @block.vector
            def _(dve):
                DV.open(dve)
                with dve.Fori(0, BL) as i:
                    dve.wait_ge(*AC.by("ga", i))
                    dve.wait_ge(*PE.by("A", i))
                    nc.vector.tensor_tensor(sga[:, :, :], sga[:, :, :], half(2), ALU.mult).then_inc(*DV.did("A"))
                    dve.wait_ge(*AC.by("gb", i))
                    dve.wait_ge(*PE.by("B", i))
                    nc.vector.tensor_tensor(sgb[:, :, :], sgb[:, :, :], half(3), ALU.mult).then_inc(*DV.did("B"))
                    dve.wait_ge(*DV.by("B", i))
                    nc.vector.tensor_tensor(mT[:, ds(i * 4, 4), :], sga[:, :, :], sgb[:, :, :], ALU.add).then_inc(*DV.did("m"))
                DV.end()
                row = lambda m: m.unsqueeze(1).broadcast_to([P, 8, SEQ])
                nc.vector.tensor_tensor(g1[:, :], modT[:, 2 * KC:3 * KC, 0], par[:, col["norm_post1"]:col["norm_post1"] + KC],
                                        ALU.mult).then_inc(dv2, 1)
                nc.vector.scalar_tensor_tensor(gain2[:, :], modT[:, 4 * KC:5 * KC, 0], 1.0,
                                               par[:, col["norm_pre2"]:col["norm_pre2"] + KC], ALU.add, ALU.mult).then_inc(dv2, 1)
                for h in range(2):
                    dve.wait_ge(pe2, h + 1)
                    nc.vector.tensor_copy(xT[:, 8 * h:8 * h + 8, :], ps[:, 4:8, :].rearrange("p b (c t) -> p (b c) t", t=SEQ)).then_inc(dv2, 1)
                dve.wait_ge(ac2, 2)
                nc.vector.reciprocal(rstd[:, :], rstd[:, :]).then_inc(dv2, 1)
                dve.wait_ge(dv2, 5)
                for j in range(KC):
                    last = nc.vector.scalar_tensor_tensor(mixT[:, j, :], mixT[:, j, :], g1[:, j:j + 1], rstd[:, :], ALU.mult, ALU.mult)
                last.then_inc(dv2, 1)
                dve.wait_ge(dv2, 6)
                for h in range(2):
                    s = slice(8 * h, 8 * h + 8)
                    nc.vector.tensor_tensor(xT[:, s, :], xT[:, s, :], mixT[:, s, :], ALU.add).then_inc(dv2, 1)
                dve.wait_ge(ac2, 4)
                nc.vector.reciprocal(rstd[:, :], rstd[:, :]).then_inc(dv2, 1)
                dve.wait_ge(dv2, 9)
                for j in range(KC):
                    last = nc.vector.scalar_tensor_tensor(h2T[:, j, :], xT[:, j, :], gain2[:, j:j + 1], rstd[:, :], ALU.mult, ALU.mult)
                last.then_inc(dv2, 1)
                dve.wait_ge(dv2, 10)
                for j in range(KC):
                    last = nc.vector.tensor_scalar(h2T[:, j, :], h2T[:, j, :], modT[:, 3 * KC + j, 0:1], None, ALU.add)
                last.then_inc(dv2, 1)


def peer(nc, sb, sem, ps, a, out, ident, ones, par, col, modT, hT, h2T, qT, xT):
    with ExitStack() as outer:
        idx = sb("idx", [P, 2 * SLOTS], U32, ctx=outer)
        gates = sb("gates", [P, 2 * SLOTS], ctx=outer)
        rows = hT[:, :, :].rearrange("p k t -> p (k t)").rearrange("p (a n d) -> p a n d", a=2, n=2)
        h2_rows, x_rows = rows[:, 0, :, :], rows[:, 1, :, :]
        g2_rows = sb("g2_rows", [P, D], ctx=outer)
        iota_f = sb("iota_f", [P, TOPK], ctx=outer)
        scores = xT[:, :, :].rearrange("p j t -> p (j t)").rearrange("p (n l k) -> p n l k", n=2, k=PK)
        route(nc, sb, sem, ps, a, ident, ones, par, col, modT, h2T, xT, qT, iota_f, scores, h2_rows, x_rows, g2_rows)
        experts(nc, sb, sem, ps, a, out, ident, iota_f, scores, idx, gates, h2_rows, x_rows, g2_rows)


def route(nc, sb, sem, ps, a, ident, ones, par, col, modT, h2T, xT, qT, iota_f, scores, h2_rows, x_rows, g2_rows):
    with ExitStack() as stage:
        def t(name, shape, dt=F32):
            return sb(name, list(shape), dt, ctx=stage)

        w = t("w_q", [P, 2, KC, 512])
        keys, keysT = t("keys", [P, KC, PK]), t("keysT", [P, KC, PK])
        g2, diag = t("g2", [P, KC]), t("diag_g2", [P, 4, P])
        iota_i = t("iota_i", [P, TOPK], U32)
        w_in = [sem("q_w0"), sem("q_w1")]
        k_in, q_mm, q_cp, k_tr, k_cp, s_mm, iotas = (sem(x) for x in ("k_in", "q_mm", "q_cp", "k_tr", "k_cp", "s_mm", "iotas"))
        r_tr, r_cp, g_dg, g_mm, g_cp, g2_done = (sem(x) for x in ("r_tr", "r_cp", "g_dg", "g_mm", "g_cp", "g2_done"))
        wq = a["peer_wq"].rearrange("l (k p) n -> (l p) k n", p=P)
        with nc.Block() as block:

            @block.sync
            def _(sp):
                for j in range(KC):
                    sp.dma_start(keys[:, j, :], a["peer_subkeys"][0, j // 2, j % 2, :, :]).then_inc(k_in, 16)
                for n in range(4):
                    if n >= 2:
                        sp.wait_ge(q_mm, n - 1)
                    sp.dma_start(w[:, n % 2, :, :], wq[:, :, n * 512:(n + 1) * 512]).then_inc(w_in[n % 2], 16)

            @block.gpsimd
            def _(pool):
                nc.gpsimd.iota(iota_i[:, :], [[1, TOPK]], base=0, channel_multiplier=0).then_inc(iotas, 1)

            @block.tensor
            def _(pe):
                for g in range(16):
                    if g >= 4:
                        pe.wait_ge(r_cp, g - 3)
                    src, n, j0 = (h2T, xT)[g // 8], (g % 8) // 4, (g % 4) * 4
                    for c in range(4):
                        last = nc.tensor.transpose(ps[:, 4 + g % 4, c * P:(c + 1) * P], src[:, j0 + c, n * P:(n + 1) * P], ident[:, :])
                    last.then_inc(r_tr, 1)
                for g in range(4):
                    pe.wait_ge(g_dg, g + 1)
                    pe.wait_ge(r_cp, 13 + g)
                    nc.tensor.matmul(ps[:, 4 + g, :], ones[:, :], diag[:, :, :].rearrange("p c t -> p (c t)"),
                                     start=True, stop=True).then_inc(g_mm, 1)
                pe.wait_ge(k_in, 16 * KC)
                for g in range(4):
                    pe.wait_ge(g_cp, g + 1)
                    for c in range(4):
                        last = nc.tensor.transpose(ps[:, 4 + g, c * P:(c + 1) * P], keys[:, 4 * g + c, :], ident[:, :])
                    last.then_inc(k_tr, 1)
                for n in range(4):
                    pe.wait_ge(w_in[n % 2], 16 * (n // 2 + 1))
                    if n >= 2:
                        pe.wait_ge(q_cp, n - 1)
                    for c in range(4):
                        for k in range(KC):
                            last = nc.tensor.matmul(ps[:, 2 * (n % 2) + c // 2, (c % 2) * SEQ:(c % 2 + 1) * SEQ],
                                                    w[:, n % 2, k, c * P:(c + 1) * P], h2T[:, k, :], start=(k == 0), stop=(k == KC - 1))
                    last.then_inc(q_mm, 1)
                pe.wait_ge(q_cp, 4)
                pe.wait_ge(k_cp, 4)
                for n in range(2):
                    for j in range(KC):
                        last = nc.tensor.matmul(ps[:, 4 * n + j // 4, (j % 4) * PK:(j % 4 + 1) * PK], qT[:, j, n * P:(n + 1) * P],
                                                keysT[:, j, :], start=True, stop=True)
                    last.then_inc(s_mm, 1)

            @block.scalar
            def _(act):
                for g in range(16):
                    act.wait_ge(r_tr, g + 1)
                    dst, n, j0 = (h2_rows, x_rows)[g // 8], (g % 8) // 4, (g % 4) * 4
                    nc.scalar.activation(dst[:, n, j0 * P:(j0 + 4) * P], ps[:, 4 + g % 4, :], ACT.Copy).then_inc(r_cp, 1)
                for g in range(4):
                    act.wait_ge(g_mm, g + 1)
                    nc.scalar.activation(g2_rows[:, g * 512:(g + 1) * 512], ps[:, 4 + g, :], ACT.Copy).then_inc(g_cp, 1)
                for g in range(4):
                    act.wait_ge(k_tr, g + 1)
                    nc.scalar.activation(keysT[:, 4 * g:4 * g + 4, :], ps[:, 4 + g, :].rearrange("p (c k) -> p c k", k=PK),
                                         ACT.Copy).then_inc(k_cp, 1)
                for n in range(4):
                    act.wait_ge(q_mm, n + 1)
                    b = 2 * (n % 2)
                    nc.scalar.activation(qT[:, 4 * n:4 * n + 4, :], ps[:, b:b + 2, :].rearrange("p b (c t) -> p (b c) t", t=SEQ),
                                         ACT.Copy).then_inc(q_cp, 1)
                for n in range(2):
                    act.wait_ge(s_mm, n + 1)
                    nc.scalar.activation(scores[:, n, :, :].rearrange("p l k -> p (l k)"),
                                         ps[:, 4 * n:4 * n + 4, :].rearrange("p b t -> p (b t)"), ACT.Copy)

            @block.vector
            def _(dve):
                nc.vector.tensor_tensor(g2[:, :], modT[:, 5 * KC:6 * KC, 0], par[:, col["norm_post2"]:col["norm_post2"] + KC],
                                        ALU.mult).then_inc(g2_done, 1)
                dve.wait_ge(g2_done, 1)
                for g in range(4):
                    if g:
                        dve.wait_ge(g_mm, g)
                    for c in range(4):
                        last = nc.vector.tensor_scalar(diag[:, c, :], ident[:, :], g2[:, 4 * g + c:4 * g + c + 1], None, ALU.mult)
                    last.then_inc(g_dg, 1)
                dve.wait_ge(iotas, 1)
                nc.vector.tensor_copy(iota_f[:, :], iota_i[:, :]).then_inc(g2_done, 1)


def experts(nc, sb, sem, ps, a, out, ident, iota_f, scores, idx, gates, h2_rows, x_rows, g2_rows):
    with ExitStack() as stage:
        def t(name, shape, dt=F32):
            return sb(name, list(shape), dt, ctx=stage)

        NB = 4
        TURNS = 2 * PH
        ub, vb = [t(f"ub{b}", [P, D]) for b in range(NB)], [t(f"vb{b}", [P, D]) for b in range(NB)]
        junk, fin = t("junk", [P, D]), t("fin", [P, D])
        fin2 = ub[0]
        ixu, ixv = t("ixu", [P, 2, TOPK], U32), t("ixv", [P, 2, TOPK], U32)
        dots, acts, coef = t("dots", [P, TOPK]), t("acts", [P, TOPK]), t("coef", [P, TOPK])
        diag = t("diag", [P, 2, P])
        zero, eps_col = t("zero", [P, P]), t("x_eps", [P, 1])
        ssq, rstd = t("x_ssq", [P, 2]), t("x_rstd", [P, 2])
        u_in, v_in = [sem(f"u_in{b}") for b in range(NB)], [sem(f"v_in{b}") for b in range(NB)]
        sc, sc2 = t("sc", [P, 2, 2, PK]), t("sc2", [P, 2, 2, PK])
        top_s, top_i, top_f = t("top_s", [P, 2, 2, TOPK]), t("top_i", [P, 2, 2, TOPK], U32), t("top_f", [P, 2, 2, TOPK])
        cand, cand2 = t("cand", [P, 2, TOPK, TOPK]), t("cand2", [P, 2, TOPK, TOPK])
        best_s, best_j = t("best_s", [P, 2, TOPK]), t("best_j", [P, 2, TOPK], U32)
        part_i, part_f = t("part_i", [P, 2, 2, TOPK], U32), t("part_f", [P, 2, 2, TOPK])
        hot = t("hot", [P, 2, TOPK, TOPK])
        ex, ef = t("ex", [P, 2, 2, TOPK]), t("ef", [P, 2, TOPK])
        soft, total = t("soft", [P, 2, TOPK]), t("total", [P, 2])
        LISTS = [(n, s) for n in range(2) for s in range(2)]
        DV = Steps(sem("tk_dve"), " ".join(
            ["sc"] + [f"{m}{n}{s}" for m in ("m1", "i1", "mr", "m2", "i2") for n, s in LISTS] + ["tf", "cand"]
            + [f"{m}{n}" for m in ("b1", "j1", "br", "b2", "j2") for n in range(2)]
            + ["hi", "lo", "pf", "eq0", "mul0", "red0", "eq1", "mul1", "red1", "ef", "idx", "diff", "sum", "rec", "gates"]), True)
        AC = Steps(sem("tk_act"), "exp", True)
        of_head = lambda m, i: m[:, :, 0:2, :] if isinstance(i, int) else m[:, :, ds(i * 2, 2), :]
        of_turns = lambda m, i: m[:, 0:2 * TOPK] if isinstance(i, int) else m[:, ds(i * 2 * TOPK, 2 * TOPK)]
        consts, opened, stored = sem("x_consts"), sem("x_open"), sem("x_stored")
        u_tab = a["peer_u"].rearrange("l e d -> (l e) d")
        v_tab = a["peer_v"].rearrange("l e d -> (l e) d")
        MID = TOPK // 2
        DU = Steps(sem("x_du"), " ".join([f"dot{k}" for k in range(MID)] + ["ixu", "ixv"] + [f"dot{k}" for k in range(MID, TOPK)]), True)
        first_ix = sem("x_first_ix")
        GE = Steps(sem("x_ge"), "gelu")
        DC = Steps(sem("x_dc"), "coef")
        DG = Steps(sem("x_dg"), " ".join(f"dg{k}" for k in range(TOPK)))
        PV = Steps(sem("x_pv"), " ".join(f"v{k}" for k in range(TOPK)), True)
        passed = sem("x_passed")
        done, fin_a = sem("x_fin"), sem("x_fin_a")

        def program(emit_u, emit_v, engine):
            emit_u(0, 0)
            with engine.Fori(0, PH - 1) as h:
                emit_v(h * 2, 0, h * 2 + 1, 1, h + 1)
                emit_v(h * 2 + 1, 1, h * 2 + 2, 0, None)
            emit_v(TURNS - 2, 0, TURNS - 1, 1, None)
            emit_v(TURNS - 1, 1, None, 0, None)

        def fresh(steps):
            steps.at = 0

        with nc.Block() as block:

            @block.gpsimd
            def _(pool):
                nc.gpsimd.memset(zero[:, :], 0.0).then_inc(consts, 1)
                nc.gpsimd.memset(eps_col[:, :], EPS).then_inc(consts, 1)

                def gather_u(u, n, k):
                    b = k % NB
                    if k == 0:
                        wait_alone(pool, passed, *DU.before("ixu", u))
                    wait_alone(pool, passed, *(DU.by(f"dot{k - NB}", u) if k >= NB else DU.before(f"dot{TOPK - NB + k}", u)))
                    nc.gpsimd.indirect_dma_start(ub[b][:, :], None, u_tab, bass.IndirectOffsetOnAxis(ap=ixu[:, n, k:k + 1], axis=0)
                                                 ).then_inc(u_in[b], 16)

                def gather_v(v, n, k):
                    b = k % NB
                    if k == 0:
                        wait_alone(pool, passed, *DU.by("ixv", v))
                    wait_alone(pool, passed, *(PV.by(f"v{k - NB}", v) if k >= NB else PV.before(f"v{TOPK - NB + k}", v)))
                    nc.gpsimd.indirect_dma_start(vb[b][:, :], None, v_tab, bass.IndirectOffsetOnAxis(ap=ixv[:, n, k:k + 1], axis=0)
                                                 ).then_inc(v_in[b], 16)

                def emit_u(u, n):
                    for k in range(TOPK):
                        gather_u(u, n, k)

                def emit_v(v, n, u, un, chosen):
                    for k in range(TOPK):
                        gather_v(v, n, k)
                        if u is not None:
                            gather_u(u, un, k)

                pool.wait_ge(first_ix, 1)
                program(emit_u, emit_v, pool)

            @block.vector
            def _(dve):
                def choose(i):
                    fresh(DV)
                    wait_alone(dve, passed, *DV.before("gates", i))
                    nc.vector.tensor_copy(sc[:, :, :, :], of_head(scores, i)).then_inc(*DV.did("sc"))
                    wait_alone(dve, passed, *DV.by("sc", i))
                    for n, s in LISTS:
                        nc.vector.max(top_s[:, n, s, 0:8], sc[:, n, s, :]).then_inc(*DV.did(f"m1{n}{s}"))
                    for n, s in LISTS:
                        wait_alone(dve, passed, *DV.by(f"m1{n}{s}", i))
                        nc.vector.max_index(top_i[:, n, s, 0:8], top_s[:, n, s, 0:8], sc[:, n, s, :]).then_inc(*DV.did(f"i1{n}{s}"))
                    for n, s in LISTS:
                        nc.vector.match_replace(sc2[:, n, s, :], top_s[:, n, s, 0:8], sc[:, n, s, :], -3.0e38).then_inc(*DV.did(f"mr{n}{s}"))
                    for n, s in LISTS:
                        wait_alone(dve, passed, *DV.by(f"mr{n}{s}", i))
                        nc.vector.max(top_s[:, n, s, 8:16], sc2[:, n, s, :]).then_inc(*DV.did(f"m2{n}{s}"))
                    for n, s in LISTS:
                        wait_alone(dve, passed, *DV.by(f"m2{n}{s}", i))
                        nc.vector.max_index(top_i[:, n, s, 8:16], top_s[:, n, s, 8:16], sc2[:, n, s, :]).then_inc(*DV.did(f"i2{n}{s}"))
                    dve.wait_ge(*DV.by("i211", i))
                    nc.vector.tensor_copy(top_f[:, :, :, :], top_i[:, :, :, :]).then_inc(*DV.did("tf"))
                    nc.vector.tensor_tensor(cand[:, :, :, :], top_s[:, :, 0, :].unsqueeze(3).broadcast_to([P, 2, TOPK, TOPK]),
                                            top_s[:, :, 1, :].unsqueeze(2).broadcast_to([P, 2, TOPK, TOPK]), ALU.add).then_inc(*DV.did("cand"))
                    wait_alone(dve, passed, *DV.by("cand", i))
                    flat = lambda m, n: m[:, n, :, :].rearrange("p a b -> p (a b)")
                    for n in range(2):
                        nc.vector.max(best_s[:, n, 0:8], flat(cand, n)).then_inc(*DV.did(f"b1{n}"))
                    for n in range(2):
                        wait_alone(dve, passed, *DV.by(f"b1{n}", i))
                        nc.vector.max_index(best_j[:, n, 0:8], best_s[:, n, 0:8], flat(cand, n)).then_inc(*DV.did(f"j1{n}"))
                    for n in range(2):
                        nc.vector.match_replace(flat(cand2, n), best_s[:, n, 0:8], flat(cand, n), -3.0e38).then_inc(*DV.did(f"br{n}"))
                    for n in range(2):
                        wait_alone(dve, passed, *DV.by(f"br{n}", i))
                        nc.vector.max(best_s[:, n, 8:16], flat(cand2, n)).then_inc(*DV.did(f"b2{n}"))
                    for n in range(2):
                        wait_alone(dve, passed, *DV.by(f"b2{n}", i))
                        nc.vector.max_index(best_j[:, n, 8:16], best_s[:, n, 8:16], flat(cand2, n)).then_inc(*DV.did(f"j2{n}"))
                    dve.wait_ge(*DV.by("j21", i))
                    nc.vector.tensor_scalar(part_i[:, 0, :, :], best_j[:, :, :], 4, None, ALU.logical_shift_right).then_inc(*DV.did("hi"))
                    nc.vector.tensor_scalar(part_i[:, 1, :, :], best_j[:, :, :], TOPK - 1, None, ALU.bitwise_and).then_inc(*DV.did("lo"))
                    dve.wait_ge(*DV.by("lo", i))
                    nc.vector.tensor_copy(part_f[:, :, :, :], part_i[:, :, :, :]).then_inc(*DV.did("pf"))
                    dve.wait_ge(*DV.by("pf", i))
                    for s in range(2):
                        if s:
                            dve.wait_ge(*DV.by("red0", i))
                        nc.vector.tensor_tensor(hot[:, :, :, :], part_f[:, s, :, :].unsqueeze(3).broadcast_to([P, 2, TOPK, TOPK]),
                                                iota_f[:, :].unsqueeze(1).unsqueeze(1).broadcast_to([P, 2, TOPK, TOPK]),
                                                ALU.is_equal).then_inc(*DV.did(f"eq{s}"))
                        dve.wait_ge(*DV.by(f"eq{s}", i))
                        nc.vector.tensor_tensor(hot[:, :, :, :], hot[:, :, :, :],
                                                top_f[:, :, s, :].unsqueeze(2).broadcast_to([P, 2, TOPK, TOPK]), ALU.mult).then_inc(*DV.did(f"mul{s}"))
                        dve.wait_ge(*DV.by(f"mul{s}", i))
                        nc.vector.tensor_reduce(ex[:, s, :, :], hot[:, :, :, :], AX, ALU.add).then_inc(*DV.did(f"red{s}"))
                    dve.wait_ge(*DV.by("red1", i))
                    nc.vector.scalar_tensor_tensor(ef[:, :, :], ex[:, 0, :, :], float(PK), ex[:, 1, :, :], ALU.mult, ALU.add).then_inc(*DV.did("ef"))
                    dve.wait_ge(*DV.by("ef", i))
                    nc.vector.tensor_copy(of_turns(idx, i), ef[:, :, :].rearrange("p n k -> p (n k)")).then_inc(*DV.did("idx"))
                    nc.vector.tensor_tensor(soft[:, :, :], best_s[:, :, :], best_s[:, :, 0:1].broadcast_to([P, 2, TOPK]),
                                            ALU.subtract).then_inc(*DV.did("diff"))
                    wait_alone(dve, passed, *DV.by("idx", i))

                def weigh(i):
                    dve.wait_ge(*AC.by("exp", i))
                    nc.vector.tensor_reduce(total[:, :], soft[:, :, :], AX, ALU.add).then_inc(*DV.did("sum"))
                    dve.wait_ge(*DV.by("sum", i))
                    nc.vector.reciprocal(total[:, :], total[:, :]).then_inc(*DV.did("rec"))
                    dve.wait_ge(*DV.by("rec", i))
                    nc.vector.tensor_tensor(of_turns(gates, i).rearrange("p (n k) -> p n k", n=2), soft[:, :, :],
                                            total[:, :].unsqueeze(2).broadcast_to([P, 2, TOPK]), ALU.mult).then_inc(*DV.did("gates"))
                    DV.end()
                    dve.wait_ge(*DV.by("gates", i))

                def dot(u, n, k):
                    dve.wait_ge(u_in[k % NB], u * (16 * TOPK // NB) + 16 * (k // NB + 1))
                    dve.wait_ge(*(DU.by(f"dot{k - 1}", u) if k else DU.before(f"dot{TOPK - 1}", u)))
                    nc.vector.scalar_tensor_tensor(junk[:, :], ub[k % NB][:, :], 1.0, h2_rows[:, n, :], ALU.mult, ALU.mult,
                                                   accum_out=dots[:, k:k + 1]).then_inc(*DU.did(f"dot{k}"))

                def emit_u(u, n, chosen=None):
                    fresh(DU)
                    for k in range(TOPK):
                        if k == 4 and chosen is not None:
                            choose(chosen)
                        if k == MID:
                            if isinstance(u, int) and u == TURNS - 1:
                                DU.skip("ixu")
                            else:
                                nc.vector.tensor_copy(ixu[:, 1 - n, :], idx[:, ds((u + 1) * TOPK, TOPK)]).then_inc(*DU.did("ixu"))
                            wait_alone(dve, passed, *PV.before(f"v{TOPK - 1}", max(u - 1, 0) if isinstance(u, int) else u - 1))
                            nc.vector.tensor_copy(ixv[:, n, :], idx[:, ds(u * TOPK, TOPK)]).then_inc(*DU.did("ixv"))
                        dot(u, n, k)

                def emit_v(v, n, u, un, chosen):
                    fresh(DC)
                    dve.wait_ge(*PV.before(f"v{TOPK - 1}", v))
                    dve.wait_ge(*GE.by("gelu", v))
                    nc.vector.tensor_tensor(coef[:, :], acts[:, :], gates[:, ds(v * TOPK, TOPK)], ALU.mult).then_inc(*DC.did("coef"))
                    if u is not None:
                        emit_u(u, un, chosen)
                    if chosen is not None:
                        weigh(chosen)

                DU.open(dve)
                DV.open(dve)
                choose(0)
                weigh(0)
                nc.vector.tensor_copy(ixu[:, 0, :], idx[:, 0:TOPK]).then_inc(first_ix, 1)
                program(emit_u, emit_v, dve)
                for n in range(2):
                    dve.wait_ge(done, 4 * n + 2)
                    nc.vector.reciprocal(rstd[:, n:n + 1], rstd[:, n:n + 1]).then_inc(done, 1)
                    dve.wait_ge(done, 4 * n + 3)
                    if n:
                        dve.wait_ge(stored, 16)
                    nc.vector.scalar_tensor_tensor(fin[:, :], ps[:, 4 * n:4 * n + 4, :].rearrange("p b t -> p (b t)"), rstd[:, n:n + 1],
                                                   g2_rows[:, :], ALU.mult, ALU.mult).then_inc(fin_a, 1)
                    dve.wait_ge(fin_a, n + 1)
                    nc.vector.tensor_tensor(fin[:, :], fin[:, :], x_rows[:, n, :], ALU.add).then_inc(done, 1)

            @block.scalar
            def _(act):
                def exponent(i):
                    fresh(AC)
                    act.wait_ge(*DV.by("diff", i))
                    nc.scalar.activation(soft[:, :, :], soft[:, :, :], ACT.Exp).then_inc(*AC.did("exp"))

                def emit_u(u, n):
                    return

                def emit_v(v, n, u, un, chosen):
                    fresh(GE)
                    fresh(DG)
                    act.wait_ge(*DU.by(f"dot{TOPK - 1}", v))
                    nc.scalar.activation(acts[:, :], dots[:, :], ACT.Gelu).then_inc(*GE.did("gelu"))
                    act.wait_ge(*DC.by("coef", v))
                    for k in range(TOPK):
                        if chosen is not None and k == 10:
                            exponent(chosen)
                        act.wait_ge(*(PV.by(f"v{k - 2}", v) if k >= 2 else PV.before(f"v{TOPK - 2 + k}", v)))
                        nc.scalar.activation(diag[:, k % 2, :], ident[:, :], ACT.Copy, scale=coef[:, k:k + 1]).then_inc(*DG.did(f"dg{k}"))

                AC.open(act)
                exponent(0)
                program(emit_u, emit_v, act)
                act.wait_ge(consts, 2)
                act.wait_ge(*PV.by(f"v{TOPK - 1}", TURNS - 1))
                act.wait_ge(opened, 2)
                for n in range(2):
                    if n:
                        act.wait_ge(done, 4)
                    nc.scalar.activation(fin2[:, :], ps[:, 4 * n:4 * n + 4, :].rearrange("p b t -> p (b t)"), ACT.Square,
                                         accum_out=ssq[:, n:n + 1]).then_inc(done, 1)
                    act.wait_ge(done, 4 * n + 1)
                    nc.scalar.activation(rstd[:, n:n + 1], ssq[:, n:n + 1], ACT.Sqrt, scale=1.0 / D, bias=eps_col[:, 0:1]).then_inc(done, 1)

            @block.tensor
            def _(pe):
                PV.open(pe)
                pe.wait_ge(consts, 1)

                def emit_u(u, n):
                    for m in range(2):
                        for c in range(4):
                            nc.tensor.matmul(ps[:, 4 * m + c, :], zero[:, :], g2_rows[:, c * 512:(c + 1) * 512], start=True, stop=False)

                def emit_v(v, n, u, un, chosen):
                    fresh(PV)
                    for k in range(TOPK):
                        pe.wait_ge(*DG.by(f"dg{k}", v))
                        pe.wait_ge(v_in[k % NB], v * (16 * TOPK // NB) + 16 * (k // NB + 1))
                        for c in range(4):
                            last = nc.tensor.matmul(ps[:, 4 * n + c, :], diag[:, k % 2, :], vb[k % NB][:, c * 512:(c + 1) * 512],
                                                    start=False, stop=False)
                        last.then_inc(*PV.did(f"v{k}"))

                program(emit_u, emit_v, pe)
                for m in range(2):
                    for c in range(4):
                        last = nc.tensor.matmul(ps[:, 4 * m + c, :], zero[:, :], g2_rows[:, c * 512:(c + 1) * 512], start=False, stop=True)
                    last.then_inc(opened, 1)

            @block.sync
            def _(sp):
                for n in range(2):
                    sp.wait_ge(done, 4 * n + 4)
                    sp.dma_start(out[0, n * P:(n + 1) * P, :], fin[:, :]).then_inc(stored, 16)
                sp.wait_ge(stored, 32)


_NAMES = ["x", "c", "ctx", "c_ctx", "w_mod", "b_mod", "norm_pre1", "norm_post1", "norm_pre2", "norm_post2", "w_in",
          "rw_mu", "rw_w0", "rw_w2", "rw_a0", "rw_a2", "rw_g2", "rw_k_k", "rw_k_a", "rw_r_k", "rw_ln_w", "rw_ln_b",
          "ssm_conv_w", "ssm_conv_b", "ssm_dt_bias", "ssm_a_log", "ssm_d", "ssm_norm_w", "w_branch_a", "w_branch_b",
          "w_out", "peer_wq", "peer_subkeys", "peer_u", "peer_v"]


def kernel(**inputs):
    import numpy as np
    import concourse.bacc as bacc
    from concourse.bass_utils import run_bass_kernel_spmd

    nc = bacc.Bacc("TRN2", target_bir_lowering=False, num_devices=1)
    arrays, aps = {}, {}
    for name in _NAMES:
        v = np.ascontiguousarray(inputs[name])
        arrays[f"in_{name}"] = v
        aps[name] = nc.dram_tensor(f"in_{name}", v.shape, mybir.dt.from_np(v.dtype), kind="ExternalInput").ap()
    out = nc.dram_tensor("out_x", (1, SEQ, D), F32, kind="ExternalOutput").ap()
    hybrid_block(nc, aps, out)
    r = run_bass_kernel_spmd(nc, [arrays], core_ids=[0])
    return r.results[0]["out_x"]
```
